# Optimizing a Trainium2 kernel written in Bass

```python
import jax, jax.numpy as jnp
from jax import lax
import numpy as np

D_MODEL = 1024
BATCH = 1
SEQ = 512
DEPTH = 1

D_A = 1024
CONV_A = 3
D_B = 1024
CONV_B = 31
D_C = 1024
N_HEADS_C = 8
HEAD_C = D_C // N_HEADS_C
CHUNK = 128
N_BRANCH = 3
SPLITS = (D_A, 2 * D_A, 3 * D_A, 3 * D_A + D_B, 3 * D_A + 2 * D_B, 3 * D_A + 2 * D_B + 2 * D_C)
D_IN = 3 * D_A + 2 * D_B + 2 * D_C + N_BRANCH * D_MODEL
N_GROUPS_MOE = 4
EXPERTS_PER_GROUP = 8
N_EXPERTS = N_GROUPS_MOE * EXPERTS_PER_GROUP
TOP_K = 2
D_FF_EXPERT = 512
MOE_BLOCK = 128
RMS_EPS = 1e-6
LN_EPS = 1e-5

kernel_name = "hybrid_conv_gmlp_hmoe_encoder"

def rms_norm(x, g):
    xf = x.astype(jnp.float32)
    y = xf * lax.rsqrt(jnp.mean(xf * xf, axis=-1, keepdims=True) + RMS_EPS)
    return (y * g.astype(jnp.float32)).astype(x.dtype)

def layer_norm(x, g, b):
    xf = x.astype(jnp.float32)
    mu = jnp.mean(xf, axis=-1, keepdims=True)
    var = jnp.mean(jnp.square(xf - mu), axis=-1, keepdims=True)
    y = (xf - mu) * lax.rsqrt(var + LN_EPS) * g.astype(jnp.float32) + b.astype(jnp.float32)
    return y.astype(x.dtype)

def depthwise_conv(x, w):
    k = w.shape[0]
    return lax.conv_general_dilated(
        x, w[:, None, :].astype(x.dtype), window_strides=(1,),
        padding=((k // 2, k // 2),), dimension_numbers=("NWC", "WIO", "NWC"),
        feature_group_count=x.shape[-1])

def short_conv_mixer(xa, ba, ca, w_conv, w_out):
    return (ba * depthwise_conv(ca * xa, w_conv)) @ w_out

def conformer_conv(val, gate, w_conv, ln_g, ln_b, w_out):
    z = val * jax.nn.sigmoid(gate)
    z = depthwise_conv(z, w_conv)
    z = jax.nn.silu(layer_norm(z, ln_g, ln_b))
    return z @ w_out

def chunked_spatial_gating(uv, ln_g, ln_b, w_s, b_s, w_out):
    uv = jax.nn.gelu(uv)
    u, v = jnp.split(uv, 2, axis=-1)
    v = layer_norm(v, ln_g, ln_b)
    bsz, s, _ = v.shape
    v = v.reshape(bsz, s // CHUNK, CHUNK, N_HEADS_C, HEAD_C)
    v = jnp.einsum("hpq,bnqhc->bnphc", w_s, v) + b_s.T[None, None, :, :, None]
    return (u * v.reshape(bsz, s, D_C)) @ w_out

def mixer_block(x, norm_g, w_in, conv_a, w_a_out, conv_b, ln_b_g, ln_b_b, w_b_out,
                ln_c_g, ln_c_b, w_s, b_s, w_c_out, w_o):
    bsz, s, d = x.shape
    h = rms_norm(x, norm_g)
    p = h @ w_in
    xa, ba, ca, val_b, gate_b, uv_c, gate_logits = jnp.split(p, SPLITS, axis=-1)
    y_a = short_conv_mixer(xa, ba, ca, conv_a, w_a_out)
    y_b = conformer_conv(val_b, gate_b, conv_b, ln_b_g, ln_b_b, w_b_out)
    y_c = chunked_spatial_gating(uv_c, ln_c_g, ln_c_b, w_s, b_s, w_c_out)
    g = jax.nn.sigmoid(gate_logits).reshape(bsz, s, N_BRANCH, d)
    merged = g[:, :, 0] * y_a + g[:, :, 1] * y_b + g[:, :, 2] * y_c
    return merged @ w_o

def hier_moe(h, w_group, b_group, w_router, b_router, w1, w3, w2):
    bsz, s, d = h.shape
    t = bsz * s
    hf = h.reshape(t, d)
    group_logits = (hf @ w_group + b_group).astype(jnp.float32)
    group_prob = jax.nn.softmax(group_logits, axis=-1)
    g_idx = jnp.argmax(group_logits, axis=-1)
    g_p = jnp.take_along_axis(group_prob, g_idx[:, None], axis=1)
    exp_logits = (hf @ w_router + b_router).astype(jnp.float32)
    exp_logits = exp_logits.reshape(t, N_GROUPS_MOE, EXPERTS_PER_GROUP)
    exp_logits = jnp.take_along_axis(exp_logits, g_idx[:, None, None], axis=1)[:, 0]
    top_logit, top_idx = lax.top_k(exp_logits, TOP_K)
    top_w = jax.nn.softmax(top_logit, axis=-1) * g_p
    n_assign = t * TOP_K
    expert = (g_idx[:, None] * EXPERTS_PER_GROUP + top_idx).reshape(-1).astype(jnp.int32)
    tok = jnp.repeat(jnp.arange(t, dtype=jnp.int32), TOP_K)
    wgt = top_w.reshape(-1).astype(h.dtype)
    order = jnp.argsort(expert)
    e_sorted = expert[order]
    tok_sorted = tok[order]
    w_sorted = wgt[order]
    counts = jnp.bincount(expert, length=N_EXPERTS)
    padded = (counts + MOE_BLOCK - 1) // MOE_BLOCK * MOE_BLOCK
    start = jnp.cumsum(counts) - counts
    padded_end = jnp.cumsum(padded)
    padded_start = padded_end - padded
    dest = padded_start[e_sorted] + jnp.arange(n_assign, dtype=jnp.int32) - start[e_sorted]
    n_blocks = n_assign // MOE_BLOCK + N_EXPERTS
    n_slots = n_blocks * MOE_BLOCK
    slot_tok = jnp.full((n_slots,), t, dtype=jnp.int32).at[dest].set(tok_sorted)
    slot_w = jnp.zeros((n_slots,), h.dtype).at[dest].set(w_sorted)
    block_start = jnp.arange(n_blocks, dtype=jnp.int32) * MOE_BLOCK
    block_expert = jnp.minimum(jnp.searchsorted(padded_end, block_start, side="right"), N_EXPERTS - 1)
    h_pad = jnp.concatenate([hf, jnp.zeros((1, d), h.dtype)], axis=0)
    xb = h_pad[slot_tok].reshape(n_blocks, MOE_BLOCK, d)

    def expert_block(args):
        xe, e = args
        return (jax.nn.silu(xe @ w1[e]) * (xe @ w3[e])) @ w2[e]

    yb = lax.map(expert_block, (xb, block_expert)).reshape(n_slots, d)
    y = jax.ops.segment_sum(yb * slot_w[:, None], slot_tok, num_segments=t + 1)[:t]
    return y.reshape(bsz, s, d)

def setup_inputs(seed: int = 0) -> dict:
    key = jax.random.key(seed)
    ks = jax.random.split(key, 26)

    def nrm(k, shape, scale):
        return jax.random.normal(k, shape, jnp.float32) * scale

    def gain(k, shape):
        return 1.0 + 0.02 * jax.random.normal(k, shape, jnp.float32)

    L, D = DEPTH, D_MODEL
    return {
        "x": nrm(ks[0], (BATCH, SEQ, D), 1.0),
        "norm_mix": gain(ks[1], (L, D)),
        "w_in": nrm(ks[2], (L, D, D_IN), D ** -0.5),
        "conv_a": nrm(ks[3], (L, CONV_A, D_A), CONV_A ** -0.5),
        "w_a_out": nrm(ks[4], (L, D_A, D), D_A ** -0.5),
        "conv_b": nrm(ks[5], (L, CONV_B, D_B), CONV_B ** -0.5),
        "ln_b_g": gain(ks[6], (L, D_B)),
        "ln_b_b": nrm(ks[7], (L, D_B), 0.02),
        "w_b_out": nrm(ks[8], (L, D_B, D), D_B ** -0.5),
        "ln_c_g": gain(ks[9], (L, D_C)),
        "ln_c_b": nrm(ks[10], (L, D_C), 0.02),
        "w_s": nrm(ks[11], (L, N_HEADS_C, CHUNK, CHUNK), CHUNK ** -0.5),
        "b_s": gain(ks[12], (L, N_HEADS_C, CHUNK)),
        "w_c_out": nrm(ks[13], (L, D_C, D), D_C ** -0.5),
        "w_o": nrm(ks[14], (L, D, D), D ** -0.5),
        "norm_ffn": gain(ks[15], (L, D)),
        "w_group": nrm(ks[16], (L, D, N_GROUPS_MOE), D ** -0.5),
        "b_group": nrm(ks[17], (L, N_GROUPS_MOE), 0.01),
        "w_router": nrm(ks[18], (L, D, N_EXPERTS), D ** -0.5),
        "b_router": nrm(ks[19], (L, N_EXPERTS), 0.01),
        "w1": nrm(ks[20], (L, N_EXPERTS, D, D_FF_EXPERT), D ** -0.5),
        "w3": nrm(ks[21], (L, N_EXPERTS, D, D_FF_EXPERT), D ** -0.5),
        "w2": nrm(ks[22], (L, N_EXPERTS, D_FF_EXPERT, D), D_FF_EXPERT ** -0.5),
        "norm_final": gain(ks[23], (D,)),
    }

def reference(x, norm_mix, w_in, conv_a, w_a_out, conv_b, ln_b_g, ln_b_b, w_b_out,
              ln_c_g, ln_c_b, w_s, b_s, w_c_out, w_o, norm_ffn, w_group, b_group,
              w_router, b_router, w1, w3, w2, norm_final):
    for l in range(DEPTH):
        x = x + mixer_block(x, norm_mix[l], w_in[l], conv_a[l], w_a_out[l], conv_b[l],
                            ln_b_g[l], ln_b_b[l], w_b_out[l], ln_c_g[l], ln_c_b[l],
                            w_s[l], b_s[l], w_c_out[l], w_o[l])
        x = x + hier_moe(rms_norm(x, norm_ffn[l]), w_group[l], b_group[l], w_router[l],
                         b_router[l], w1[l], w3[l], w2[l])
    return rms_norm(x, norm_final)


_drawn_inputs = setup_inputs


def setup_inputs(seed=0):
    import zlib

    import numpy as np

    out = dict(_drawn_inputs(seed))
    spreads = {}
    factors = {'ln_b_g': 14.351,
     'ln_b_b': 16.005,
     'ln_c_g': 17.052,
     'ln_c_b': 17.515,
     'b_s': 16.673,
     'b_group': 23.65,
     'b_router': 19.996,
     'norm_final': 8.436,
     'norm_ffn': 4.401}
    for name, (base, spread) in spreads.items():
        noise = np.random.default_rng([zlib.crc32(name.encode()), seed]).standard_normal(out[name].shape)
        drawn = base * np.exp(spread * noise) if base else spread * noise
        out[name] = __import__('jax').numpy.asarray(drawn.astype(out[name].dtype))
    for name, factor in factors.items():
        out[name] = (out[name] * factor).astype(out[name].dtype)
    return out
```

```python
from contextlib import ExitStack

import concourse.bass as bass
from concourse import mybir

F32 = mybir.dt.float32
F32R = mybir.dt.float32r
I32 = mybir.dt.int32
U32 = mybir.dt.uint32
ALU = mybir.AluOpType
ACT = mybir.ActivationFunctionType
AX = mybir.AxisListType

P = 128
D = 1024
T = 512
K = D // P
TT = T // P
TAPS_A, TAPS_B = 3, 31
PAD_A, PAD_B = TAPS_A // 2, TAPS_B // 2
G, EPG = 4, 8
E = G * EPG
FF = 512
SLOTS = 64
ITEMS = 2 * T // SLOTS + E
PAIRS_MIN = T // SLOTS
ITEMS_HS = ITEMS + 2
FILL_ROWS = P
FILLS = ITEMS_HS * SLOTS // FILL_ROWS
FILLS_PER = 5
FILLS_PER_PAIR_END = 1 + FILLS // FILLS_PER
assert FILLS % FILLS_PER == 0
RMS_EPS, LN_EPS = 1e-6, 1e-5
BIG = 1e30
CREDIT = 2

PB, PC, PA1, PA2, PGA, PGC, PGB, PW, PEND = 0, 8, 16, 24, 28, 36, 44, 52, 56

C_ID, C_ONE, C_UP, C_THR, C_I32, C_I48, C_EVEN = 0, 128, 256, 384, 392, 424, 472
C_N = 496
V_CB, V_CA, V_GM, V_BG, V_BB, V_CG, V_CBI = 0, 31, 34, 35, 36, 37, 38
V_N = 39


def build(nc, xT, x, stream, params, wsT, bs, wr, rbias, gffn, gfin, w13, w2, consts, lower, out):
    with ExitStack() as ctx:
        def sem(name):
            return ctx.enter_context(nc.semaphore(name))

        KB = 1024
        base = (nc.sbuf_base + 63) // 64 * 64

        def at(name, shape, dt, offset):
            return nc.alloc_sbuf_tensor_at(name, shape, dt, offset=base + offset)

        R0, R1, R2 = 0, 48 * KB, 80 * KB
        R3 = R2 + K * (T + 2 * PAD_B) * 4
        R4 = R3 + 16 * KB
        R5 = R4 + 16 * KB
        R6 = R5 + 16 * KB
        R7 = R6 + K * (T + 2 * PAD_A) * 4
        R8 = R7 + 32 * KB
        w_raw = [at(f"w_raw{s}", [P, 2, K, P], F32, R0 + 8 * KB * s) for s in range(2)]
        w_hi = [at(f"w_hi{s}", [P, 2, K, P], F32R, R0 + 16 * KB + 8 * KB * s) for s in range(2)]
        w_lo = [at(f"w_lo{s}", [P, 2, K, P], F32R, R0 + 32 * KB + 8 * KB * s) for s in range(2)]
        h_hi = at("h_hi", [P, K, T], F32R, R1)
        h_lo = at("h_lo", [P, K, T], F32R, R1 + 16 * KB)
        zb_pad = at("zb_pad", [P, K, T + 2 * PAD_B], F32, R2)
        zb = at("zb", [P, K, T], F32, R3)
        zb_lo = at("zb_lo", [P, K, T], F32R, R3)
        u = at("u", [P, K, T], F32, R4)
        zc_lo = at("zc_lo", [P, K, T], F32R, R4)
        v = at("v", [P, K, T], F32, R5)
        zc_hi = at("zc_hi", [P, K, T], F32R, R5)
        xt = at("xt", [P, K, T], F32, R6)
        ca_pad = at("ca_pad", [P, K, T + 2 * PAD_A], F32, R6)
        ws_sb = at("ws_sb", [P, K, P], F32, R6)
        bs_sb = at("bs_sb", [P, K, P], F32, R6 + 4 * KB)
        sqz = [at(f"sqz{s}", [P, T], F32, R6 + 8 * KB + 2 * KB * s) for s in range(2)]
        sqz_sum = at("sqz_sum", [P, T], F32, R6 + 12 * KB)
        x_tok = at("x_tok", [P, TT, D], F32, R6)
        za_hi = at("za_hi", [P, K, T], F32R, R7)
        za_lo = at("za_lo", [P, K, T], F32R, R7 + 16 * KB)
        zb_hi = at("zb_hi", [P, K, T], F32R, R7)
        xsq = at("xsq", [P, K, T], F32, R7)
        zeros = at("zeros", [P, D], F32, R7 + 16 * KB)
        v_sum = at("v_sum", [P, T], F32, R7 + 20 * KB)
        merged = at("merged", [P, K, T], F32, R2)
        sqv = [at(f"sqv{s}", [P, T], F32, R2 + 2 * KB * s) for s in range(2)]
        sqv_sum = at("sqv_sum", [P, T], F32, R2 + 4 * KB)
        m_hi = at("m_hi", [P, K, T], F32R, R4)
        m_lo = at("m_lo", [P, K, T], F32R, R5)
        cst = at("cst", [P, C_N], F32, R8)
        par = at("par", [P, K, V_N], F32, R8 + 2 * KB)
        sig = [at(f"sig{s}", [P, T], F32, R8 + 3328 + 2 * KB * s) for s in range(2)]
        tmp = [at(f"tmp{s}", [P, T], F32, R8 + 3328 + 4 * KB + 2 * KB * s) for s in range(2)]
        z_sum = at("z_sum", [P, T], F32, R8 + 3328 + 8 * KB)
        assert K * V_N * 4 <= 1280 and C_N * 4 <= 2 * KB
        small = at("small", [P, 64], F32, R8 + 3328 + 10 * KB)
        assert base + R8 + 3328 + 10 * KB + 256 <= nc.sbuf_usable_end
        ident, ones, upper = cst[:, C_ID:C_ID + P], cst[:, C_ONE:C_ONE + P], cst[:, C_UP:C_UP + P]
        eps_rms, eps_ln = small[:, 0:1], small[:, 1:2]
        v_rstd, z_rstd = tmp[0][:, :], z_sum[:, :]
        sum_sq, rstd = small[:, 4:8], small[:, 8:12]

        ew13 = [at("ew13_0", [P, K, 2, FF], F32, R7), at("ew13_1", [P, K, 2, FF], F32, R0)]
        ew2 = [at("ew2_0", [P, FF // P, D], F32, R3), at("ew2_1", [P, FF // P, D], F32, R0 + 32 * KB)]
        h2 = at("h2", [P, TT, D], F32, R1)
        gffn_sb = at("gffn_sb", [P, D], F32, R1 + 16 * KB)
        lower_sb = at("lower_sb", [P, E, E], F32, R1 + 20 * KB)
        wr_sb = at("wr_sb", [P, K, G + E], F32, R1 + 24 * KB)
        rb_sb = at("rb_sb", [P, G + E], F32, R1 + 26 * KB)
        RT = R1 + 26 * KB + 256
        h2T = at("h2T", [P, TT, K, P], F32, R2)
        scr = at("scr", [P, 48 * E], F32, R4)
        o = [RT]

        def small_tile(name, shape, dt=F32):
            n = 4
            for s in shape[1:]:
                n *= s
            t = at(name, shape, dt, o[0])
            o[0] += (n + 31) // 32 * 32
            assert o[0] <= R2
            return t

        lg = small_tile("lg", [P, TT, G + E])
        gmax = small_tile("gmax", [P, TT])
        geq = small_tile("geq", [P, TT, G])
        gidx = small_tile("gidx", [P, TT])
        ghot = small_tile("ghot", [P, TT, G])
        gexp = small_tile("gexp", [P, TT, G])
        gden = small_tile("gden", [P, TT])
        elog = [small_tile(f"elog{k}", [P, TT, E]) for k in range(2)]
        emax = [small_tile(f"emax{k}", [P, TT]) for k in range(2)]
        eidx = [small_tile(f"eidx{k}", [P, TT]) for k in range(2)]
        wgt = [small_tile(f"wgt{k}", [P, TT]) for k in range(2)]
        R4b = R4 + 6 * KB
        o2 = [R4b]

        def late_tile(name, shape, dt=F32):
            n = 4
            for s in shape[1:]:
                n *= s
            t = at(name, shape, dt, o2[0])
            o2[0] += (n + 31) // 32 * 32
            assert o2[0] <= R5 + 16 * KB
            return t

        ehot = [late_tile(f"ehot{k}", [P, TT, E]) for k in range(2)]
        both = late_tile("both", [P, TT, E])
        slot = late_tile("slot", [P, TT, E])
        count = late_tile("count", [P, E])
        blocks = late_tile("blocks", [P, E])
        istart = late_tile("istart", [P, E])
        iend = late_tile("iend", [P, E])
        posf = late_tile("posf", [P, 2, TT])
        pos = late_tile("pos", [P, 2, TT], U32)
        itemf = late_tile("itemf", [P, 48])
        tabf = late_tile("tabf", [P, 2])
        tab = late_tile("tab", [P, E + 2 + 48], I32)
        T_END, T_N, T_EXP = 0, E, E + 2
        xg = [late_tile(f"xg{s}", [SLOTS, D]) for s in range(2)]
        xgT = [late_tile(f"xgT{s}", [P, K, SLOTS]) for s in range(2)]
        esig = [at(f"esig{s}", [P, FF // 2], F32, R1 + 1 * KB * s) for s in range(2)]
        eup = [at(f"eup{s}", [P, FF // 2], F32, R1 + 2 * KB + 1 * KB * s) for s in range(2)]
        eact = [at(f"eact{s}", [P, FF // 2], F32, R1 + 4 * KB + 1 * KB * s) for s in range(2)]
        eactT = [at(f"eactT{s}", [P, 2, P], F32, R1 + 6 * KB + 1 * KB * s) for s in range(2)]
        ey = [at(f"ey{s}", [P, FF], F32, R1 + 8 * KB + 2 * KB * s) for s in range(2)]
        gfin_sb = at("gfin_sb", [P, D], F32, R2)
        got = [[at(f"got{k}{t}", [P, D], F32, R0 + 4 * KB * (k * TT + t)) for t in range(TT)] for k in range(2)]
        junk = at("junk", [P, D], F32, R2 + 8 * KB)

        hs = nc.dram_tensor("hs", [ITEMS_HS * SLOTS, D], F32, kind="Internal").ap()
        ys = nc.dram_tensor("ys", [ITEMS_HS * SLOTS, D], F32, kind="Internal").ap()

        def bank(name, shape):
            return ctx.enter_context(nc.psum_tensor(name, shape, F32))

        mm = [[bank(f"mm{s}{j}", [P, T]) for j in range(2)] for s in range(2)]
        st = [bank(f"st{s}", [P, T]) for s in range(2)]
        tr = [bank(f"tr{s}", [P, TT, P]) for s in range(2)]
        px = [tr[s][:, :, :].rearrange("p a b -> p (a b)") for s in range(2)]

        names = """cst_ld par_ld x_ld tok_ld ws_ld g_ld fin_ld fill_done xsq_ready xsq_sum eps_set stat rms_root h_step
            h_ready h_hi_ready h_lo_ready w_hi_ready w_lo_ready mm_done b_free c_free a1_free a2_free ga_free gc_free
            gb_free w_free sig_ready ca_ready tap zb_conv vsum_done zsum_done v_centred v_sq v_sq_added
            z_centred z_sq z_sq_added v_root z_root v_step v_ready vt_ps vt_ready sp_ps sp_free sp_step zc_ready zc_hi_ready
            zc_lo_ready za_step za_ready za_hi_ready za_lo_ready z_root_inv zs_step zs_norm z_inv eup_ready fs_inv edge_set all_stored zs_sig zb_ready zb_hi_ready
            zb_lo_ready m_step m_ready m_hi_ready m_lo_ready o_copied o_tr x1_ready
            ss_ready rs_root rs_ready h2_ready h2_ps h2T_ready lg_ps r_step r_exp r_expd hot_ready cum_ps tab_ready
            pos_ready scattered x_done x_copied m13_done esig_ready eact_ready ea_ps ea_copied y_ps y_copied
            gathered fs_ready fs_root fs_step fin_ready out_done zero_set""".split()
        S = {n: sem(n) for n in names}
        raw_ld = [sem(f"raw_ld{s}") for s in range(2)]
        w13_ld = [sem(f"w13_ld{s}") for s in range(2)]
        w2_ld = [sem(f"w2_ld{s}") for s in range(2)]
        xg_ld = [sem(f"xg_ld{s}") for s in range(2)]
        gathered = [sem(f"gathered{t}") for t in range(TT)]
        y_st = [sem(f"y_st{s}") for s in range(2)]

        block = ctx.enter_context(nc.Block())
        ds = bass.ds

        def ot(m):
            return [sig[0], sig[1], tmp[0], tmp[1]][m % 4]

        @block.sync
        def _(sp):
            sp.dma_start(xt[:, :, :], xT).then_inc(S["x_ld"], 16)
            sp.dma_start(par[:, :, :], params).then_inc(S["par_ld"], 16)
            sp.dma_start(cst[:, :], consts).then_inc(S["cst_ld"], 16)
            for s in range(2):
                sp.dma_start(w_raw[s][:, :, :, :], stream[s]).then_inc(raw_ld[s], 16)
            sp.wait_ge(S["zero_set"], 1)

            def next_pairs(i):
                for s in range(2):
                    sp.wait_ge(S["w_lo_ready"], 2 * i + s - 1)
                    sp.dma_start(w_raw[s][:, :, :, :], stream[2 * i + s]).then_inc(raw_ld[s], 16)

            with sp.Fori(1, FILLS_PER_PAIR_END) as i:
                next_pairs(i)
                for f in range(FILLS_PER):
                    row = ds((i - 1) * (FILLS_PER * FILL_ROWS) + f * FILL_ROWS, FILL_ROWS)
                    for slots in (hs, ys):
                        sp.dma_start(slots[row, :], zeros[:, :]).then_inc(S["fill_done"], 16)
            with sp.Fori(FILLS_PER_PAIR_END, PEND // 2) as i:
                next_pairs(i)
            for s in range(2):
                if s == 0:
                    sp.wait_ge(S["mm_done"], 2 * PW)
                else:
                    sp.wait_ge(S["mm_done"], 2 * PEND)
                    sp.wait_ge(S["w_lo_ready"], PEND)
                sp.dma_start(ew13[s][:, :, :, :], w13[s]).then_inc(w13_ld[s], 16)
                sp.dma_start(ew2[s][:, :, :], w2[s]).then_inc(w2_ld[s], 16)
            sp.wait_ge(S["tab_ready"], 1)
            with sp.Fori(1, E // 2) as i:
                for s in range(2):
                    done = sp.value_load(tab[0:1, ds(T_END + 2 * i + s - 2, 1)], min_val=1, max_val=ITEMS + 1)
                    sp.wait_ge(w13_ld[s], 16 * i)
                    sp.wait_ge(S["m13_done"], done)
                    sp.dma_start(ew13[s][:, :, :, :], w13[2 * i + s]).then_inc(w13_ld[s], 16)
                    sp.wait_ge(w2_ld[s], 16 * i)
                    sp.wait_ge(S["y_ps"], done)
                    sp.dma_start(ew2[s][:, :, :], w2[2 * i + s]).then_inc(w2_ld[s], 16)
            for t in range(TT):
                sp.wait_ge(S["fin_ready"], t + 1)
                sp.dma_start(out[t * P:(t + 1) * P, :], x_tok[:, t, :]).then_inc(S["out_done"], 16)
            sp.wait_ge(S["out_done"], 16 * TT)

        @block.tensor
        def _(pe):
            def tile(acc, s, j, hi, lo):
                for k in range(K):
                    nc.tensor.matmul(acc[:, :], w_hi[s][:, j, k, :], hi[:, k, :], start=(k == 0), stop=False)
                    nc.tensor.matmul(acc[:, :], w_hi[s][:, j, k, :], lo[:, k, :], start=False, stop=False)
                    last = nc.tensor.matmul(acc[:, :], w_lo[s][:, j, k, :], hi[:, k, :], start=False, stop=(k == K - 1))
                last.then_inc(S["mm_done"], 1)

            def pair(p, s, q, free, first, second, ready=None):
                pe.wait_ge(S["w_hi_ready"], p + 1)
                pe.wait_ge(S["w_lo_ready"], p + 1)
                pe.wait_ge(free, q + 1)
                tile(mm[s][0], s, 0, *first)
                if ready is not None:
                    pe.wait_ge(ready, K)
                tile(mm[s][1], s, 1, *second)

            def stage(base_pair, q0, pairs, free, first, second, ready=None):
                with pe.Fori(q0 // 2, (q0 + pairs) // 2) as i:
                    for s in range(2):
                        pair(2 * i + (base_pair + s), s, 2 * i + s, free, first, second, ready)

            h = (h_hi, h_lo)
            pe.wait_ge(S["cst_ld"], 16)
            pe.wait_ge(S["xsq_sum"], 3)
            nc.tensor.matmul(st[1][:, :], ones, xsq[:, 0, :], start=True, stop=True).then_inc(S["stat"], 1)
            pe.wait_ge(S["h_lo_ready"], K)
            pe.wait_ge(S["h_hi_ready"], K)
            pe.sem_inc(S["b_free"], CREDIT)
            stage(PB, 0, 8, S["b_free"], h, h)
            pe.wait_ge(S["b_free"], 8 + CREDIT)
            pe.sem_inc(S["c_free"], CREDIT)
            stage(PC, 0, 8, S["c_free"], h, h)
            pe.wait_ge(S["c_free"], 8 + CREDIT)
            pe.sem_inc(S["a1_free"], CREDIT)
            stage(PA1, 0, 8, S["a1_free"], h, h)
            pe.wait_ge(S["vsum_done"], K + 1)
            nc.tensor.matmul(st[0][:, :], ones, v_sum[:, :], start=True, stop=True).then_inc(S["stat"], 1)
            pe.wait_ge(S["a1_free"], 8 + CREDIT)
            pe.sem_inc(S["a2_free"], CREDIT)
            stage(PA2, 0, 4, S["a2_free"], h, h)
            pe.wait_ge(S["v_sq_added"], K + 1)
            nc.tensor.matmul(st[1][:, :], ones, sqv_sum[:, :], start=True, stop=True).then_inc(S["stat"], 1)
            pe.wait_ge(S["v_centred"], K)
            pe.wait_ge(S["zsum_done"], K + 1)
            nc.tensor.matmul(st[0][:, :], ones, z_sum[:, :], start=True, stop=True).then_inc(S["stat"], 1)
            pe.wait_ge(S["a2_free"], 4 + CREDIT)
            pe.sem_inc(S["ga_free"], CREDIT)
            stage(PGA, 0, 4, S["ga_free"], h, (za_hi, za_lo), S["za_lo_ready"])
            for m in range(K):
                pe.wait_ge(S["v_ready"], m + 1)
                if m >= 2:
                    pe.wait_ge(S["vt_ready"], m - 1)
                for n in range(TT):
                    last = nc.tensor.transpose(tr[m % 2][:, n, :], v[:, m, n * P:(n + 1) * P], ident)
                last.then_inc(S["vt_ps"], 1)
            pe.wait_ge(S["ws_ld"], 32)
            pe.wait_ge(S["vt_ready"], K)
            for m in range(K):
                if m >= 2:
                    pe.wait_ge(S["sp_free"], m - 1)
                for n in range(TT):
                    last = nc.tensor.matmul(tr[m % 2][:, n, :], v[:, m, n * P:(n + 1) * P], ws_sb[:, m, :],
                                            start=True, stop=True)
                last.then_inc(S["sp_ps"], 1)
            stage(PGA, 4, 4, S["ga_free"], h, (za_hi, za_lo), S["za_lo_ready"])
            pe.wait_ge(S["z_sq_added"], K + 1)
            pe.wait_ge(S["v_root"], 1)
            nc.tensor.matmul(st[1][:, :], ones, sqz_sum[:, :], start=True, stop=True).then_inc(S["stat"], 1)
            pe.wait_ge(S["ga_free"], 8 + CREDIT)
            pe.sem_inc(S["gc_free"], CREDIT)
            stage(PGC, 0, 8, S["gc_free"], h, (zc_hi, zc_lo), S["zc_lo_ready"])
            pe.wait_ge(S["gc_free"], 8 + CREDIT)
            pe.sem_inc(S["gb_free"], CREDIT)
            stage(PGB, 0, 8, S["gb_free"], h, (zb_hi, zb_lo), S["zb_lo_ready"])
            pe.wait_ge(S["gb_free"], 8 + CREDIT)
            pe.wait_ge(S["m_lo_ready"], K)

            def out_transposes(m):
                pe.wait_ge(S["o_copied"], m + 1)
                if m >= 2:
                    pe.wait_ge(S["x1_ready"], m - 1)
                for n in range(TT):
                    last = nc.tensor.transpose(tr[m % 2][:, n, :], ot(m)[:, n * P:(n + 1) * P], ident)
                last.then_inc(S["o_tr"], 1)

            pe.sem_inc(S["w_free"], CREDIT)
            for q in range(4):
                pair(PW + q, q % 2, q, S["w_free"], (m_hi, m_lo), (m_hi, m_lo))
                if q:
                    for m in (2 * q - 2, 2 * q - 1):
                        out_transposes(m)
            for m in (K - 2, K - 1):
                out_transposes(m)

            for t in range(TT):
                pe.wait_ge(S["h2_ready"], t + 1)
                if t == 0:
                    pe.wait_ge(S["w_free"], 4 + CREDIT)
                for half in range(2):
                    if t >= 2:
                        pe.wait_ge(S["h2T_ready"], 2 * (t - 2) + half + 1)
                    for k in range(4):
                        last = nc.tensor.transpose(mm[t % 2][half][:, k * P:(k + 1) * P],
                                                   h2[:, t, (4 * half + k) * P:(4 * half + k + 1) * P], ident)
                    last.then_inc(S["h2_ps"], 1)
            pe.wait_ge(S["g_ld"], 64)
            for t in range(TT):
                pe.wait_ge(S["h2T_ready"], 2 * t + 2)
                for k in range(K):
                    last = nc.tensor.matmul(st[0][:, t * (G + E):(t + 1) * (G + E)], h2T[:, t, k, :], wr_sb[:, k, :],
                                            start=(k == 0), stop=(k == K - 1))
            last.then_inc(S["lg_ps"], 1)
            pe.wait_ge(S["hot_ready"], 1)
            for t in range(TT):
                for b in range(t):
                    nc.tensor.matmul(st[1][:, t * E:(t + 1) * E], ones, both[:, b, :], start=(b == 0), stop=False)
                nc.tensor.matmul(st[1][:, t * E:(t + 1) * E], upper, both[:, t, :], start=(t == 0), stop=True)
            for t in range(TT):
                last = nc.tensor.matmul(st[1][:, TT * E:(TT + 1) * E], ones, both[:, t, :],
                                        start=(t == 0), stop=(t == TT - 1))
            last.then_inc(S["cum_ps"], 1)

            pe.wait_ge(S["tab_ready"], 1)
            pairs = pe.value_load(tab[0:1, T_N:T_N + 1], min_val=PAIRS_MIN, max_val=ITEMS // 2)
            pe.sem_inc(S["m13_done"], 1)
            pe.sem_inc(S["y_ps"], 1)

            def rows_T(s):
                for k in range(K):
                    last = nc.tensor.transpose(px[s][:, k * SLOTS:(k + 1) * SLOTS], xg[s][:, k * P:(k + 1) * P],
                                               ident[0:SLOTS, 0:SLOTS])
                last.then_inc(S["x_done"], 1)

            def up(s, w):
                for k in range(K):
                    for j in range(2):
                        last = nc.tensor.matmul(mm[s][0][j * SLOTS:(j + 1) * SLOTS, :], xgT[s][:, k, :],
                                                ew13[w][:, k, j, :], start=(k == 0), stop=(k == K - 1))
                last.then_inc(S["m13_done"], 1)

            def down(s, w):
                for c in range(FF // P):
                    for j in range(2):
                        last = nc.tensor.matmul(mm[s][1][j * SLOTS:(j + 1) * SLOTS, :],
                                                eactT[s][:, c % 2, (c // 2) * SLOTS:(c // 2 + 1) * SLOTS],
                                                ew2[w][:, c, j * FF:(j + 1) * FF],
                                                start=(c == 0), stop=(c == FF // P - 1))
                last.then_inc(S["y_ps"], 1)

            pe.wait_ge(xg_ld[0], 16)
            rows_T(0)
            with pe.Fori(0, pairs) as i:
                for s in range(2):
                    n = 2 * i + s
                    e = pe.value_load(tab[0:1, ds(n + T_EXP, 1)], min_val=0, max_val=E - 1)
                    turn = pe.snap(e // 2 * 16 + 16)
                    odd = pe.snap(e % 2)
                    pe.wait_ge(xg_ld[1 - s], i * 16 + (16 if s == 0 else 32))
                    pe.wait_ge(S["x_copied"], n + 1)
                    with pe.If(odd == 0):
                        pe.wait_ge(w13_ld[0], turn)
                        up(s, 0)
                    with pe.Else():
                        pe.wait_ge(w13_ld[1], turn)
                        up(s, 1)
                    rows_T(1 - s)
                    pe.wait_ge(S["eact_ready"], n + 1)
                    for c in range(2):
                        last = nc.tensor.transpose(st[s][:, c * P:(c + 1) * P], eact[s][:, c * P:(c + 1) * P], ident)
                    last.then_inc(S["ea_ps"], 1)
                    pe.wait_ge(S["ea_copied"], n + 1)
                    with pe.If(odd == 0):
                        pe.wait_ge(w2_ld[0], turn)
                        down(s, 0)
                    with pe.Else():
                        pe.wait_ge(w2_ld[1], turn)
                        down(s, 1)

        @block.scalar
        def _(act):
            A = nc.scalar.activation

            def split(p, s, turn, done=None):
                if done is not None:
                    act.wait_ge(S["mm_done"], done)
                act.wait_ge(raw_ld[s], 16 * turn)
                A(w_hi[s][:, :, :, :], w_raw[s][:, :, :, :], ACT.Copy).then_inc(S["w_hi_ready"], 1)

            act.wait_ge(S["x_ld"], 16)
            for half in range(2):
                A(xsq[:, 4 * half:4 * half + 4, :], xt[:, 4 * half:4 * half + 4, :], ACT.Square).then_inc(S["xsq_ready"], 1)
            for s in range(2):
                split(s, s, 1)
            act.wait_ge(S["stat"], 1)
            act.wait_ge(S["eps_set"], 2)
            A(tmp[0][:, :], st[1][:, :], ACT.Sqrt, scale=1.0 / D, bias=eps_rms).then_inc(S["rms_root"], 1)
            for k in range(K):
                act.wait_ge(S["h_ready"], k + 1)
                A(h_hi[:, k, :], xt[:, k, :], ACT.Copy).then_inc(S["h_hi_ready"], 1)

            with act.Fori(0, 4) as i:
                for s in range(2):
                    p = 2 * i + (PB + s)
                    act.wait_ge(S["mm_done"], 2 * p + 2)
                    A(sig[s][:, :], mm[s][1][:, :], ACT.Sigmoid).then_inc(S["sig_ready"], 1)
                    split(p, s, i + (PB // 2 + 2))
            with act.Fori(0, 4) as i:
                for s in range(2):
                    p, q = 2 * i + (PC + s), 2 * i + s
                    act.wait_ge(S["mm_done"], 2 * p + 1)
                    A(u[:, q, :], mm[s][0][:, :], ACT.Gelu_apprx_tanh)
                    act.wait_ge(S["mm_done"], 2 * p + 2)
                    A(v[:, q, :], mm[s][1][:, :], ACT.Gelu_apprx_tanh).then_inc(S["c_free"], 1)
                    split(p, s, i + (PC // 2 + 2))
            with act.Fori(0, 4) as i:
                for s in range(2):
                    p = 2 * i + (PA1 + s)
                    act.wait_ge(S["mm_done"], 2 * p + 1)
                    A(sig[s][:, :], mm[s][0][:, :], ACT.Copy).then_inc(S["ca_ready"], 1)
                    split(p, s, i + (PA1 // 2 + 2), 2 * p + 2)
            def squares(a, q, ring, centred, ready, added):
                for j in range(2):
                    act.wait_ge(centred, 2 * q + (j + 1))
                    act.wait_ge(added, 2 * q + j if j else 2 * q + 1)
                    A(ring[j][:, :], a[:, ds(2 * q + j, 1), :], ACT.Square).then_inc(ready, 1)

            with act.Fori(0, 2) as i:
                for s in range(2):
                    p, q = 2 * i + (PA2 + s), 2 * i + s
                    squares(v, q, sqv, S["v_centred"], S["v_sq"], S["v_sq_added"])
                    for j in range(2):
                        act.wait_ge(S["za_ready"], 2 * q + j + 1)
                        A(za_hi[:, 2 * q + j, :], tmp[j][:, :], ACT.Copy).then_inc(S["za_hi_ready"], 1)
                    split(p, s, i + (PA2 // 2 + 2), 2 * p + 2)
            act.wait_ge(S["stat"], 3)
            act.wait_ge(S["za_lo_ready"], K)
            A(v_rstd, st[1][:, :], ACT.Sqrt, scale=1.0 / D, bias=eps_ln).then_inc(S["v_root"], 1)

            def gate(p, s):
                act.wait_ge(S["mm_done"], 2 * p + 1)
                A(sig[s][:, :], mm[s][0][:, :], ACT.Sigmoid).then_inc(S["sig_ready"], 1)

            with act.Fori(0, 2) as i:
                for s in range(2):
                    p = 2 * i + (PGA + s)
                    squares(zb, 2 * i + s, sqz, S["z_centred"], S["z_sq"], S["z_sq_added"])
                    gate(p, s)
                    split(p, s, i + (PGA // 2 + 2), 2 * p + 2)
            for m in range(K):
                act.wait_ge(S["vt_ps"], m + 1)
                A(v[:, m, :], px[m % 2], ACT.Copy).then_inc(S["vt_ready"], 1)
            for m in range(K):
                act.wait_ge(S["zc_ready"], m + 1)
                A(zc_hi[:, m, :], u[:, m, :], ACT.Copy).then_inc(S["zc_hi_ready"], 1)
            with act.Fori(2, 4) as i:
                for s in range(2):
                    p = 2 * i + (PGA + s)
                    gate(p, s)
                    split(p, s, i + (PGA // 2 + 2), 2 * p + 2)
            act.wait_ge(S["stat"], 5)
            act.wait_ge(S["stat"], 4)
            A(z_rstd, st[1][:, :], ACT.Sqrt, scale=1.0 / D, bias=eps_ln).then_inc(S["z_root"], 1)
            with act.Fori(0, 4) as i:
                for s in range(2):
                    p, q = 2 * i + (PGC + s), 2 * i + s
                    act.wait_ge(S["zs_norm"], q + 1)
                    A(tmp[s][:, :], zb[:, ds(q, 1), :], ACT.Sigmoid,
                      scale=par[:, ds(q, 1), V_BG:V_BG + 1], bias=par[:, ds(q, 1), V_BB:V_BB + 1]).then_inc(S["zs_sig"], 1)
                    gate(p, s)
                    act.wait_ge(S["zb_ready"], q + 1)
                    A(zb_hi[:, ds(q, 1), :], zb[:, ds(q, 1), :], ACT.Copy).then_inc(S["zb_hi_ready"], 1)
                    split(p, s, i + (PGC // 2 + 2), 2 * p + 2)
            with act.Fori(0, 4) as i:
                for s in range(2):
                    p, q = 2 * i + (PGB + s), 2 * i + s
                    gate(p, s)
                    act.wait_ge(S["gb_free"], q + 1 + CREDIT)
                    A(m_hi[:, ds(q, 1), :], merged[:, ds(q, 1), :], ACT.Copy).then_inc(S["m_hi_ready"], 1)
                    split(p, s, i + (PGB // 2 + 2), 2 * p + 2)
            for q in range(4):
                s, p = q % 2, PW + q
                for j in range(2):
                    m = 2 * q + j
                    act.wait_ge(S["mm_done"], 2 * p + j + 1)
                    if m >= 4:
                        act.wait_ge(S["o_tr"], m - 3)
                    last = A(ot(m)[:, :], mm[s][j][:, :], ACT.Copy)
                    last.then_inc(S["o_copied"], 1)
                act.wait_ge(S["o_copied"], 2 * q + 2)
                act.sem_inc(S["w_free"], 1)
                if q < 2:
                    split(p, s, p // 2 + 2)
            act.wait_ge(S["x1_ready"], K)
            for t in range(TT):
                A(h2[:, t, :], x_tok[:, t, :], ACT.Square, accum_out=sum_sq[:, t:t + 1]).then_inc(S["ss_ready"], 1)
            act.wait_ge(S["ss_ready"], TT)
            A(rstd, sum_sq, ACT.Sqrt, scale=1.0 / D, bias=eps_rms).then_inc(S["rs_root"], 1)
            for t in range(TT):
                for half in range(2):
                    act.wait_ge(S["h2_ps"], 2 * t + half + 1)
                    A(h2T[:, t, 4 * half:4 * half + 4, :].rearrange("p a b -> p (a b)"), mm[t % 2][half][:, :],
                      ACT.Copy).then_inc(S["h2T_ready"], 1)
            act.wait_ge(S["r_exp"], 1)
            A(gexp[:, :, :], gexp[:, :, :], ACT.Exp).then_inc(S["r_expd"], 1)
            act.wait_ge(S["r_exp"], 2)
            A(wgt[1][:, :], wgt[1][:, :], ACT.Exp).then_inc(S["r_expd"], 1)

            act.wait_ge(S["tab_ready"], 1)
            act.wait_ge(S["scattered"], 16 * 2 * TT)
            pairs = act.value_load(tab[0:1, T_N:T_N + 1], min_val=PAIRS_MIN, max_val=ITEMS // 2)

            def rows(s, n):
                act.wait_ge(S["x_done"], n + 1)
                A(xgT[s][:, :, :].rearrange("p a b -> p (a b)"), px[s], ACT.Copy).then_inc(S["x_copied"], 1)

            rows(0, 0)

            def item(s, n, stored):
                act.wait_ge(S["m13_done"], n + 2)
                A(esig[s][:, :], mm[s][0][:, 0:FF // 2], ACT.Sigmoid).then_inc(S["esig_ready"], 1)
                rows(1 - s, n + 1)
                act.wait_ge(S["ea_ps"], n + 1)
                A(eactT[s][:, :, :].rearrange("p a b -> p (a b)"), st[s][:, 0:2 * P], ACT.Copy).then_inc(S["ea_copied"], 1)
                if stored is not None:
                    act.wait_ge(y_st[s], stored)
                act.wait_ge(S["y_ps"], n + 2)
                A(ey[s][:, :], mm[s][1][:, :], ACT.Copy).then_inc(S["y_copied"], 1)

            for s in range(2):
                item(s, s, None)
            with act.Fori(1, pairs) as i:
                for s in range(2):
                    item(s, 2 * i + s, 32 * i)
            for t in range(TT):
                act.wait_ge(S["fs_ready"], t + 1)
                A(junk[:, :], x_tok[:, t, :], ACT.Square, accum_out=sum_sq[:, t:t + 1]).then_inc(S["ss_ready"], 1)
                act.wait_ge(S["ss_ready"], TT + t + 1)
                A(rstd[:, t:t + 1], sum_sq[:, t:t + 1], ACT.Sqrt, scale=1.0 / D, bias=eps_rms).then_inc(S["fs_root"], 1)

        @block.gpsimd
        def _(pool):
            TTo = nc.gpsimd.tensor_tensor
            nc.gpsimd.memset(zeros[:, :], 0.0).then_inc(S["zero_set"], 1)

            def split(p, s):
                pool.wait_ge(S["w_hi_ready"], p + 1)
                TTo(w_lo[s][:, :, :, :], w_raw[s][:, :, :, :], w_hi[s][:, :, :, :].bitcast(F32),
                    ALU.subtract).then_inc(S["w_lo_ready"], 1)

            for s in range(2):
                split(s, s)

            def add(acc, x_ap, done, first):
                if first:
                    nc.gpsimd.tensor_copy(acc, x_ap).then_inc(done, 1)
                else:
                    TTo(acc, acc, x_ap, ALU.add).then_inc(done, 1)

            with pool.Fori(0, 4) as i:
                for s in range(2):
                    split(2 * i + (PB + 2 + s), s)
            nc.gpsimd.memset(v_sum[:, :], 0.0).then_inc(S["vsum_done"], 1)
            nc.gpsimd.memset(z_sum[:, :], 0.0).then_inc(S["zsum_done"], 1)
            with pool.Fori(0, 4) as i:
                for s in range(2):
                    q = 2 * i + s
                    pool.wait_ge(S["c_free"], q + 1 + CREDIT)
                    pool.wait_ge(S["vsum_done"], q + 1)
                    TTo(v_sum[:, :], v_sum[:, :], v[:, q, :], ALU.add).then_inc(S["vsum_done"], 1)
                    split(2 * i + (PC + 2 + s), s)
                pool.wait_ge(S["zb_conv"], i + 1)
                pool.wait_ge(S["zsum_done"], i + 1)
                TTo(z_sum[:, :], z_sum[:, :], zb[:, ds(i, 1), :], ALU.add).then_inc(S["zsum_done"], 1)
            with pool.Fori(0, 4) as i:
                for s in range(2):
                    split(2 * i + (PA1 + 2 + s), s)
                pool.wait_ge(S["zb_conv"], i + 5)
                pool.wait_ge(S["zsum_done"], i + 5)
                TTo(z_sum[:, :], z_sum[:, :], zb[:, ds(i + 4, 1), :], ALU.add).then_inc(S["zsum_done"], 1)
            pool.wait_ge(S["zsum_done"], K + 1)

            def squares(acc, q, ring, ready, added):
                for j in range(2):
                    pool.wait_ge(ready, 2 * q + (j + 1))
                    pool.wait_ge(added, 2 * q + (j + 1))
                    TTo(acc[:, :], acc[:, :], ring[j][:, :], ALU.add).then_inc(added, 1)

            pool.wait_ge(S["zb_conv"], K)
            nc.gpsimd.memset(sqv_sum[:, :], 0.0).then_inc(S["v_sq_added"], 1)
            with pool.Fori(0, 2) as i:
                for s in range(2):
                    squares(sqv_sum, 2 * i + s, sqv, S["v_sq"], S["v_sq_added"])
                    split(2 * i + (PA2 + 2 + s), s)
            pool.wait_ge(S["za_lo_ready"], K)
            nc.gpsimd.memset(sqz_sum[:, :], 0.0).then_inc(S["z_sq_added"], 1)
            pool.dma_start(ws_sb[:, :, :], wsT).then_inc(S["ws_ld"], 16)
            pool.dma_start(bs_sb[:, :, :].rearrange("p a b -> p (a b)"), bs.partition_broadcast(P)).then_inc(S["ws_ld"], 16)
            with pool.Fori(0, 2) as i:
                for s in range(2):
                    squares(sqz_sum, 2 * i + s, sqz, S["z_sq"], S["z_sq_added"])
                    split(2 * i + (PGA + 2 + s), s)
            with pool.Fori(2, 4) as i:
                for s in range(2):
                    split(2 * i + (PGA + 2 + s), s)
            pool.wait_ge(S["sp_free"], K)
            pool.wait_ge(S["z_root"], 1)
            pool.dma_start(x_tok[:, :, :], x.rearrange("(t p) d -> p t d", p=P)).then_inc(S["tok_ld"], 16)
            with pool.Fori(0, (PEND - PGC) // 2 - 1) as i:
                for s in range(2):
                    split(2 * i + (PGC + 2 + s), s)

            pool.wait_ge(S["mm_done"], 2 * PW)
            pool.dma_start(gffn_sb[:, :], gffn.partition_broadcast(P)).then_inc(S["g_ld"], 16)
            pool.dma_start(lower_sb[:, :, :].rearrange("p a b -> p (a b)"), lower.partition_broadcast(P)).then_inc(S["g_ld"], 16)
            pool.dma_start(wr_sb[:, :, :], wr).then_inc(S["g_ld"], 16)
            pool.dma_start(rb_sb[:, :], rbias.partition_broadcast(P)).then_inc(S["g_ld"], 16)
            pool.wait_ge(S["fill_done"], 16 * 2 * FILLS)
            pool.wait_ge(S["pos_ready"], 1)
            pool.wait_ge(S["h2_ready"], TT)
            for k in range(2):
                for t in range(TT):
                    nc.gpsimd.indirect_dma_start(
                        hs[:, :], bass.IndirectOffsetOnAxis(ap=pos[:, k, t:t + 1], axis=0), h2[:, t, :], None,
                        bounds_check=ITEMS_HS * SLOTS - 1).then_inc(S["scattered"], 16)
            pool.wait_ge(S["scattered"], 16 * 2 * TT)
            pool.wait_ge(S["h2T_ready"], 2 * TT)
            pool.wait_ge(S["lg_ps"], 1)
            pool.dma_start(gfin_sb[:, :], gfin.partition_broadcast(P)).then_inc(S["fin_ld"], 16)
            pool.wait_ge(S["tab_ready"], 1)
            pairs = pool.value_load(tab[0:1, T_N:T_N + 1], min_val=PAIRS_MIN, max_val=ITEMS // 2)
            for s in range(2):
                pool.dma_start(xg[s][:, :], hs[s * SLOTS:(s + 1) * SLOTS, :]).then_inc(xg_ld[s], 16)
            with pool.Fori(0, pairs) as i:
                for s in range(2):
                    n = 2 * i + s
                    pool.wait_ge(S["x_done"], n + 1)
                    pool.dma_start(xg[s][:, :], hs[ds((n + 2) * SLOTS, SLOTS), :]).then_inc(xg_ld[s], 16)
                    pool.wait_ge(S["y_copied"], n + 1)
                    for j in range(2):
                        pool.dma_start(ys[ds(n * SLOTS, SLOTS), j * FF:(j + 1) * FF],
                                       ey[s][j * SLOTS:(j + 1) * SLOTS, :]).then_inc(y_st[s], 16)
            stored = pool.snap(pairs * 32)
            loaded = pool.snap(pairs * 16 + 16)
            for s in range(2):
                pool.wait_ge(y_st[s], stored)
                pool.wait_ge(xg_ld[s], loaded)
            for landed in (*w13_ld, *w2_ld):
                pool.wait_ge(landed, 16 * (E // 2))
            pool.sem_inc(S["all_stored"], 1)
            pool.wait_ge(S["all_stored"], 1)
            for t in range(TT):
                for k in range(2):
                    nc.gpsimd.indirect_dma_start(
                        got[k][t][:, :], None, ys[:, :], bass.IndirectOffsetOnAxis(ap=pos[:, k, t:t + 1], axis=0),
                        bounds_check=ITEMS_HS * SLOTS - 1).then_inc(gathered[t], 16)

        @block.vector
        def _(dve):
            V = nc.vector
            STT, TTo, TS = V.scalar_tensor_tensor, V.tensor_tensor, V.tensor_scalar

            for edge in (zb_pad[:, :, 0:PAD_B], zb_pad[:, :, PAD_B + T:]):
                V.memset(edge, 0.0).then_inc(S["edge_set"], 1)
            V.memset(eps_rms, RMS_EPS).then_inc(S["eps_set"], 1)
            V.memset(eps_ln, LN_EPS).then_inc(S["eps_set"], 1)
            dve.wait_ge(S["xsq_ready"], 2)
            for step, n in enumerate((4, 2, 1)):
                TTo(xsq[:, 0:n, :], xsq[:, 0:n, :], xsq[:, n:2 * n, :], ALU.add).then_inc(S["xsq_sum"], 1)
                dve.wait_ge(S["xsq_sum"], step + 1)
            dve.wait_ge(S["rms_root"], 1)
            V.reciprocal(tmp[0][:, :], tmp[0][:, :]).then_inc(S["h_step"], 1)
            dve.wait_ge(S["h_step"], 1)
            dve.wait_ge(S["par_ld"], 16)
            for k in range(K):
                STT(xt[:, k, :], xt[:, k, :], par[:, k, V_GM:V_GM + 1], tmp[0][:, :], ALU.mult, ALU.mult)\
                    .then_inc(S["h_ready"], 1)
            for k in range(K):
                dve.wait_ge(S["h_hi_ready"], k + 1)
                TTo(h_lo[:, k, :], xt[:, k, :], h_hi[:, k, :].bitcast(F32), ALU.subtract).then_inc(S["h_lo_ready"], 1)
            dve.wait_ge(S["h_lo_ready"], K)
            for edge in (ca_pad[:, :, 0:PAD_A], ca_pad[:, :, PAD_A + T:]):
                V.memset(edge, 0.0).then_inc(S["edge_set"], 1)
            dve.wait_ge(S["edge_set"], 4)

            def taps_b(m, j0, j1):
                for j in range(j0, j1):
                    acc = zb[:, ds(m, 1), :] if j % 2 == 0 else tmp[0][:, :]
                    z = zb_pad[:, ds(m, 1), j:j + T]
                    w = par[:, ds(m, 1), V_CB + j:V_CB + j + 1]
                    if j < 2:
                        TS(acc, z, w, None, ALU.mult).then_inc(S["tap"], 1)
                    else:
                        dve.wait_ge(S["tap"], m * (TAPS_B + 1) + (j - 1))
                        STT(acc, z, w, acc, ALU.mult, ALU.add).then_inc(S["tap"], 1)
                if j1 == TAPS_B:
                    dve.wait_ge(S["tap"], m * (TAPS_B + 1) + TAPS_B)
                    TTo(zb[:, ds(m, 1), :], zb[:, ds(m, 1), :], tmp[0][:, :], ALU.add).then_inc(S["zb_conv"], 1)
                    dve.wait_ge(S["zb_conv"], m + 1)
                    dve.sem_inc(S["tap"], 1)

            def conv_part(m, s):
                half = (TAPS_B + 1) // 2
                taps_b(m, *((0, half) if s == 0 else (half, TAPS_B)))

            def value_gated(q, s):
                dve.wait_ge(S["sig_ready"], q + 1)
                TTo(zb_pad[:, ds(q, 1), PAD_B:PAD_B + T], mm[s][0][:, :], sig[s][:, :], ALU.mult)\
                    .then_inc(S["b_free"], 1)

            def a_product(q, s):
                dve.wait_ge(S["ca_ready"], q + 1)
                dve.wait_ge(S["mm_done"], 2 * q + (2 * (PA1 + 1)))
                TTo(ca_pad[:, ds(q, 1), PAD_A:PAD_A + T], mm[s][1][:, :], sig[s][:, :], ALU.mult)\
                    .then_inc(S["a1_free"], 1)

            for s in range(2):
                value_gated(s, s)
            with dve.Fori(1, 4) as i:
                for s in range(2):
                    value_gated(2 * i + s, s)
                    dve.wait_ge(S["b_free"], i + (1 + CREDIT))
                    conv_part(i - 1, s)
            dve.wait_ge(S["b_free"], 8 + CREDIT)
            with dve.Fori(3, 7) as i:
                for s in range(2):
                    conv_part(i, s)
            for s in range(2):
                a_product(s, s)
                conv_part(K - 1, s)
            with dve.Fori(1, 4) as i:
                for s in range(2):
                    a_product(2 * i + s, s)
            def centre(a, m, done):
                STT(a[:, ds(m, 1), :], st[0][:, :], -1.0 / D, a[:, ds(m, 1), :], ALU.mult, ALU.add).then_inc(done, 1)

            dve.wait_ge(S["stat"], 2)
            dve.wait_ge(S["a1_free"], 8 + CREDIT)
            dve.wait_ge(S["fill_done"], 16 * 2 * FILLS)
            with dve.Fori(0, 2) as i:
                for s in range(2):
                    p, q = 2 * i + (PA2 + s), 2 * i + s
                    for j in range(2):
                        centre(v, 2 * q + j, S["v_centred"])
                    for j in range(2):
                        m = 2 * q + j
                        for tap in range(TAPS_A):
                            c = ca_pad[:, ds(m, 1), tap:tap + T]
                            w = par[:, ds(m, 1), V_CA + tap:V_CA + tap + 1]
                            if tap == 0:
                                TS(sig[j][:, :], c, w, None, ALU.mult).then_inc(S["za_step"], 1)
                            else:
                                STT(sig[j][:, :], c, w, sig[j][:, :], ALU.mult, ALU.add).then_inc(S["za_step"], 1)
                            dve.wait_ge(S["za_step"], m * TAPS_A + (tap + 1))
                        dve.wait_ge(S["mm_done"], 2 * p + j + 1)
                        TTo(tmp[j][:, :], mm[s][j][:, :], sig[j][:, :], ALU.mult).then_inc(S["za_ready"], 1)
                    dve.wait_ge(S["za_ready"], 2 * q + 2)
                    dve.sem_inc(S["a2_free"], 1)
                    for j in range(2):
                        m = 2 * q + j
                        dve.wait_ge(S["za_hi_ready"], m + 1)
                        TTo(za_lo[:, ds(m, 1), :], tmp[j][:, :], za_hi[:, ds(m, 1), :].bitcast(F32), ALU.subtract)\
                            .then_inc(S["za_lo_ready"], 1)
            dve.wait_ge(S["v_root"], 1)
            V.reciprocal(v_rstd, v_rstd).then_inc(S["v_step"], 1)
            dve.wait_ge(S["v_step"], 1)
            dve.wait_ge(S["v_centred"], K)

            def first_gated(q, s):
                dve.wait_ge(S["sig_ready"], q + 9)
                dve.wait_ge(S["mm_done"], 2 * q + (2 * (PGA + 1)))
                TTo(merged[:, ds(q, 1), :], mm[s][1][:, :], sig[s][:, :], ALU.mult).then_inc(S["ga_free"], 1)

            dve.wait_ge(S["stat"], 4)
            with dve.Fori(0, 2) as i:
                for s in range(2):
                    q = 2 * i + s
                    for m in (2 * q, 2 * q + 1):
                        TTo(v[:, ds(m, 1), :], v[:, ds(m, 1), :], v_rstd, ALU.mult).then_inc(S["v_step"], 1)
                        centre(zb, m, S["z_centred"])
                    for m in (2 * q, 2 * q + 1):
                        dve.wait_ge(S["v_step"], m + 2)
                        TS(v[:, ds(m, 1), :], v[:, ds(m, 1), :], par[:, ds(m, 1), V_CG:V_CG + 1],
                           par[:, ds(m, 1), V_CBI:V_CBI + 1], ALU.mult, ALU.add).then_inc(S["v_ready"], 1)
                    first_gated(q, s)
            dve.wait_ge(S["ws_ld"], 32)
            for m in range(K):
                dve.wait_ge(S["sp_ps"], m + 1)
                t = tmp[m % 2]
                TTo(t[:, :].rearrange("p (n q) -> p n q", n=TT), tr[m % 2][:, :, :],
                    bs_sb[:, m, :].unsqueeze(1).to_broadcast([P, TT, P]), ALU.add).then_inc(S["sp_free"], 1)
                dve.wait_ge(S["sp_free"], m + 1)
                TTo(u[:, m, :], u[:, m, :], t[:, :], ALU.mult).then_inc(S["zc_ready"], 1)
            for m in range(K):
                dve.wait_ge(S["zc_hi_ready"], m + 1)
                TTo(zc_lo[:, m, :], u[:, m, :], zc_hi[:, m, :].bitcast(F32), ALU.subtract).then_inc(S["zc_lo_ready"], 1)
            with dve.Fori(2, 4) as i:
                for s in range(2):
                    first_gated(2 * i + s, s)
            dve.wait_ge(S["ga_free"], 8 + CREDIT)
            dve.wait_ge(S["z_root"], 1)
            V.reciprocal(z_rstd, z_rstd).then_inc(S["z_inv"], 1)
            dve.wait_ge(S["z_inv"], 1)

            def add_gated(p, q, s, first_sig, step, free):
                dve.wait_ge(S["sig_ready"], q + first_sig)
                dve.wait_ge(S["mm_done"], 2 * p + 2)
                TTo(sig[s][:, :], mm[s][1][:, :], sig[s][:, :], ALU.mult).then_inc(S["m_step"], 1)
                dve.wait_ge(S["m_step"], q + step)
                TTo(merged[:, ds(q, 1), :], merged[:, ds(q, 1), :], sig[s][:, :], ALU.add).then_inc(free, 1)

            with dve.Fori(0, 4) as i:
                for s in range(2):
                    p, q = 2 * i + (PGC + s), 2 * i + s
                    z = zb[:, ds(q, 1), :]
                    TTo(z, z, z_rstd, ALU.mult).then_inc(S["zs_norm"], 1)
                    dve.wait_ge(S["zs_sig"], q + 1)
                    TS(z, z, par[:, ds(q, 1), V_BG:V_BG + 1], par[:, ds(q, 1), V_BB:V_BB + 1], ALU.mult, ALU.add)\
                        .then_inc(S["zs_step"], 1)
                    dve.wait_ge(S["zs_step"], q + 1)
                    TTo(z, z, tmp[s][:, :], ALU.mult).then_inc(S["zb_ready"], 1)
                    add_gated(p, q, s, 17, 1, S["gc_free"])
                    dve.wait_ge(S["zb_hi_ready"], q + 1)
                    TTo(zb_lo[:, ds(q, 1), :], z, zb_hi[:, ds(q, 1), :].bitcast(F32), ALU.subtract)\
                        .then_inc(S["zb_lo_ready"], 1)
            dve.wait_ge(S["gc_free"], 8 + CREDIT)
            with dve.Fori(0, 4) as i:
                for s in range(2):
                    p, q = 2 * i + (PGB + s), 2 * i + s
                    add_gated(p, q, s, 25, 9, S["gb_free"])
                    dve.wait_ge(S["m_hi_ready"], q + 1)
                    TTo(m_lo[:, ds(q, 1), :], merged[:, ds(q, 1), :], m_hi[:, ds(q, 1), :].bitcast(F32), ALU.subtract)\
                        .then_inc(S["m_lo_ready"], 1)
            dve.wait_ge(S["tok_ld"], 16)
            for m in range(K):
                dve.wait_ge(S["o_tr"], m + 1)
                xm = x_tok[:, :, m * P:(m + 1) * P]
                TTo(xm, xm, tr[m % 2][:, :, :], ALU.add).then_inc(S["x1_ready"], 1)
            dve.wait_ge(S["rs_root"], 1)
            V.reciprocal(rstd, rstd).then_inc(S["rs_ready"], 1)
            dve.wait_ge(S["rs_ready"], 1)
            dve.wait_ge(S["g_ld"], 64)
            for t in range(TT):
                STT(h2[:, t, :], x_tok[:, t, :], rstd[:, t:t + 1], gffn_sb[:, :], ALU.mult, ALU.mult)\
                    .then_inc(S["h2_ready"], 1)

            steps = [0]

            def step(ins):
                steps[0] += 1
                ins.then_inc(S["r_step"], 1)
                dve.wait_ge(S["r_step"], steps[0])

            def over(ap, shape, axis):
                return ap.unsqueeze(axis).to_broadcast(shape)

            def first_max(values, top, hot, where, width):
                shape = [P, TT, width]
                index = over(cst[:, C_I32:C_I32 + width], shape, 1)
                step(V.tensor_reduce(top[:, :], values, AX.X, ALU.max))
                step(TTo(hot[:, :, :], values, over(top[:, :], shape, 2), ALU.is_equal))
                step(STT(hot[:, :, :], hot[:, :, :], -100.0, index, ALU.mult, ALU.add))
                step(V.tensor_reduce(where[:, :], hot[:, :, :], AX.X, ALU.min))
                step(STT(hot[:, :, :], index, -100.0, over(where[:, :], shape, 2), ALU.add, ALU.is_equal))

            dve.wait_ge(S["lg_ps"], 1)
            step(TTo(lg[:, :, :], st[0][:, 0:TT * (G + E)].rearrange("p (t e) -> p t e", t=TT),
                     over(rb_sb[:, :], [P, TT, G + E], 1), ALU.add))
            first_max(lg[:, :, 0:G], gmax, ghot, gidx, G)
            step(TTo(gexp[:, :, :], lg[:, :, 0:G], over(gmax[:, :], [P, TT, G], 2), ALU.subtract))
            dve.sem_inc(S["r_exp"], 1)
            step(TS(ghot[:, :, :], ghot[:, :, :], BIG, -BIG, ALU.mult, ALU.add))
            by_group = [P, TT, G, EPG]
            step(TTo(elog[0][:, :, :].rearrange("p t (g e) -> p t g e", g=G),
                     lg[:, :, G:].rearrange("p t (g e) -> p t g e", g=G), over(ghot[:, :, :], by_group, 3), ALU.add))
            first_max(elog[0][:, :, :], emax[0], ehot[0], eidx[0], E)
            step(STT(elog[1][:, :, :], ehot[0][:, :, :], -4 * BIG, elog[0][:, :, :], ALU.mult, ALU.add))
            first_max(elog[1][:, :, :], emax[1], ehot[1], eidx[1], E)
            step(TTo(both[:, :, :], ehot[0][:, :, :], ehot[1][:, :, :], ALU.add))
            dve.sem_inc(S["hot_ready"], 1)
            step(TTo(wgt[1][:, :], emax[1][:, :], emax[0][:, :], ALU.subtract))
            dve.sem_inc(S["r_exp"], 1)
            dve.wait_ge(S["r_expd"], 2)
            step(V.tensor_reduce(gden[:, :], gexp[:, :, :], AX.X, ALU.add))
            step(STT(wgt[0][:, :], wgt[1][:, :], 1.0, gden[:, :], ALU.add, ALU.mult))
            step(V.reciprocal(wgt[0][:, :], wgt[0][:, :]))
            step(TTo(wgt[1][:, :], wgt[1][:, :], wgt[0][:, :], ALU.mult))
            dve.wait_ge(S["cum_ps"], 1)
            step(V.tensor_copy(count[:, :], st[1][:, TT * E:(TT + 1) * E]))
            cmp = scr[:, 0:E * 8].rearrange("p (e b) -> p e b", e=E)
            step(TTo(cmp, over(count[:, :], [P, E, 8], 2), over(cst[:, C_THR:C_THR + 8], [P, E, 8], 1), ALU.is_gt))
            step(V.tensor_reduce(blocks[:, :], cmp, AX.X, ALU.add))
            before = scr[:, 0:E * E].rearrange("p (e f) -> p e f", e=E)
            step(TTo(before, lower_sb[:, :, :], over(blocks[:, :], [P, E, E], 1), ALU.mult))
            step(V.tensor_reduce(istart[:, :], before, AX.X, ALU.add))
            step(TTo(iend[:, :], istart[:, :], blocks[:, :], ALU.add))
            step(STT(slot[:, :, :], over(istart[:, :], [P, TT, E], 1), float(SLOTS),
                     st[1][:, 0:TT * E].rearrange("p (t e) -> p t e", t=TT), ALU.mult, ALU.add))
            for k in range(2):
                step(TTo(ehot[k][:, :, :], ehot[k][:, :, :], slot[:, :, :], ALU.mult))
                step(V.tensor_reduce(posf[:, k, :], ehot[k][:, :, :], AX.X, ALU.add))
            V.tensor_copy(pos[:, :, :], posf[:, :, :]).then_inc(S["pos_ready"], 1)
            owner = scr[:, :].rearrange("p (i e) -> p i e", e=E)
            step(TTo(owner, over(iend[:, :], [P, 48, E], 1), over(cst[:, C_I48:C_I48 + 48], [P, 48, E], 2), ALU.is_le))
            step(V.tensor_reduce(itemf[:, :], owner, AX.X, ALU.add))
            step(TS(itemf[:, :], itemf[:, :], float(E - 1), None, ALU.min))
            evens = scr[:, 0:24]
            step(TTo(evens, iend[:, E - 1:E].to_broadcast([P, 24]), cst[:, C_EVEN:C_EVEN + 24], ALU.is_gt))
            step(V.tensor_reduce(tabf[:, 0:1], evens, AX.X, ALU.add))
            step(TS(tab[:, T_END:T_END + E], iend[:, :], 1.0, None, ALU.add))
            step(V.tensor_copy(tab[:, T_N:T_N + 1], tabf[:, 0:1]))
            step(V.tensor_copy(tab[:, T_EXP:T_EXP + 48], itemf[:, :]))
            dve.sem_inc(S["tab_ready"], 1)

            pairs = dve.value_load(tab[0:1, T_N:T_N + 1], min_val=PAIRS_MIN, max_val=ITEMS // 2)
            with dve.Fori(0, pairs) as i:
                for s in range(2):
                    n = 2 * i + s
                    dve.wait_ge(S["esig_ready"], n + 1)
                    TTo(eup[s][:, :], mm[s][0][:, 0:FF // 2], esig[s][:, :], ALU.mult).then_inc(S["eup_ready"], 1)
                    dve.wait_ge(S["eup_ready"], n + 1)
                    TTo(eact[s][:, :], mm[s][0][:, FF // 2:], eup[s][:, :], ALU.mult).then_inc(S["eact_ready"], 1)
            for t in range(TT):
                dve.wait_ge(gathered[t], 32)
                for k in range(2):
                    STT(x_tok[:, t, :], got[k][t][:, :], wgt[k][:, t:t + 1], x_tok[:, t, :], ALU.mult, ALU.add)\
                        .then_inc(S["fs_ready"] if k else S["fs_step"], 1)
                    if k == 0:
                        dve.wait_ge(S["fs_step"], t + 1)
            dve.wait_ge(S["fin_ld"], 16)
            for t in range(TT):
                dve.wait_ge(S["fs_root"], t + 1)
                V.reciprocal(rstd[:, t:t + 1], rstd[:, t:t + 1]).then_inc(S["fs_inv"], 1)
                dve.wait_ge(S["fs_inv"], t + 1)
                STT(x_tok[:, t, :], x_tok[:, t, :], rstd[:, t:t + 1], gfin_sb[:, :], ALU.mult, ALU.mult)\
                    .then_inc(S["fin_ready"], 1)


def kernel(x, norm_mix, w_in, conv_a, w_a_out, conv_b, ln_b_g, ln_b_b, w_b_out, ln_c_g, ln_c_b, w_s, b_s,
           w_c_out, w_o, norm_ffn, w_group, b_group, w_router, b_router, w1, w3, w2, norm_final):
    import numpy as np
    import concourse.bacc as bacc
    from concourse.bass_utils import run_bass_kernel_spmd

    def tiles(w):
        return w.reshape(K, P, -1, P).transpose(2, 1, 0, 3)

    def features(a):
        return a.reshape(-1, K, P).transpose(2, 1, 0)

    w_in = np.asarray(w_in)[0]
    cuts = np.cumsum([D] * 9)
    xa, ba, ca, val, gate, uc, vc, ga, gb, gc = [tiles(a) for a in np.split(w_in, cuts, axis=1)]
    wa, wb, wc, wo = [tiles(np.asarray(a)[0]) for a in (w_a_out, w_b_out, w_c_out, w_o)]

    def two(a, b):
        return np.stack([a, b], axis=2)

    def own(a):
        return two(a[0::2], a[1::2])

    stream = np.concatenate([two(val, gate), two(uc, vc), two(ca, xa), own(ba), two(ga, wa), two(gc, wc),
                             two(gb, wb), own(wo)])
    params = np.concatenate([features(np.asarray(a)) for a in
                             (conv_b[0], conv_a[0], norm_mix, ln_b_g, ln_b_b, ln_c_g, ln_c_b)], axis=2)
    w13 = np.stack([np.asarray(w1)[0].reshape(E, K, P, 2, FF // 2), np.asarray(w3)[0].reshape(E, K, P, 2, FF // 2)],
                   axis=4).transpose(0, 2, 1, 3, 4, 5).reshape(E, P, K, 2, FF)
    consts = np.zeros((P, C_N), np.float32)
    consts[:, C_ID:C_ID + P] = np.eye(P)
    consts[:, C_ONE:C_ONE + P] = 1
    consts[:, C_UP:C_UP + P] = np.triu(np.ones((P, P)), 1)
    consts[:, C_THR:C_THR + 8] = SLOTS * np.arange(8)
    consts[:, C_I32:C_I32 + E] = np.arange(E)
    consts[:, C_I48:C_I48 + 48] = np.arange(48)
    consts[:, C_EVEN:C_EVEN + 24] = 2 * np.arange(24)
    x2 = np.asarray(x)[0]
    arrays = {
        "xT": x2.T.reshape(K, P, T).transpose(1, 0, 2),
        "x": x2,
        "stream": stream,
        "params": params,
        "wsT": np.asarray(w_s)[0].transpose(2, 0, 1),
        "bs": np.asarray(b_s)[0].reshape(-1),
        "wr": np.concatenate([np.asarray(w_group)[0], np.asarray(w_router)[0]], axis=1)
        .reshape(K, P, G + E).transpose(1, 0, 2),
        "rbias": np.concatenate([np.asarray(b_group)[0], np.asarray(b_router)[0]]),
        "gffn": np.asarray(norm_ffn)[0],
        "gfin": np.asarray(norm_final),
        "w13": w13,
        "w2": np.asarray(w2)[0].reshape(E, FF // P, P, D).transpose(0, 2, 1, 3),
        "consts": consts,
        "lower": np.tril(np.ones((E, E), np.float32), -1).reshape(-1),
    }
    nc = bacc.Bacc("TRN2", target_bir_lowering=False, num_devices=1)
    feed, args = {}, []
    for name, a in arrays.items():
        a = np.ascontiguousarray(a, np.float32)
        feed[f"in_{name}"] = a
        args.append(nc.dram_tensor(f"in_{name}", a.shape, F32, kind="ExternalInput").ap())
    args.append(nc.dram_tensor("out_dram", (T, D), F32, kind="ExternalOutput").ap())
    build(nc, *args)
    r = run_bass_kernel_spmd(nc, [feed], core_ids=[0])
    return np.asarray(r.results[0]["out_dram"]).reshape(1, T, D)
```

```python
from contextlib import ExitStack

import concourse.bass as bass
from concourse import mybir

F32 = mybir.dt.float32
F32R = mybir.dt.float32r
I32 = mybir.dt.int32
U32 = mybir.dt.uint32
ALU = mybir.AluOpType
ACT = mybir.ActivationFunctionType
AX = mybir.AxisListType

P = 128
D = 1024
T = 512
K = D // P
TT = T // P
TAPS_A, TAPS_B = 3, 31
PAD_A, PAD_B = TAPS_A // 2, TAPS_B // 2
G, EPG = 4, 8
E = G * EPG
FF = 512
SLOTS = 64
ITEMS = 2 * T // SLOTS + E
PAIRS_MIN = T // SLOTS
ITEMS_HS = ITEMS + 2
RING = 3
TURNS = (E + RING - 1) // RING
assert TURNS <= 12
FILL_ROWS = P
FILLS = ITEMS_HS * SLOTS // FILL_ROWS
FILLS_PER = 5
FILLS_PER_PAIR_END = 1 + FILLS // FILLS_PER
assert FILLS % FILLS_PER == 0
RMS_EPS, LN_EPS = 1e-6, 1e-5
BIG = 1e30
CREDIT = 2

PB, PC, PA1, PA2, PGA, PGC, PGB, PW, PEND = 0, 8, 16, 24, 28, 36, 44, 52, 56

C_ID, C_ONE, C_UP, C_THR, C_I32, C_I48, C_EVEN = 0, 128, 256, 384, 392, 424, 472
C_TURN = 496
C_N = 508
V_CB, V_CA, V_GM, V_BG, V_BB, V_CG, V_CBI, V_GF = 0, 31, 34, 35, 36, 37, 38, 39
V_N = 40


def build(nc, xT, stream, params, wsT, bs, wr, rbias, gffn, gfin, w13, w2, consts, out):
    with ExitStack() as ctx:
        def sem(name):
            return ctx.enter_context(nc.semaphore(name))

        KB = 1024
        base = (nc.sbuf_base + 63) // 64 * 64

        def at(name, shape, dt, offset):
            return nc.alloc_sbuf_tensor_at(name, shape, dt, offset=base + offset)

        R0, R1, R2 = 0, 48 * KB, 80 * KB
        R3 = R2 + K * (T + 2 * PAD_B) * 4
        R4 = R3 + 16 * KB
        R5 = R4 + 16 * KB
        R6 = R5 + 16 * KB
        R7 = R6 + K * (T + 2 * PAD_A) * 4
        R8 = R7 + 32 * KB
        w_raw = [at(f"w_raw{s}", [P, 2, K, P], F32, R0 + 8 * KB * s) for s in range(2)]
        w_hi = [at(f"w_hi{s}", [P, 2, K, P], F32R, R0 + 16 * KB + 8 * KB * s) for s in range(2)]
        w_lo = [at(f"w_lo{s}", [P, 2, K, P], F32R, R0 + 32 * KB + 8 * KB * s) for s in range(2)]
        h_hi = at("h_hi", [P, K, T], F32R, R1)
        h_lo = at("h_lo", [P, K, T], F32R, R1 + 16 * KB)
        zb_pad = at("zb_pad", [P, K, T + 2 * PAD_B], F32, R2)
        zb = at("zb", [P, K, T], F32, R3)
        zb_lo = at("zb_lo", [P, K, T], F32R, R3)
        u = at("u", [P, K, T], F32, R4)
        zc_lo = at("zc_lo", [P, K, T], F32R, R4)
        v = at("v", [P, K, T], F32, R5)
        zc_hi = at("zc_hi", [P, K, T], F32R, R5)
        xt = at("xt", [P, K, T], F32, R6)
        ca_pad = at("ca_pad", [P, K, T + 2 * PAD_A], F32, R6)
        ws_sb = at("ws_sb", [P, K, P], F32, R6)
        bs_sb = at("bs_sb", [P, K, P], F32, R6 + 4 * KB)
        sqz = [at(f"sqz{s}", [P, T], F32, R6 + 8 * KB + 2 * KB * s) for s in range(2)]
        sqz_sum = at("sqz_sum", [P, T], F32, R6 + 12 * KB)
        x1T = at("x1T", [P, K, T], F32, R6)
        x_tok = at("x_tok", [P, TT, D], F32, R2)
        za_hi = at("za_hi", [P, K, T], F32R, R7)
        za_lo = at("za_lo", [P, K, T], F32R, R7 + 16 * KB)
        zb_hi = at("zb_hi", [P, K, T], F32R, R7)
        xsq = at("xsq", [P, K, T], F32, R7)
        zeros = at("zeros", [P, D], F32, R7 + 16 * KB)
        v_sum = at("v_sum", [P, T], F32, R7 + 20 * KB)
        merged = at("merged", [P, K, T], F32, R2)
        sqv = [at(f"sqv{s}", [P, T], F32, R2 + 2 * KB * s) for s in range(2)]
        sqv_sum = at("sqv_sum", [P, T], F32, R2 + 4 * KB)
        m_hi = at("m_hi", [P, K, T], F32R, R4)
        m_lo = at("m_lo", [P, K, T], F32R, R5)
        cst = at("cst", [P, C_N], F32, R8)
        par = at("par", [P, K, V_N], F32, R8 + 2 * KB)
        sig = [at(f"sig{s}", [P, T], F32, R8 + 3328 + 2 * KB * s) for s in range(2)]
        tmp = [at(f"tmp{s}", [P, T], F32, R8 + 3328 + 4 * KB + 2 * KB * s) for s in range(2)]
        z_sum = at("z_sum", [P, T], F32, R8 + 3328 + 8 * KB)
        assert K * V_N * 4 <= 1280 and C_N * 4 <= 2 * KB
        sq1 = sig
        lgT = sig[0]
        wr_sb = at("wr_sb", [P, K, P // 2], F32, R8 + 3328 + 4 * KB)
        gffn_sb = at("gffn_sb", [P, D], F32, R8 + 3328 + 6 * KB)
        small = at("small", [P, 64], F32, R8 + 3328 + 10 * KB)
        assert base + R8 + 3328 + 10 * KB + 256 <= nc.sbuf_usable_end
        rb_sb = small[:, 16:16 + G + E]
        ident, ones, upper = cst[:, C_ID:C_ID + P], cst[:, C_ONE:C_ONE + P], cst[:, C_UP:C_UP + P]
        eps_rms, eps_ln = small[:, 0:1], small[:, 1:2]
        v_rstd, z_rstd = tmp[0][:, :], z_sum[:, :]
        sum_sq, rstd = small[:, 4:8], small[:, 8:12]

        ew13 = [at(f"ew13_{b}", [P, K, 2, FF], F32, r) for b, r in enumerate((R7, R1, R0))]
        ew2 = [at(f"ew2_{b}", [P, FF // P, D], F32, r) for b, r in enumerate((R3, R5, R0 + 32 * KB))]
        h2 = at("h2", [P, TT, D], F32, R4)
        scr = at("scr", [P, 48 * E], F32, R6)
        RT = R6 + 6 * KB
        o = [RT]

        def small_tile(name, shape, dt=F32):
            n = 4
            for s in shape[1:]:
                n *= s
            t = at(name, shape, dt, o[0])
            o[0] += (n + 31) // 32 * 32
            assert o[0] <= R7
            return t

        lg = small_tile("lg", [P, TT, G + E])
        gmax = small_tile("gmax", [P, TT])
        geq = small_tile("geq", [P, TT, G])
        gidx = small_tile("gidx", [P, TT])
        ghot = small_tile("ghot", [P, TT, G])
        gexp = small_tile("gexp", [P, TT, G])
        gden = small_tile("gden", [P, TT])
        elog = [small_tile(f"elog{k}", [P, TT, E]) for k in range(2)]
        emax = [small_tile(f"emax{k}", [P, TT]) for k in range(2)]
        eidx = [small_tile(f"eidx{k}", [P, TT]) for k in range(2)]
        wgt = [small_tile(f"wgt{k}", [P, TT]) for k in range(2)]
        ehots = small_tile("ehots", [P, 2, TT, E])
        ehot = [ehots[:, k, :, :] for k in range(2)]
        both = small_tile("both", [P, TT, E])
        earlier = small_tile("earlier", [P, TT + 1, E])
        slot = small_tile("slot", [P, TT, E])
        PADDED = E // 2 + E
        blocks = small_tile("blocks", [P, PADDED])
        scan = [small_tile(f"scan{k}", [P, PADDED]) for k in range(2)]
        posf = small_tile("posf", [P, 2, TT])
        pos = small_tile("pos", [P, 2, TT], U32)
        itemf = small_tile("itemf", [P, 48])
        turnf = small_tile("turnf", [P, 48])
        buff = small_tile("buff", [P, 48])
        tabf = small_tile("tabf", [P, 2])
        tab = small_tile("tab", [P, E + 2 + 96], I32)
        T_END, T_N, T_TURN, T_BUF = 0, E, E + 2, E + 2 + 48
        xg = at("xg", [2 * SLOTS, D], F32, R4)
        xgT = at("xgT", [P, K, 2 * SLOTS], F32, R4 + 4 * KB)
        ey = [at(f"ey{s}", [P, FF], F32, R4 + 8 * KB + 2 * KB * s) for s in range(2)]
        esig = [at(f"esig{s}", [P, FF // 2], F32, R4 + 12 * KB + 1 * KB * s) for s in range(2)]
        eup = [at(f"eup{s}", [P, FF // 2], F32, R4 + 14 * KB + 1 * KB * s) for s in range(2)]
        eact = [at(f"eact{s}", [P, FF // 2], F32, R8 + 3328 + 1 * KB * s) for s in range(2)]
        eactT = [at(f"eactT{s}", [P, 2, P], F32, R8 + 3328 + 2 * KB + 1 * KB * s) for s in range(2)]
        gfin_sb = at("gfin_sb", [P, D], F32, R8 + 3328 + 6 * KB)
        got = [[at(f"got{k}{t}", [P, D], F32, R0 + 4 * KB * (k * TT + t)) for t in range(TT)] for k in range(2)]
        junk = at("junk", [P, D], F32, R0 + 32 * KB)

        hs = nc.dram_tensor("hs", [ITEMS_HS * SLOTS, D], F32, kind="Internal").ap()
        ys = nc.dram_tensor("ys", [ITEMS_HS * SLOTS, D], F32, kind="Internal").ap()

        def bank(name, shape):
            return ctx.enter_context(nc.psum_tensor(name, shape, F32))

        mm = [[bank(f"mm{s}{j}", [P, T]) for j in range(2)] for s in range(2)]
        st = [bank(f"st{s}", [P, T]) for s in range(2)]
        tr = [bank(f"tr{s}", [P, TT, P]) for s in range(2)]
        px = [tr[s][:, :, :].rearrange("p a b -> p (a b)") for s in range(2)]

        names = """cst_ld par_ld x_ld tok_ld ws_ld g_ld fin_ld fill_done xsq_ready xsq_sum eps_set stat rms_root h_step
            h_ready h_hi_ready h_lo_ready w_hi_ready w_lo_ready mm_done b_free c_free a1_free a2_free ga_free gc_free
            gb_free w_free sig_ready ca_ready tap zb_conv vsum_done zsum_done v_centred v_sq v_sq_added
            z_centred z_sq z_sq_added v_root z_root v_step v_ready vt_ps vt_ready sp_ps sp_free sp_step zc_ready zc_hi_ready
            zc_lo_ready za_step za_ready za_hi_ready za_lo_ready z_root_inv zs_step zs_norm z_inv eup_ready fs_inv edge_set all_stored zs_sig zb_ready zb_hi_ready
            zb_lo_ready m_step m_ready m_hi_ready m_lo_ready o_copied o_tr x1_ready
            ss_ready rs_root rs_ready h2_ready h2_ps h2T_ready lg_ps r_step r_exp r_expd hot_ready cum_ps tab_ready
            pos_ready xg_ld scattered x_done x_copied m13_done esig_ready eact_ready ea_ps ea_copied y_ps y_copied
            x1T_ready x1_sq_ready ss_mm lgT_ready lgt_ps routed_set act_tables scaled wr_ld wr_scaled preset
            fs_ready fs_root fs_step fin_ready out_done zero_set w_half_ready""".split()
        S = {n: sem(n) for n in names}
        x_ld = [sem(f"x_ld{c}") for c in range(K // 2)]
        raw_ld = [sem(f"raw_ld{s}") for s in range(2)]
        w13_ld = [sem(f"w13_ld{b}") for b in range(RING)]
        w2_ld = [sem(f"w2_ld{b}") for b in range(RING)]
        gathered = [sem(f"gathered{t}") for t in range(TT)]
        y_st = [sem(f"y_st{s}") for s in range(2)]

        block = ctx.enter_context(nc.Block())
        ds = bass.ds

        @block.sync
        def _(sp):
            for c in range(K // 2):
                sp.dma_start(xt[:, 2 * c:2 * c + 2, :], xT[:, 2 * c:2 * c + 2, :]).then_inc(x_ld[c], 16)
                if c == 0:
                    sp.dma_start(cst[:, :], consts).then_inc(S["cst_ld"], 16)
            sp.dma_start(par[:, :, :], params).then_inc(S["par_ld"], 16)
            for s in range(2):
                sp.dma_start(w_raw[s][:, :, :, :], stream[s]).then_inc(raw_ld[s], 16)
            sp.wait_ge(S["zero_set"], 1)

            def next_pairs(i):
                for s in range(2):
                    sp.wait_ge(S["w_lo_ready"], 2 * i + s - 1)
                    sp.dma_start(w_raw[s][:, :, :, :], stream[2 * i + s]).then_inc(raw_ld[s], 16)

            with sp.Fori(1, FILLS_PER_PAIR_END) as i:
                next_pairs(i)
                for f in range(FILLS_PER):
                    row = ds((i - 1) * (FILLS_PER * FILL_ROWS) + f * FILL_ROWS, FILL_ROWS)
                    for slots in (hs, ys):
                        sp.dma_start(slots[row, :], zeros[:, :]).then_inc(S["fill_done"], 16)
            with sp.Fori(FILLS_PER_PAIR_END, PEND // 2) as i:
                next_pairs(i)
            def load13(e, b):
                sp.dma_start(ew13[b][:, :, :, :], w13[e]).then_inc(w13_ld[b], 16)

            def load2(e, b):
                sp.dma_start(ew2[b][:, :, :], w2[e]).then_inc(w2_ld[b], 16)

            sp.wait_ge(S["mm_done"], 2 * PW)
            load13(0, 0)
            load2(0, 0)
            load13(1, 1)
            sp.wait_ge(S["mm_done"], 2 * PEND)
            sp.wait_ge(S["w_lo_ready"], PEND)
            load2(1, 1)
            load13(2, 2)
            load2(2, 2)

            def next_expert(i, b):
                e = RING * i + b
                done = sp.value_load(tab[0:1, ds(T_END + e - RING, 1)], min_val=1, max_val=ITEMS + 1)
                sp.wait_ge(w13_ld[b], 16 * i)
                sp.wait_ge(S["m13_done"], done)
                load13(e, b)
                sp.wait_ge(w2_ld[b], 16 * i)
                sp.wait_ge(S["y_ps"], done)
                load2(e, b)

            sp.wait_ge(S["tab_ready"], 1)
            with sp.Fori(1, E // RING) as i:
                for b in range(RING):
                    next_expert(i, b)
            for b in range(E % RING):
                next_expert(E // RING, b)
            for t in range(TT):
                sp.wait_ge(S["fin_ready"], t + 1)
                sp.dma_start(out[t * P:(t + 1) * P, :], x_tok[:, t, :]).then_inc(S["out_done"], 16)
            sp.wait_ge(S["out_done"], 16 * TT)

        @block.tensor
        def _(pe):
            def tile(acc, s, j, hi, lo, arriving=None):
                for k in range(K):
                    if arriving is not None:
                        pe.wait_ge(arriving, k + 1)
                    nc.tensor.matmul(acc[:, :], w_hi[s][:, j, k, :], hi[:, k, :], start=(k == 0), stop=False)
                    nc.tensor.matmul(acc[:, :], w_hi[s][:, j, k, :], lo[:, k, :], start=False, stop=False)
                    last = nc.tensor.matmul(acc[:, :], w_lo[s][:, j, k, :], hi[:, k, :], start=False, stop=(k == K - 1))
                last.then_inc(S["mm_done"], 1)

            def pair(p, s, q, free, first, second, ready=None, before=None):
                pe.wait_ge(S["w_hi_ready"], p + 1)
                pe.wait_ge(S["w_lo_ready"], p + 1)
                if before is not None:
                    pe.wait_ge(before[0], before[1] + (CREDIT - 1) + s)
                pe.wait_ge(free, q + 1)
                tile(mm[s][0], s, 0, *first)
                if ready is not None:
                    pe.wait_ge(ready, K)
                tile(mm[s][1], s, 1, *second)

            def stage(base_pair, q0, pairs, free, first, second, ready=None, before=None):
                with pe.Fori(q0 // 2, (q0 + pairs) // 2) as i:
                    for s in range(2):
                        pair(2 * i + (base_pair + s), s, 2 * i + s, free, first, second, ready, before)

            h = (h_hi, h_lo)
            pe.wait_ge(S["cst_ld"], 16)
            for c in range(K // 2):
                pe.wait_ge(S["xsq_sum"], c + 1)
                last = nc.tensor.matmul(st[1][:, :], ones, xsq[:, 2 * c, :], start=(c == 0), stop=(c == K // 2 - 1))
            last.then_inc(S["stat"], 1)
            pe.sem_inc(S["b_free"], CREDIT)
            for k in range(K):
                pe.wait_ge(S["h_lo_ready"], k + 1)
                if k == 0:
                    pe.wait_ge(S["w_half_ready"], 1)
                elif k == K // 2:
                    pe.wait_ge(S["w_lo_ready"], 1)
                for j in range(2):
                    acc = mm[0][j][:, :]
                    nc.tensor.matmul(acc, w_hi[0][:, j, k, :], h_hi[:, k, :], start=(k == 0), stop=False)
                    nc.tensor.matmul(acc, w_hi[0][:, j, k, :], h_lo[:, k, :], start=False, stop=False)
                    last = nc.tensor.matmul(acc, w_lo[0][:, j, k, :], h_hi[:, k, :], start=False, stop=(k == K - 1))
                    if k == K - 1:
                        last.then_inc(S["mm_done"], 1)
            pair(PB + 1, 1, 1, S["b_free"], h, h)
            stage(PB, 2, 6, S["b_free"], h, h)
            pe.sem_inc(S["c_free"], CREDIT)
            stage(PC, 0, 8, S["c_free"], h, h, before=(S["b_free"], 8))
            pe.sem_inc(S["a1_free"], CREDIT)
            stage(PA1, 0, 8, S["a1_free"], h, h, before=(S["c_free"], 8))
            pe.wait_ge(S["vsum_done"], K + 1)
            nc.tensor.matmul(st[0][:, :], ones, v_sum[:, :], start=True, stop=True).then_inc(S["stat"], 1)
            pe.sem_inc(S["a2_free"], CREDIT)
            stage(PA2, 0, 4, S["a2_free"], h, h, before=(S["a1_free"], 8))
            pe.wait_ge(S["v_sq_added"], K + 1)
            nc.tensor.matmul(st[1][:, :], ones, sqv_sum[:, :], start=True, stop=True).then_inc(S["stat"], 1)
            pe.wait_ge(S["v_centred"], K)
            pe.wait_ge(S["zsum_done"], K + 1)
            nc.tensor.matmul(st[0][:, :], ones, z_sum[:, :], start=True, stop=True).then_inc(S["stat"], 1)
            pe.sem_inc(S["ga_free"], CREDIT)
            stage(PGA, 0, 4, S["ga_free"], h, (za_hi, za_lo), S["za_lo_ready"], (S["a2_free"], 4))
            for m in range(K):
                pe.wait_ge(S["v_ready"], m + 1)
                if m >= 2:
                    pe.wait_ge(S["vt_ready"], m - 1)
                for n in range(TT):
                    last = nc.tensor.transpose(tr[m % 2][:, n, :], v[:, m, n * P:(n + 1) * P], ident)
                last.then_inc(S["vt_ps"], 1)
            pe.wait_ge(S["ws_ld"], 32)
            pe.wait_ge(S["vt_ready"], K)
            for m in range(K):
                if m >= 2:
                    pe.wait_ge(S["sp_free"], m - 1)
                for n in range(TT):
                    last = nc.tensor.matmul(tr[m % 2][:, n, :], v[:, m, n * P:(n + 1) * P], ws_sb[:, m, :],
                                            start=True, stop=True)
                last.then_inc(S["sp_ps"], 1)
            stage(PGA, 4, 4, S["ga_free"], h, (za_hi, za_lo), S["za_lo_ready"])
            pe.wait_ge(S["z_sq_added"], K + 1)
            pe.wait_ge(S["v_root"], 1)
            nc.tensor.matmul(st[1][:, :], ones, sqz_sum[:, :], start=True, stop=True).then_inc(S["stat"], 1)
            pe.sem_inc(S["gc_free"], CREDIT)
            stage(PGC, 0, 8, S["gc_free"], h, (zc_hi, zc_lo), S["zc_lo_ready"], (S["ga_free"], 8))
            pe.sem_inc(S["gb_free"], CREDIT)
            stage(PGB, 0, 8, S["gb_free"], h, (zb_hi, zb_lo), S["zb_lo_ready"], (S["gc_free"], 8))

            def logits(m):
                pe.wait_ge(S["x1T_ready"], m + 1)
                nc.tensor.matmul(st[0][0:P // 2, :], wr_sb[:, m, :], x1T[:, m, :], start=(m == 0), stop=(m == K - 1))
                pe.wait_ge(S["x1_sq_ready"], m + 1)
                nc.tensor.matmul(st[0][P // 2:, :], ones[:, 0:P // 2], sq1[m % 2][:, :],
                                 start=(m == 0), stop=(m == K - 1)).then_inc(S["ss_mm"], 1)

            def to_tokens(m):
                if m >= 2:
                    pe.wait_ge(S["x1_ready"], m - 1)
                for n in range(TT):
                    last = nc.tensor.transpose(tr[m % 2][:, n, :], x1T[:, m, n * P:(n + 1) * P], ident)
                last.then_inc(S["o_tr"], 1)

            pe.wait_ge(S["wr_scaled"], 1)
            for q in range(4):
                p, s = PW + q, q % 2
                pe.wait_ge(S["w_hi_ready"], p + 1)
                pe.wait_ge(S["w_lo_ready"], p + 1)
                if q < 2:
                    pe.wait_ge(S["gb_free"], 7 + q + CREDIT)
                else:
                    pe.wait_ge(S["x1T_ready"], 2 * q - 2)
                tile(mm[s][0], s, 0, m_hi, m_lo, S["m_lo_ready"] if q == 0 else None)
                tile(mm[s][1], s, 1, m_hi, m_lo)
                if q:
                    for m in (2 * q - 2, 2 * q - 1):
                        logits(m)
                        to_tokens(m)
            for m in (K - 2, K - 1):
                logits(m)
            for m in (K - 2, K - 1):
                to_tokens(m)

            pe.wait_ge(S["lgT_ready"], 1)
            for t in range(TT):
                last = nc.tensor.transpose(st[1][:, t * P:(t + 1) * P], lgT[:, t * P:(t + 1) * P], ident)
            last.then_inc(S["lg_ps"], 1)
            pe.wait_ge(S["hot_ready"], 1)
            nc.tensor.matmul(st[0][:, 0:(TT + 1) * E], ones, earlier[:, :, :].rearrange("p t e -> p (t e)"),
                             start=True, stop=False)
            nc.tensor.matmul(st[0][:, 0:TT * E], upper, both[:, :, :].rearrange("p t e -> p (t e)"),
                             start=False, stop=True).then_inc(S["cum_ps"], 1)

            pe.wait_ge(S["tab_ready"], 1)
            pairs = pe.value_load(tab[0:1, T_N:T_N + 1], min_val=PAIRS_MIN, max_val=ITEMS // 2)
            pe.sem_inc(S["m13_done"], 1)
            pe.sem_inc(S["y_ps"], 1)

            def rows_T():
                for k in range(K):
                    last = nc.tensor.transpose(tr[k // 4][:, k % 4, :], xg[:, k * P:(k + 1) * P], ident)
                last.then_inc(S["x_done"], 1)

            def up(s, w):
                for k in range(K):
                    for j in range(2):
                        last = nc.tensor.matmul(mm[s][0][j * SLOTS:(j + 1) * SLOTS, :], xgT[:, k, s * SLOTS:(s + 1) * SLOTS],
                                                ew13[w][:, k, j, :], start=(k == 0), stop=(k == K - 1))
                last.then_inc(S["m13_done"], 1)

            def down(s, w):
                for c in range(FF // P):
                    for j in range(2):
                        last = nc.tensor.matmul(mm[s][1][j * SLOTS:(j + 1) * SLOTS, :],
                                                eactT[s][:, c % 2, (c // 2) * SLOTS:(c // 2 + 1) * SLOTS],
                                                ew2[w][:, c, j * FF:(j + 1) * FF],
                                                start=(c == 0), stop=(c == FF // P - 1))
                last.then_inc(S["y_ps"], 1)

            def by_buffer(buf, turn, landed, products, s):
                with pe.If(buf == 0):
                    pe.wait_ge(landed[0], turn)
                    products(s, 0)
                with pe.Else():
                    with pe.If(buf == 1):
                        pe.wait_ge(landed[1], turn)
                        products(s, 1)
                    with pe.Else():
                        pe.wait_ge(landed[2], turn)
                        products(s, 2)

            pe.wait_ge(S["xg_ld"], 16)
            rows_T()
            with pe.Fori(0, pairs) as i:
                for s in range(2):
                    n = 2 * i + s
                    turn = pe.value_load(tab[0:1, ds(n + T_TURN, 1)], min_val=16, max_val=16 * TURNS)
                    buf = pe.value_load(tab[0:1, ds(n + T_BUF, 1)], min_val=0, max_val=RING - 1)
                    pe.wait_ge(S["x_copied"], i + 1)
                    by_buffer(buf, turn, w13_ld, up, s)
                    if s == 1:
                        pe.wait_ge(S["xg_ld"], i * 16 + 32)
                        rows_T()
                    pe.wait_ge(S["eact_ready"], n + 1)
                    for c in range(2):
                        last = nc.tensor.transpose(st[s][:, c * P:(c + 1) * P], eact[s][:, c * P:(c + 1) * P], ident)
                    last.then_inc(S["ea_ps"], 1)
                    pe.wait_ge(S["ea_copied"], n + 1)
                    by_buffer(buf, turn, w2_ld, down, s)

        @block.scalar
        def _(act):
            A = nc.scalar.activation

            def split(p, s, turn, done=None):
                if done is not None:
                    act.wait_ge(S["mm_done"], done)
                act.wait_ge(raw_ld[s], 16 * turn)
                A(w_hi[s][:, :, :, :], w_raw[s][:, :, :, :], ACT.Copy).then_inc(S["w_hi_ready"], 1)

            for c in range(K // 2):
                act.wait_ge(x_ld[c], 16)
                A(xsq[:, 2 * c:2 * c + 2, :], xt[:, 2 * c:2 * c + 2, :], ACT.Square).then_inc(S["xsq_ready"], 1)
            act.wait_ge(S["stat"], 1)
            act.wait_ge(S["eps_set"], 2)
            A(tmp[0][:, :], st[1][:, :], ACT.Sqrt, scale=1.0 / D, bias=eps_rms).then_inc(S["rms_root"], 1)
            for s in range(2):
                split(s, s, 1)
            for k in range(K):
                act.wait_ge(S["h_ready"], k + 1)
                A(h_hi[:, k, :], xt[:, k, :], ACT.Copy).then_inc(S["h_hi_ready"], 1)

            with act.Fori(0, 4) as i:
                for s in range(2):
                    p = 2 * i + (PB + s)
                    act.wait_ge(S["mm_done"], 2 * p + 2)
                    A(sig[s][:, :], mm[s][1][:, :], ACT.Sigmoid).then_inc(S["sig_ready"], 1)
                    split(p, s, i + (PB // 2 + 2))
            with act.Fori(0, 4) as i:
                for s in range(2):
                    p, q = 2 * i + (PC + s), 2 * i + s
                    act.wait_ge(S["mm_done"], 2 * p + 1)
                    A(u[:, q, :], mm[s][0][:, :], ACT.Gelu_apprx_tanh)
                    act.wait_ge(S["mm_done"], 2 * p + 2)
                    A(v[:, q, :], mm[s][1][:, :], ACT.Gelu_apprx_tanh).then_inc(S["c_free"], 1)
                    split(p, s, i + (PC // 2 + 2))
            with act.Fori(0, 4) as i:
                for s in range(2):
                    p = 2 * i + (PA1 + s)
                    act.wait_ge(S["mm_done"], 2 * p + 1)
                    A(sig[s][:, :], mm[s][0][:, :], ACT.Copy).then_inc(S["ca_ready"], 1)
                    split(p, s, i + (PA1 // 2 + 2), 2 * p + 2)
            def squares(a, q, ring, centred, ready, added):
                for j in range(2):
                    act.wait_ge(centred, 2 * q + (j + 1))
                    act.wait_ge(added, 2 * q + j if j else 2 * q + 1)
                    A(ring[j][:, :], a[:, ds(2 * q + j, 1), :], ACT.Square).then_inc(ready, 1)

            with act.Fori(0, 2) as i:
                for s in range(2):
                    p, q = 2 * i + (PA2 + s), 2 * i + s
                    squares(v, q, sqv, S["v_centred"], S["v_sq"], S["v_sq_added"])
                    for j in range(2):
                        act.wait_ge(S["za_ready"], 2 * q + j + 1)
                        A(za_hi[:, 2 * q + j, :], tmp[j][:, :], ACT.Copy).then_inc(S["za_hi_ready"], 1)
                    split(p, s, i + (PA2 // 2 + 2), 2 * p + 2)
            act.wait_ge(S["stat"], 3)
            act.wait_ge(S["za_lo_ready"], K)
            A(v_rstd, st[1][:, :], ACT.Sqrt, scale=1.0 / D, bias=eps_ln).then_inc(S["v_root"], 1)

            def gate(p, s):
                act.wait_ge(S["mm_done"], 2 * p + 1)
                A(sig[s][:, :], mm[s][0][:, :], ACT.Sigmoid).then_inc(S["sig_ready"], 1)

            with act.Fori(0, 2) as i:
                for s in range(2):
                    p = 2 * i + (PGA + s)
                    squares(zb, 2 * i + s, sqz, S["z_centred"], S["z_sq"], S["z_sq_added"])
                    gate(p, s)
                    split(p, s, i + (PGA // 2 + 2), 2 * p + 2)
            for m in range(K):
                act.wait_ge(S["vt_ps"], m + 1)
                A(v[:, m, :], px[m % 2], ACT.Copy).then_inc(S["vt_ready"], 1)
            for m in range(K):
                act.wait_ge(S["zc_ready"], m + 1)
                A(zc_hi[:, m, :], u[:, m, :], ACT.Copy).then_inc(S["zc_hi_ready"], 1)
            with act.Fori(2, 4) as i:
                for s in range(2):
                    p = 2 * i + (PGA + s)
                    gate(p, s)
                    split(p, s, i + (PGA // 2 + 2), 2 * p + 2)
            act.wait_ge(S["stat"], 5)
            act.wait_ge(S["stat"], 4)
            A(z_rstd, st[1][:, :], ACT.Sqrt, scale=1.0 / D, bias=eps_ln).then_inc(S["z_root"], 1)
            with act.Fori(0, 4) as i:
                for s in range(2):
                    p, q = 2 * i + (PGC + s), 2 * i + s
                    act.wait_ge(S["zs_norm"], q + 1)
                    A(tmp[s][:, :], zb[:, ds(q, 1), :], ACT.Sigmoid,
                      scale=par[:, ds(q, 1), V_BG:V_BG + 1], bias=par[:, ds(q, 1), V_BB:V_BB + 1]).then_inc(S["zs_sig"], 1)
                    gate(p, s)
                    act.wait_ge(S["zb_ready"], q + 1)
                    A(zb_hi[:, ds(q, 1), :], zb[:, ds(q, 1), :], ACT.Copy).then_inc(S["zb_hi_ready"], 1)
                    split(p, s, i + (PGC // 2 + 2), 2 * p + 2)
            with act.Fori(0, 4) as i:
                for s in range(2):
                    p, q = 2 * i + (PGB + s), 2 * i + s
                    gate(p, s)
                    act.wait_ge(S["gb_free"], q + 1 + CREDIT)
                    A(m_hi[:, ds(q, 1), :], merged[:, ds(q, 1), :], ACT.Copy).then_inc(S["m_hi_ready"], 1)
                    split(p, s, i + (PGB // 2 + 2), 2 * p + 2)
            act.wait_ge(S["gb_free"], 8 + CREDIT)
            A(small[:, 2:3], eps_ln, ACT.Sqrt)
            for q in range(4):
                s, p = q % 2, PW + q
                if q < 2:
                    split(p, s, p // 2 + 2, 2 * p + 2)
                for j in range(2):
                    m = 2 * q + j
                    act.wait_ge(S["x1T_ready"], m + 1)
                    if m >= 2:
                        act.wait_ge(S["ss_mm"], m - 1)
                    A(sq1[j][:, :], x1T[:, m, :], ACT.Square).then_inc(S["x1_sq_ready"], 1)
            act.wait_ge(S["ss_mm"], K)
            A(lgT[:, :], st[0][:, :], ACT.Copy).then_inc(S["lgT_ready"], 1)
            act.wait_ge(S["lg_ps"], 1)
            A(rstd, st[1][:, :].rearrange("p (t r) -> p t r", t=TT)[:, :, P // 2], ACT.Sqrt,
              scale=1.0 / D, bias=eps_rms).then_inc(S["rs_root"], 1)
            for m in (K - 2, K - 1):
                act.wait_ge(S["o_tr"], m + 1)
                A(x_tok[:, :, m * P:(m + 1) * P], tr[m % 2][:, :, :], ACT.Copy).then_inc(S["x1_ready"], 1)
            act.wait_ge(S["rs_ready"], 1)
            act.wait_ge(S["x1_ready"], K)
            for t in range(TT):
                A(h2[:, t, :], x_tok[:, t, :], ACT.Copy, scale=rstd[:, t:t + 1]).then_inc(S["scaled"], 1)
            act.wait_ge(S["r_exp"], 1)
            A(gexp[:, :, :], gexp[:, :, :], ACT.Exp).then_inc(S["r_expd"], 1)
            act.wait_ge(S["r_exp"], 2)
            A(wgt[1][:, :], wgt[1][:, :], ACT.Exp).then_inc(S["r_expd"], 1)
            A(small[:, 3:4], eps_ln, ACT.Sigmoid)

            act.wait_ge(S["tab_ready"], 1)
            act.wait_ge(S["scattered"], 16 * 2 * TT)
            pairs = act.value_load(tab[0:1, T_N:T_N + 1], min_val=PAIRS_MIN, max_val=ITEMS // 2)

            def rows(i):
                act.wait_ge(S["x_done"], i + 1)
                for half in range(2):
                    last = A(xgT[:, 4 * half:4 * half + 4, :], tr[half][:, :, :], ACT.Copy)
                last.then_inc(S["x_copied"], 1)

            rows(0)

            def item(s, n, stored, i):
                act.wait_ge(S["m13_done"], n + 2)
                A(esig[s][:, :], mm[s][0][:, 0:FF // 2], ACT.Sigmoid).then_inc(S["esig_ready"], 1)
                if s == 1:
                    rows(i + 1)
                act.wait_ge(S["ea_ps"], n + 1)
                A(eactT[s][:, :, :].rearrange("p a b -> p (a b)"), st[s][:, 0:2 * P], ACT.Copy).then_inc(S["ea_copied"], 1)
                if stored is not None:
                    act.wait_ge(y_st[s], stored)
                act.wait_ge(S["y_ps"], n + 2)
                A(ey[s][:, :], mm[s][1][:, :], ACT.Copy).then_inc(S["y_copied"], 1)

            for s in range(2):
                item(s, s, None, 0)
            with act.Fori(1, pairs) as i:
                for s in range(2):
                    item(s, 2 * i + s, 32 * i, i)
            for t in range(TT):
                act.wait_ge(S["fs_ready"], t + 1)
                A(junk[:, :], x_tok[:, t, :], ACT.Square, accum_out=sum_sq[:, t:t + 1]).then_inc(S["ss_ready"], 1)
                act.wait_ge(S["ss_ready"], t + 1)
                A(rstd[:, t:t + 1], sum_sq[:, t:t + 1], ACT.Sqrt, scale=1.0 / D, bias=eps_rms).then_inc(S["fs_root"], 1)

        @block.gpsimd
        def _(pool):
            TTo = nc.gpsimd.tensor_tensor
            nc.gpsimd.memset(zeros[:, :], 0.0).then_inc(S["zero_set"], 1)

            def split(p, s):
                pool.wait_ge(S["w_hi_ready"], p + 1)
                TTo(w_lo[s][:, :, :, :], w_raw[s][:, :, :, :], w_hi[s][:, :, :, :].bitcast(F32),
                    ALU.subtract).then_inc(S["w_lo_ready"], 1)

            pool.wait_ge(S["w_hi_ready"], 1)
            for half, done in ((0, S["w_half_ready"]), (1, S["w_lo_ready"])):
                k = slice(half * K // 2, (half + 1) * K // 2)
                TTo(w_lo[0][:, :, k, :], w_raw[0][:, :, k, :], w_hi[0][:, :, k, :].bitcast(F32), ALU.subtract)\
                    .then_inc(done, 1)
            split(1, 1)

            with pool.Fori(0, 4) as i:
                for s in range(2):
                    split(2 * i + (PB + 2 + s), s)
            nc.gpsimd.memset(v_sum[:, :], 0.0).then_inc(S["vsum_done"], 1)
            nc.gpsimd.memset(z_sum[:, :], 0.0).then_inc(S["zsum_done"], 1)
            with pool.Fori(0, 4) as i:
                for s in range(2):
                    q = 2 * i + s
                    pool.wait_ge(S["c_free"], q + 1 + CREDIT)
                    pool.wait_ge(S["vsum_done"], q + 1)
                    TTo(v_sum[:, :], v_sum[:, :], v[:, q, :], ALU.add).then_inc(S["vsum_done"], 1)
                    split(2 * i + (PC + 2 + s), s)
                pool.wait_ge(S["zb_conv"], i + 1)
                pool.wait_ge(S["zsum_done"], i + 1)
                TTo(z_sum[:, :], z_sum[:, :], zb[:, ds(i, 1), :], ALU.add).then_inc(S["zsum_done"], 1)
            with pool.Fori(0, 4) as i:
                for s in range(2):
                    split(2 * i + (PA1 + 2 + s), s)
                pool.wait_ge(S["zb_conv"], i + 5)
                pool.wait_ge(S["zsum_done"], i + 5)
                TTo(z_sum[:, :], z_sum[:, :], zb[:, ds(i + 4, 1), :], ALU.add).then_inc(S["zsum_done"], 1)
            pool.wait_ge(S["zsum_done"], K + 1)

            def squares(acc, q, ring, ready, added):
                for j in range(2):
                    pool.wait_ge(ready, 2 * q + (j + 1))
                    pool.wait_ge(added, 2 * q + (j + 1))
                    TTo(acc[:, :], acc[:, :], ring[j][:, :], ALU.add).then_inc(added, 1)

            pool.wait_ge(S["zb_conv"], K)
            nc.gpsimd.memset(sqv_sum[:, :], 0.0).then_inc(S["v_sq_added"], 1)
            with pool.Fori(0, 2) as i:
                for s in range(2):
                    squares(sqv_sum, 2 * i + s, sqv, S["v_sq"], S["v_sq_added"])
                    split(2 * i + (PA2 + 2 + s), s)
            pool.wait_ge(S["za_lo_ready"], K)
            nc.gpsimd.memset(sqz_sum[:, :], 0.0).then_inc(S["z_sq_added"], 1)
            pool.dma_start(ws_sb[:, :, :], wsT).then_inc(S["ws_ld"], 16)
            pool.dma_start(bs_sb[:, :, :].rearrange("p a b -> p (a b)"), bs.partition_broadcast(P)).then_inc(S["ws_ld"], 16)
            with pool.Fori(0, 2) as i:
                for s in range(2):
                    squares(sqz_sum, 2 * i + s, sqz, S["z_sq"], S["z_sq_added"])
                    split(2 * i + (PGA + 2 + s), s)
            with pool.Fori(2, 4) as i:
                for s in range(2):
                    split(2 * i + (PGA + 2 + s), s)
            pool.wait_ge(S["sp_free"], K)
            pool.wait_ge(S["z_root"], 1)
            pool.dma_start(x1T[:, :, :], xT).then_inc(S["tok_ld"], 16)
            with pool.Fori(0, 4) as i:
                for s in range(2):
                    split(2 * i + (PGC + 2 + s), s)
            pool.wait_ge(S["zb_ready"], K)
            pool.dma_start(wr_sb[:, :, :], wr).then_inc(S["wr_ld"], 16)
            pool.dma_start(gffn_sb[:, :], gffn.partition_broadcast(P)).then_inc(S["g_ld"], 16)
            pool.dma_start(rb_sb, rbias.partition_broadcast(P)).then_inc(S["g_ld"], 16)
            pool.wait_ge(S["wr_ld"], 16)
            TTo(wr_sb[:, :, :], wr_sb[:, :, :], par[:, :, V_GF:V_GF + 1].to_broadcast([P, K, P // 2]), ALU.mult)\
                .then_inc(S["wr_scaled"], 1)
            with pool.Fori(4, (PEND - PGC) // 2 - 1) as i:
                for s in range(2):
                    split(2 * i + (PGC + 2 + s), s)
            pool.wait_ge(S["g_ld"], 32)
            for t in range(TT):
                pool.wait_ge(S["scaled"], t + 1)
                TTo(h2[:, t, :], h2[:, t, :], gffn_sb[:, :], ALU.mult).then_inc(S["h2_ready"], 1)
            pool.wait_ge(S["h2_ready"], TT)
            pool.wait_ge(S["fill_done"], 16 * 2 * FILLS)
            pool.wait_ge(S["pos_ready"], 1)
            for k in range(2):
                for t in range(TT):
                    nc.gpsimd.indirect_dma_start(
                        hs[:, :], bass.IndirectOffsetOnAxis(ap=pos[:, k, t:t + 1], axis=0), h2[:, t, :], None,
                        bounds_check=ITEMS_HS * SLOTS - 1).then_inc(S["scattered"], 16)
            pool.wait_ge(S["scattered"], 16 * 2 * TT)
            pool.dma_start(xg[:, :], hs[0:2 * SLOTS, :]).then_inc(S["xg_ld"], 16)
            pool.wait_ge(S["tab_ready"], 1)
            pairs = pool.value_load(tab[0:1, T_N:T_N + 1], min_val=PAIRS_MIN, max_val=ITEMS // 2)
            pool.dma_start(gfin_sb[:, :], gfin.partition_broadcast(P)).then_inc(S["fin_ld"], 16)
            with pool.Fori(0, pairs) as i:
                pool.wait_ge(S["x_done"], i + 1)
                pool.dma_start(xg[:, :], hs[ds((i + 1) * (2 * SLOTS), 2 * SLOTS), :]).then_inc(S["xg_ld"], 16)
                for s in range(2):
                    n = 2 * i + s
                    pool.wait_ge(S["y_copied"], n + 1)
                    for j in range(2):
                        pool.dma_start(ys[ds(n * SLOTS, SLOTS), j * FF:(j + 1) * FF],
                                       ey[s][j * SLOTS:(j + 1) * SLOTS, :]).then_inc(y_st[s], 16)
            stored = pool.snap(pairs * 32)
            loaded = pool.snap(pairs * 16 + 16)
            for s in range(2):
                pool.wait_ge(y_st[s], stored)
            pool.wait_ge(S["xg_ld"], loaded)
            for b in range(RING):
                turns = (E - b + RING - 1) // RING
                pool.wait_ge(w13_ld[b], 16 * turns)
                pool.wait_ge(w2_ld[b], 16 * turns)
            pool.sem_inc(S["all_stored"], 1)
            pool.wait_ge(S["all_stored"], 1)
            for t in range(TT):
                for k in range(2):
                    nc.gpsimd.indirect_dma_start(
                        got[k][t][:, :], None, ys[:, :], bass.IndirectOffsetOnAxis(ap=pos[:, k, t:t + 1], axis=0),
                        bounds_check=ITEMS_HS * SLOTS - 1).then_inc(gathered[t], 16)

        @block.vector
        def _(dve):
            V = nc.vector
            STT, TTo, TS = V.scalar_tensor_tensor, V.tensor_tensor, V.tensor_scalar

            for edge in (zb_pad[:, :, 0:PAD_B], zb_pad[:, :, PAD_B + T:]):
                V.memset(edge, 0.0).then_inc(S["edge_set"], 1)
            V.memset(eps_rms, RMS_EPS).then_inc(S["eps_set"], 1)
            V.memset(eps_ln, LN_EPS).then_inc(S["eps_set"], 1)
            for c in range(K // 2):
                dve.wait_ge(S["xsq_ready"], c + 1)
                TTo(xsq[:, 2 * c, :], xsq[:, 2 * c, :], xsq[:, 2 * c + 1, :], ALU.add).then_inc(S["xsq_sum"], 1)
            dve.wait_ge(S["rms_root"], 1)
            V.reciprocal(tmp[0][:, :], tmp[0][:, :]).then_inc(S["h_step"], 1)
            dve.wait_ge(S["h_step"], 1)
            dve.wait_ge(S["par_ld"], 16)
            for k in range(K + 1):
                if k < K:
                    STT(xt[:, k, :], xt[:, k, :], par[:, k, V_GM:V_GM + 1], tmp[0][:, :], ALU.mult, ALU.mult)\
                        .then_inc(S["h_ready"], 1)
                if k:
                    dve.wait_ge(S["h_hi_ready"], k)
                    TTo(h_lo[:, k - 1, :], xt[:, k - 1, :], h_hi[:, k - 1, :].bitcast(F32), ALU.subtract)\
                        .then_inc(S["h_lo_ready"], 1)
            dve.wait_ge(S["h_lo_ready"], K)
            for edge in (ca_pad[:, :, 0:PAD_A], ca_pad[:, :, PAD_A + T:]):
                V.memset(edge, 0.0).then_inc(S["edge_set"], 1)
            dve.wait_ge(S["edge_set"], 4)

            def taps_b(m, j0, j1):
                for j in range(j0, j1):
                    acc = zb[:, ds(m, 1), :] if j % 2 == 0 else tmp[0][:, :]
                    z = zb_pad[:, ds(m, 1), j:j + T]
                    w = par[:, ds(m, 1), V_CB + j:V_CB + j + 1]
                    if j < 2:
                        TS(acc, z, w, None, ALU.mult).then_inc(S["tap"], 1)
                    else:
                        dve.wait_ge(S["tap"], m * (TAPS_B + 1) + (j - 1))
                        STT(acc, z, w, acc, ALU.mult, ALU.add).then_inc(S["tap"], 1)
                if j1 == TAPS_B:
                    dve.wait_ge(S["tap"], m * (TAPS_B + 1) + TAPS_B)
                    TTo(zb[:, ds(m, 1), :], zb[:, ds(m, 1), :], tmp[0][:, :], ALU.add).then_inc(S["zb_conv"], 1)
                    dve.wait_ge(S["zb_conv"], m + 1)
                    dve.sem_inc(S["tap"], 1)

            def conv_part(m, s):
                half = (TAPS_B + 1) // 2
                taps_b(m, *((0, half) if s == 0 else (half, TAPS_B)))

            def value_gated(q, s):
                dve.wait_ge(S["sig_ready"], q + 1)
                TTo(zb_pad[:, ds(q, 1), PAD_B:PAD_B + T], mm[s][0][:, :], sig[s][:, :], ALU.mult)\
                    .then_inc(S["b_free"], 1)

            def a_product(q, s):
                dve.wait_ge(S["ca_ready"], q + 1)
                dve.wait_ge(S["mm_done"], 2 * q + (2 * (PA1 + 1)))
                TTo(ca_pad[:, ds(q, 1), PAD_A:PAD_A + T], mm[s][1][:, :], sig[s][:, :], ALU.mult)\
                    .then_inc(S["a1_free"], 1)

            for s in range(2):
                value_gated(s, s)
            with dve.Fori(1, 4) as i:
                for s in range(2):
                    value_gated(2 * i + s, s)
                    dve.wait_ge(S["b_free"], i + (1 + CREDIT))
                    conv_part(i - 1, s)
            dve.wait_ge(S["b_free"], 8 + CREDIT)
            with dve.Fori(3, 7) as i:
                for s in range(2):
                    conv_part(i, s)
            for s in range(2):
                a_product(s, s)
                conv_part(K - 1, s)
            with dve.Fori(1, 4) as i:
                for s in range(2):
                    a_product(2 * i + s, s)
            def centre(a, m, done):
                STT(a[:, ds(m, 1), :], st[0][:, :], -1.0 / D, a[:, ds(m, 1), :], ALU.mult, ALU.add).then_inc(done, 1)

            dve.wait_ge(S["stat"], 2)
            dve.wait_ge(S["a1_free"], 8 + CREDIT)
            dve.wait_ge(S["fill_done"], 16 * 2 * FILLS)
            with dve.Fori(0, 2) as i:
                for s in range(2):
                    p, q = 2 * i + (PA2 + s), 2 * i + s
                    for j in range(2):
                        centre(v, 2 * q + j, S["v_centred"])
                    for j in range(2):
                        m = 2 * q + j
                        for tap in range(TAPS_A):
                            c = ca_pad[:, ds(m, 1), tap:tap + T]
                            w = par[:, ds(m, 1), V_CA + tap:V_CA + tap + 1]
                            if tap == 0:
                                TS(sig[j][:, :], c, w, None, ALU.mult).then_inc(S["za_step"], 1)
                            else:
                                STT(sig[j][:, :], c, w, sig[j][:, :], ALU.mult, ALU.add).then_inc(S["za_step"], 1)
                            dve.wait_ge(S["za_step"], m * TAPS_A + (tap + 1))
                        dve.wait_ge(S["mm_done"], 2 * p + j + 1)
                        TTo(tmp[j][:, :], mm[s][j][:, :], sig[j][:, :], ALU.mult).then_inc(S["za_ready"], 1)
                    dve.wait_ge(S["za_ready"], 2 * q + 2)
                    dve.sem_inc(S["a2_free"], 1)
                    for j in range(2):
                        m = 2 * q + j
                        dve.wait_ge(S["za_hi_ready"], m + 1)
                        TTo(za_lo[:, ds(m, 1), :], tmp[j][:, :], za_hi[:, ds(m, 1), :].bitcast(F32), ALU.subtract)\
                            .then_inc(S["za_lo_ready"], 1)
            dve.wait_ge(S["v_root"], 1)
            V.reciprocal(v_rstd, v_rstd).then_inc(S["v_step"], 1)
            dve.wait_ge(S["v_step"], 1)
            dve.wait_ge(S["v_centred"], K)

            def first_gated(q, s):
                dve.wait_ge(S["sig_ready"], q + 9)
                dve.wait_ge(S["mm_done"], 2 * q + (2 * (PGA + 1)))
                TTo(merged[:, ds(q, 1), :], mm[s][1][:, :], sig[s][:, :], ALU.mult).then_inc(S["ga_free"], 1)

            dve.wait_ge(S["stat"], 4)
            with dve.Fori(0, 2) as i:
                for s in range(2):
                    q = 2 * i + s
                    for m in (2 * q, 2 * q + 1):
                        TTo(v[:, ds(m, 1), :], v[:, ds(m, 1), :], v_rstd, ALU.mult).then_inc(S["v_step"], 1)
                        centre(zb, m, S["z_centred"])
                    for m in (2 * q, 2 * q + 1):
                        dve.wait_ge(S["v_step"], m + 2)
                        TS(v[:, ds(m, 1), :], v[:, ds(m, 1), :], par[:, ds(m, 1), V_CG:V_CG + 1],
                           par[:, ds(m, 1), V_CBI:V_CBI + 1], ALU.mult, ALU.add).then_inc(S["v_ready"], 1)
                    first_gated(q, s)
            dve.wait_ge(S["ws_ld"], 32)
            for m in range(K):
                dve.wait_ge(S["sp_ps"], m + 1)
                t = tmp[m % 2]
                TTo(t[:, :].rearrange("p (n q) -> p n q", n=TT), tr[m % 2][:, :, :],
                    bs_sb[:, m, :].unsqueeze(1).to_broadcast([P, TT, P]), ALU.add).then_inc(S["sp_free"], 1)
                dve.wait_ge(S["sp_free"], m + 1)
                TTo(u[:, m, :], u[:, m, :], t[:, :], ALU.mult).then_inc(S["zc_ready"], 1)
            for m in range(K):
                dve.wait_ge(S["zc_hi_ready"], m + 1)
                TTo(zc_lo[:, m, :], u[:, m, :], zc_hi[:, m, :].bitcast(F32), ALU.subtract).then_inc(S["zc_lo_ready"], 1)
            with dve.Fori(2, 4) as i:
                for s in range(2):
                    first_gated(2 * i + s, s)
            dve.wait_ge(S["ga_free"], 8 + CREDIT)
            dve.wait_ge(S["z_root"], 1)
            V.reciprocal(z_rstd, z_rstd).then_inc(S["z_inv"], 1)
            dve.wait_ge(S["z_inv"], 1)

            def add_gated(p, q, s, first_sig, step, free):
                dve.wait_ge(S["sig_ready"], q + first_sig)
                dve.wait_ge(S["mm_done"], 2 * p + 2)
                TTo(sig[s][:, :], mm[s][1][:, :], sig[s][:, :], ALU.mult).then_inc(S["m_step"], 1)
                dve.wait_ge(S["m_step"], q + step)
                TTo(merged[:, ds(q, 1), :], merged[:, ds(q, 1), :], sig[s][:, :], ALU.add).then_inc(free, 1)

            with dve.Fori(0, 4) as i:
                for s in range(2):
                    p, q = 2 * i + (PGC + s), 2 * i + s
                    z = zb[:, ds(q, 1), :]
                    TTo(z, z, z_rstd, ALU.mult).then_inc(S["zs_norm"], 1)
                    dve.wait_ge(S["zs_sig"], q + 1)
                    TS(z, z, par[:, ds(q, 1), V_BG:V_BG + 1], par[:, ds(q, 1), V_BB:V_BB + 1], ALU.mult, ALU.add)\
                        .then_inc(S["zs_step"], 1)
                    dve.wait_ge(S["zs_step"], q + 1)
                    TTo(z, z, tmp[s][:, :], ALU.mult).then_inc(S["zb_ready"], 1)
                    add_gated(p, q, s, 17, 1, S["gc_free"])
                    dve.wait_ge(S["zb_hi_ready"], q + 1)
                    TTo(zb_lo[:, ds(q, 1), :], z, zb_hi[:, ds(q, 1), :].bitcast(F32), ALU.subtract)\
                        .then_inc(S["zb_lo_ready"], 1)
            dve.wait_ge(S["gc_free"], 8 + CREDIT)
            with dve.Fori(0, 4) as i:
                for s in range(2):
                    p, q = 2 * i + (PGB + s), 2 * i + s
                    add_gated(p, q, s, 25, 9, S["gb_free"])
                    dve.wait_ge(S["m_hi_ready"], q + 1)
                    TTo(m_lo[:, ds(q, 1), :], merged[:, ds(q, 1), :], m_hi[:, ds(q, 1), :].bitcast(F32), ALU.subtract)\
                        .then_inc(S["m_lo_ready"], 1)
            dve.wait_ge(S["tok_ld"], 16)
            for q in range(4):
                for j in range(2):
                    m = 2 * q + j
                    dve.wait_ge(S["mm_done"], 2 * PW + m + 1)
                    TTo(x1T[:, m, :], mm[q % 2][j][:, :], x1T[:, m, :], ALU.add).then_inc(S["x1T_ready"], 1)
                if q:
                    for m in (2 * q - 2, 2 * q - 1):
                        dve.wait_ge(S["o_tr"], m + 1)
                        V.tensor_copy(x_tok[:, :, m * P:(m + 1) * P], tr[m % 2][:, :, :]).then_inc(S["x1_ready"], 1)

            steps = [0]

            def step(ins):
                steps[0] += 1
                ins.then_inc(S["r_step"], 1)
                dve.wait_ge(S["r_step"], steps[0])

            def over(ap, shape, axis):
                return ap.unsqueeze(axis).to_broadcast(shape)

            def first_max(values, top, hot, where, width):
                shape = [P, TT, width]
                index = over(cst[:, C_I32:C_I32 + width], shape, 1)
                step(V.tensor_reduce(top[:, :], values, AX.X, ALU.max))
                step(TTo(hot[:, :, :], values, over(top[:, :], shape, 2), ALU.is_equal))
                step(STT(hot[:, :, :], hot[:, :, :], -100.0, index, ALU.mult, ALU.add))
                step(V.tensor_reduce(where[:, :], hot[:, :, :], AX.X, ALU.min))
                step(STT(hot[:, :, :], index, -100.0, over(where[:, :], shape, 2), ALU.add, ALU.is_equal))

            dve.wait_ge(S["o_tr"], K)
            for zero in (earlier[:, 0, :], blocks[:, 0:E // 2], scan[0][:, 0:E // 2], scan[1][:, 0:E // 2]):
                V.memset(zero, 0.0).then_inc(S["preset"], 1)
            dve.wait_ge(S["preset"], 4)
            dve.wait_ge(S["lg_ps"], 1)
            dve.wait_ge(S["rs_root"], 1)
            V.reciprocal(rstd, rstd).then_inc(S["rs_ready"], 1)
            dve.wait_ge(S["rs_ready"], 1)
            step(TTo(lg[:, :, :], st[1][:, :].rearrange("p (t r) -> p t r", t=TT)[:, :, 0:G + E],
                     over(rstd, [P, TT, G + E], 2), ALU.mult))
            dve.wait_ge(S["g_ld"], 32)
            step(TTo(lg[:, :, :], lg[:, :, :], over(rb_sb, [P, TT, G + E], 1), ALU.add))
            first_max(lg[:, :, 0:G], gmax, ghot, gidx, G)
            step(TTo(gexp[:, :, :], lg[:, :, 0:G], over(gmax[:, :], [P, TT, G], 2), ALU.subtract))
            dve.sem_inc(S["r_exp"], 1)
            step(TS(ghot[:, :, :], ghot[:, :, :], BIG, -BIG, ALU.mult, ALU.add))
            by_group = [P, TT, G, EPG]
            step(TTo(elog[0][:, :, :].rearrange("p t (g e) -> p t g e", g=G),
                     lg[:, :, G:].rearrange("p t (g e) -> p t g e", g=G), over(ghot[:, :, :], by_group, 3), ALU.add))
            first_max(elog[0][:, :, :], emax[0], ehot[0], eidx[0], E)
            step(STT(elog[1][:, :, :], ehot[0][:, :, :], -4 * BIG, elog[0][:, :, :], ALU.mult, ALU.add))
            first_max(elog[1][:, :, :], emax[1], ehot[1], eidx[1], E)
            step(TTo(both[:, :, :], ehot[0][:, :, :], ehot[1][:, :, :], ALU.add))
            for t in range(TT):
                step(TTo(earlier[:, t + 1, :], earlier[:, t, :], both[:, t, :], ALU.add))
            dve.sem_inc(S["hot_ready"], 1)
            step(TTo(wgt[1][:, :], emax[1][:, :], emax[0][:, :], ALU.subtract))
            dve.sem_inc(S["r_exp"], 1)
            dve.wait_ge(S["r_expd"], 2)
            step(V.tensor_reduce(gden[:, :], gexp[:, :, :], AX.X, ALU.add))
            step(STT(wgt[0][:, :], wgt[1][:, :], 1.0, gden[:, :], ALU.add, ALU.mult))
            step(V.reciprocal(wgt[0][:, :], wgt[0][:, :]))
            step(TTo(wgt[1][:, :], wgt[1][:, :], wgt[0][:, :], ALU.mult))
            dve.wait_ge(S["cum_ps"], 1)
            count = st[0][:, TT * E:(TT + 1) * E]
            cmp = scr[:, 0:E * 8].rearrange("p (e b) -> p e b", e=E)
            step(TTo(cmp, over(count, [P, E, 8], 2), over(cst[:, C_THR:C_THR + 8], [P, E, 8], 1), ALU.is_gt))
            step(V.tensor_reduce(blocks[:, E // 2:], cmp, AX.X, ALU.add))
            sums, n = blocks, 0
            for shift in (1, 2, 4, 8, 16):
                step(TTo(scan[n % 2][:, E // 2:], sums[:, E // 2:], sums[:, E // 2 - shift:E // 2 + E - shift], ALU.add))
                sums, n = scan[n % 2], n + 1
            iend, istart = sums[:, E // 2:], sums[:, E // 2 - 1:E // 2 + E - 1]
            step(STT(slot[:, :, :], over(istart, [P, TT, E], 1), float(SLOTS),
                     st[0][:, 0:TT * E].rearrange("p (t e) -> p t e", t=TT), ALU.mult, ALU.add))
            step(TTo(ehots[:, :, :, :], ehots[:, :, :, :], over(slot[:, :, :], [P, 2, TT, E], 1), ALU.mult))
            step(V.tensor_reduce(posf[:, :, :], ehots[:, :, :, :], AX.X, ALU.add))
            V.tensor_copy(pos[:, :, :], posf[:, :, :]).then_inc(S["pos_ready"], 1)
            owner = scr[:, :].rearrange("p (i e) -> p i e", e=E)
            step(TTo(owner, over(iend, [P, 48, E], 1), over(cst[:, C_I48:C_I48 + 48], [P, 48, E], 2), ALU.is_le))
            step(V.tensor_reduce(itemf[:, :], owner, AX.X, ALU.add))
            step(TS(itemf[:, :], itemf[:, :], float(E - 1), None, ALU.min))
            thirds = scr[:, 0:48 * TURNS].rearrange("p (i j) -> p i j", j=TURNS)
            step(TTo(thirds, over(itemf[:, :], [P, 48, TURNS], 2),
                     over(cst[:, C_TURN:C_TURN + TURNS], [P, 48, TURNS], 1), ALU.is_ge))
            step(V.tensor_reduce(turnf[:, :], thirds, AX.X, ALU.add))
            step(STT(buff[:, :], turnf[:, :], -float(RING), itemf[:, :], ALU.mult, ALU.add))
            evens = scr[:, 0:24]
            step(TTo(evens, iend[:, E - 1:E].to_broadcast([P, 24]), cst[:, C_EVEN:C_EVEN + 24], ALU.is_gt))
            step(V.tensor_reduce(tabf[:, 0:1], evens, AX.X, ALU.add))
            step(TS(tab[:, T_END:T_END + E], iend, 1.0, None, ALU.add))
            step(V.tensor_copy(tab[:, T_N:T_N + 1], tabf[:, 0:1]))
            step(TS(tab[:, T_TURN:T_TURN + 48], turnf[:, :], 16.0, None, ALU.mult))
            step(TS(tab[:, T_BUF:T_BUF + 48], buff[:, :], float(RING), None, ALU.add))
            dve.sem_inc(S["tab_ready"], 1)

            pairs = dve.value_load(tab[0:1, T_N:T_N + 1], min_val=PAIRS_MIN, max_val=ITEMS // 2)
            with dve.Fori(0, pairs) as i:
                for s in range(2):
                    n = 2 * i + s
                    dve.wait_ge(S["esig_ready"], n + 1)
                    TTo(eup[s][:, :], mm[s][0][:, 0:FF // 2], esig[s][:, :], ALU.mult).then_inc(S["eup_ready"], 1)
                    dve.wait_ge(S["eup_ready"], n + 1)
                    TTo(eact[s][:, :], mm[s][0][:, FF // 2:], eup[s][:, :], ALU.mult).then_inc(S["eact_ready"], 1)
            dve.wait_ge(S["fin_ld"], 16)
            for t in range(TT + 1):
                if t < TT:
                    dve.wait_ge(gathered[t], 32)
                    for k in range(2):
                        STT(x_tok[:, t, :], got[k][t][:, :], wgt[k][:, t:t + 1], x_tok[:, t, :], ALU.mult, ALU.add)\
                            .then_inc(S["fs_ready"] if k else S["fs_step"], 1)
                        if k == 0:
                            dve.wait_ge(S["fs_step"], t + 1)
                if t:
                    dve.wait_ge(S["fs_root"], t)
                    V.reciprocal(rstd[:, t - 1:t], rstd[:, t - 1:t]).then_inc(S["fs_inv"], 1)
                    dve.wait_ge(S["fs_inv"], t)
                    STT(x_tok[:, t - 1, :], x_tok[:, t - 1, :], rstd[:, t - 1:t], gfin_sb[:, :], ALU.mult, ALU.mult)\
                        .then_inc(S["fin_ready"], 1)


def kernel(x, norm_mix, w_in, conv_a, w_a_out, conv_b, ln_b_g, ln_b_b, w_b_out, ln_c_g, ln_c_b, w_s, b_s,
           w_c_out, w_o, norm_ffn, w_group, b_group, w_router, b_router, w1, w3, w2, norm_final):
    import numpy as np
    import concourse.bacc as bacc
    from concourse.bass_utils import run_bass_kernel_spmd

    def tiles(w):
        return w.reshape(K, P, -1, P).transpose(2, 1, 0, 3)

    def features(a):
        return a.reshape(-1, K, P).transpose(2, 1, 0)

    w_in = np.asarray(w_in)[0]
    cuts = np.cumsum([D] * 9)
    xa, ba, ca, val, gate, uc, vc, ga, gb, gc = [tiles(a) for a in np.split(w_in, cuts, axis=1)]
    wa, wb, wc, wo = [tiles(np.asarray(a)[0]) for a in (w_a_out, w_b_out, w_c_out, w_o)]

    def two(a, b):
        return np.stack([a, b], axis=2)

    def own(a):
        return two(a[0::2], a[1::2])

    stream = np.concatenate([two(val, gate), two(uc, vc), two(ca, xa), own(ba), two(ga, wa), two(gc, wc),
                             two(gb, wb), own(wo)])
    params = np.concatenate([features(np.asarray(a)) for a in
                             (conv_b[0], conv_a[0], norm_mix, ln_b_g, ln_b_b, ln_c_g, ln_c_b, norm_ffn)],
                            axis=2)
    w13 = np.stack([np.asarray(w1)[0].reshape(E, K, P, 2, FF // 2), np.asarray(w3)[0].reshape(E, K, P, 2, FF // 2)],
                   axis=4).transpose(0, 2, 1, 3, 4, 5).reshape(E, P, K, 2, FF)
    consts = np.zeros((P, C_N), np.float32)
    consts[:, C_ID:C_ID + P] = np.eye(P)
    consts[:, C_ONE:C_ONE + P] = 1
    consts[:, C_UP:C_UP + P] = np.triu(np.ones((P, P)), 1)
    consts[:, C_THR:C_THR + 8] = SLOTS * np.arange(8)
    consts[:, C_I32:C_I32 + E] = np.arange(E)
    consts[:, C_I48:C_I48 + 48] = np.arange(48)
    consts[:, C_EVEN:C_EVEN + 24] = 2 * np.arange(24)
    consts[:, C_TURN:C_TURN + TURNS] = RING * np.arange(TURNS)
    x2 = np.asarray(x)[0]
    arrays = {
        "xT": x2.T.reshape(K, P, T).transpose(1, 0, 2),
        "stream": stream,
        "params": params,
        "wsT": np.asarray(w_s)[0].transpose(2, 0, 1),
        "bs": np.asarray(b_s)[0].reshape(-1),
        "wr": np.concatenate([np.asarray(w_group)[0], np.asarray(w_router)[0],
                              np.zeros((D, P // 2 - G - E), np.float32)], axis=1)
        .reshape(K, P, P // 2).transpose(1, 0, 2),
        "rbias": np.concatenate([np.asarray(b_group)[0], np.asarray(b_router)[0]]),
        "gffn": np.asarray(norm_ffn)[0],
        "gfin": np.asarray(norm_final),
        "w13": w13,
        "w2": np.asarray(w2)[0].reshape(E, FF // P, P, D).transpose(0, 2, 1, 3),
        "consts": consts,
    }
    nc = bacc.Bacc("TRN2", target_bir_lowering=False, num_devices=1)
    feed, args = {}, []
    for name, a in arrays.items():
        a = np.ascontiguousarray(a, np.float32)
        feed[f"in_{name}"] = a
        args.append(nc.dram_tensor(f"in_{name}", a.shape, F32, kind="ExternalInput").ap())
    args.append(nc.dram_tensor("out_dram", (T, D), F32, kind="ExternalOutput").ap())
    build(nc, *args)
    r = run_bass_kernel_spmd(nc, [feed], core_ids=[0])
    return np.asarray(r.results[0]["out_dram"]).reshape(1, T, D)
```

```python
from contextlib import ExitStack

import concourse.bass as bass
from concourse import mybir

F32 = mybir.dt.float32
F32R = mybir.dt.float32r
I32 = mybir.dt.int32
U32 = mybir.dt.uint32
ALU = mybir.AluOpType
ACT = mybir.ActivationFunctionType
AX = mybir.AxisListType

P = 128
D = 1024
T = 512
K = D // P
TT = T // P
TAPS_A, TAPS_B = 3, 31
PAD_A, PAD_B = TAPS_A // 2, TAPS_B // 2
G, EPG = 4, 8
E = G * EPG
FF = 512
SLOTS = 64
ITEMS = 2 * T // SLOTS + E
PAIRS_MIN = T // SLOTS
RUN = ITEMS + 4
RING = 3
TURNS = (E + RING - 1) // RING
assert TURNS <= 12
RMS_EPS, LN_EPS = 1e-6, 1e-5
BIG = 1e30
GATE_AFTER = 3
SUMS_AFTER = 3
CREDIT = 2

PB, PC, PA1, PA2, PGA, PGC, PGB, PW, PEND = 0, 8, 16, 24, 28, 36, 44, 52, 56

C_ID, C_ONE, C_UP, C_THR, C_I32, C_ITEM, C_EVEN = 0, 128, 256, 384, 392, 424, 476
C_TURN, C_Q, C_TOK, C_SLOT = 500, 512, 576, 584
C_N = 636

V_CB, V_CA, V_GM, V_BG, V_BB, V_CG, V_CBI, V_GF = 0, 31, 34, 35, 36, 37, 38, 39
V_N = 40


def build(nc, xT, stream, params, wsT, bs, wr, rbias, gfin, w13, w2, consts, out):
    with ExitStack() as ctx:
        def sem(name):
            return ctx.enter_context(nc.semaphore(name))

        KB = 1024
        base = (nc.sbuf_base + 63) // 64 * 64

        def at(name, shape, dt, offset):
            return nc.alloc_sbuf_tensor_at(name, shape, dt, offset=base + offset)

        R0, R1, R2 = 0, 48 * KB, 80 * KB
        R3 = R2 + K * (T + 2 * PAD_B) * 4
        R4 = R3 + 16 * KB
        R5 = R4 + 16 * KB
        R6 = R5 + 16 * KB
        R7 = R6 + K * (T + 2 * PAD_A) * 4
        R8 = R7 + 32 * KB
        R9 = R8 + 3840
        w_raw = [at(f"w_raw{s}", [P, 2, K, P], F32, R0 + 8 * KB * s) for s in range(2)]
        w_hi = [at(f"w_hi{s}", [P, 2, K, P], F32R, R0 + 16 * KB + 8 * KB * s) for s in range(2)]
        w_lo = [at(f"w_lo{s}", [P, 2, K, P], F32R, R0 + 32 * KB + 8 * KB * s) for s in range(2)]
        h_hi = at("h_hi", [P, K, T], F32R, R1)
        h_lo = at("h_lo", [P, K, T], F32R, R1 + 16 * KB)
        zb_pad = at("zb_pad", [P, K, T + 2 * PAD_B], F32, R2)
        zb = at("zb", [P, K, T], F32, R3)
        zb_lo = at("zb_lo", [P, K, T], F32R, R3)
        u = at("u", [P, K, T], F32, R4)
        zc_lo = at("zc_lo", [P, K, T], F32R, R4)
        v = at("v", [P, K, T], F32, R5)
        hp_hi = at("hp_hi", [P, K, T], F32R, R4)
        hp_lo = at("hp_lo", [P, K, T], F32R, R5)
        zc_hi = at("zc_hi", [P, K, T], F32R, R5)
        xt = at("xt", [P, K, T], F32, R6)
        ca_pad = at("ca_pad", [P, K, T + 2 * PAD_A], F32, R6)
        ws_sb = at("ws_sb", [P, K, P], F32, R6)
        bs_sb = at("bs_sb", [P, K, P], F32, R6 + 4 * KB)
        sqz = [at(f"sqz{s}", [P, T], F32, R6 + 8 * KB + 2 * KB * s) for s in range(2)]
        sqz_sum = at("sqz_sum", [P, T], F32, R6 + 12 * KB)
        x1T = at("x1T", [P, K, T], F32, R6)
        x_tok = at("x_tok", [P, TT, D], F32, R2)
        za_hi = at("za_hi", [P, K, T], F32R, R7)
        za_lo = at("za_lo", [P, K, T], F32R, R7 + 16 * KB)
        zb_hi = at("zb_hi", [P, K, T], F32R, R7)
        xsq = at("xsq", [P, K, T], F32, R7)
        v_sum = at("v_sum", [P, T], F32, R7 + 20 * KB)
        merged = at("merged", [P, K, T], F32, R2)
        sqv = [at(f"sqv{s}", [P, T], F32, R2 + 2 * KB * s) for s in range(2)]
        sqv_sum = at("sqv_sum", [P, T], F32, R2 + 4 * KB)
        m_hi = at("m_hi", [P, K, T], F32R, R4)
        m_lo = at("m_lo", [P, K, T], F32R, R5)
        cst = at("cst", [P, C_N], F32, R8)
        par = at("par", [P, K, V_N], F32, R8 + 2560)
        sig = [at(f"sig{s}", [P, T], F32, R9 + 2 * KB * s) for s in range(2)]
        tmp = [at(f"tmp{s}", [P, T], F32, R9 + 4 * KB + 2 * KB * s) for s in range(2)]
        z_sum = at("z_sum", [P, T], F32, R9 + 8 * KB)
        assert K * V_N * 4 <= 1280 and C_N * 4 <= 2560
        sq1 = sig
        lgT = sig[0]
        wr_sb = at("wr_sb", [P, K, P // 2], F32, R9 + 4 * KB)
        xg = at("xg", [2 * SLOTS, D], F32, R9 + 6 * KB)
        small = at("small", [P, 64], F32, R9 + 10 * KB)
        assert base + R9 + 10 * KB + 256 <= nc.sbuf_usable_end
        rb_sb = small[:, 16:16 + G + E]
        ident, ones, upper = cst[:, C_ID:C_ID + P], cst[:, C_ONE:C_ONE + P], cst[:, C_UP:C_UP + P]
        eps_rms, eps_ln = small[:, 0:1], small[:, 1:2]
        v_rstd, z_rstd = tmp[0][:, :], z_sum[:, :]
        sum_sq, rstd = small[:, 4:8], small[:, 8:12]

        ew13 = [at(f"ew13_{b}", [P, K, 2, FF], F32, r) for b, r in enumerate((R7, R1, R0 + 16 * KB))]
        ew2 = [at(f"ew2_{b}", [P, FF // P, D], F32, r) for b, r in enumerate((R3, R0, R5))]
        h2 = at("h2", [P, TT, D], F32, R4)
        scr = at("scr", [P, ITEMS * E], F32, R6)
        RT = R6 + 6 * KB
        o = [RT]

        def small_tile(name, shape, dt=F32):
            n = 4
            for s in shape[1:]:
                n *= s
            t = at(name, shape, dt, o[0])
            o[0] += (n + 31) // 32 * 32
            assert o[0] <= R7
            return t

        lg = small_tile("lg", [P, TT, G + E])
        gmax = small_tile("gmax", [P, TT])
        gidx = small_tile("gidx", [P, TT])
        ghot = small_tile("ghot", [P, TT, G])
        gexp = small_tile("gexp", [P, TT, G])
        gden = small_tile("gden", [P, TT])
        elog = [small_tile(f"elog{k}", [P, TT, E]) for k in range(2)]
        emax = [small_tile(f"emax{k}", [P, TT]) for k in range(2)]
        eidx = [small_tile(f"eidx{k}", [P, TT]) for k in range(2)]
        wgt = [small_tile(f"wgt{k}", [P, TT]) for k in range(2)]
        ehots = small_tile("ehots", [P, 2, TT, E])
        ehot = [ehots[:, k, :, :] for k in range(2)]
        both = small_tile("both", [P, TT, E])
        earlier = small_tile("earlier", [P, TT + 1, E])
        slot = small_tile("slot", [P, TT, E])
        PADDED = E // 2 + E
        blocks = small_tile("blocks", [P, PADDED])
        scan = [small_tile(f"scan{k}", [P, PADDED]) for k in range(2)]
        posf = small_tile("posf", [P, 2, TT])
        pitem = small_tile("pitem", [P, 2, TT])
        pq = small_tile("pq", [P, 2, TT])
        value = small_tile("value", [P, 2, TT])
        filled = small_tile("filled", [P, RUN])
        past = small_tile("past", [P, RUN])
        row_y = small_tile("row_y", [P, RUN, 2], U32)
        row_x = small_tile("row_x", [P, RUN], U32)
        reach = small_tile("reach", [P, E])
        lessf = small_tile("lessf", [P, RUN])
        less = small_tile("less", [P, RUN], I32)
        item_rows = [small_tile(f"item_rows{s}", [SLOTS, 2], U32) for s in range(2)]
        next_rows = [small_tile(f"next_rows{s}", [SLOTS, 1], U32) for s in range(2)]
        itemf = small_tile("itemf", [P, ITEMS])
        turnf = small_tile("turnf", [P, ITEMS])
        buff = small_tile("buff", [P, ITEMS])
        tabf = small_tile("tabf", [P, 2])
        tab = small_tile("tab", [P, E + 2 + 2 * ITEMS], I32)
        is_q = at("is_q", [P, 2 * TT, SLOTS], F32, R9)
        is_item = at("is_item", [P, 2 * TT, RUN], F32, R9 + 4 * KB)
        T_END, T_N, T_TURN, T_BUF = 0, E, E + 2, E + 2 + ITEMS
        xgT = at("xgT", [P, K, 2 * SLOTS], F32, R4 + 4 * KB)
        ey = [at(f"ey{s}", [P, FF], F32, R4 + 8 * KB + 2 * KB * s) for s in range(2)]
        esig = [at(f"esig{s}", [P, FF // 2], F32, R4 + 12 * KB + 1 * KB * s) for s in range(2)]
        eup = [at(f"eup{s}", [P, FF // 2], F32, R4 + 14 * KB + 1 * KB * s) for s in range(2)]
        eact = [at(f"eact{s}", [P, FF // 2], F32, R9 + 1 * KB * s) for s in range(2)]
        eactT = [at(f"eactT{s}", [P, 2, P], F32, R9 + 2 * KB + 1 * KB * s) for s in range(2)]
        gfin_sb = at("gfin_sb", [P, D], F32, R4)
        got = [[at(f"got{k}{t}", [P, D], F32, R0 + 4 * KB * (k * TT + t)) for t in range(TT)] for k in range(2)]
        junk = at("junk", [P, D], F32, R0 + 32 * KB)

        hs = nc.dram_tensor("hs", [T, D], F32, kind="Internal").ap()
        ys = nc.dram_tensor("ys", [2 * T + RUN * SLOTS, D], F32, kind="Internal").ap()
        ys_halves = ys.rearrange("r (j f) -> (r j) f", j=2)

        def bank(name, shape):
            return ctx.enter_context(nc.psum_tensor(name, shape, F32))

        mm = [[bank(f"mm{s}{j}", [P, T]) for j in range(2)] for s in range(2)]
        st = [bank(f"st{s}", [P, T]) for s in range(2)]
        tr = [bank(f"tr{s}", [P, TT, P]) for s in range(2)]
        mix = [t[:, :, :] for t in tr] + [t[:, :].rearrange("p (n q) -> p n q", n=TT) for t in st]

        names = """
            cst_ld par_ld x_again_ld ws_ld rbias_ld gfin_ld xsq_ready xsq_sum eps_set stat rms_root
            h_step h_ready h_hi_ready h_lo_ready w_hi_ready w_lo_ready mm_done b_free c_free a1_free
            a2_free ga_free gc_free gb_free sig_ready ca_ready tap_done zb_conv vsum_done zsum_done
            v_centred v_sq v_sq_added z_centred z_sq z_sq_added v_root z_root v_step v_ready vt_ps
            vt_ready mix_ps mix_free zc_ready zc_hi_ready zc_lo_ready za_step za_ready za_hi_ready
            za_lo_ready z_affine z_normed z_inv eup_ready final_inv edge_set all_stored z_sig zb_ready
            zb_hi_ready zb_lo_ready gated m_hi_ready m_lo_ready x1_ps x1_ready ss_ready x1_root x1_rstd
            h2_ready logits_ps route_step exp_wanted exp_ready hot_ready ranks_ps tab_ready xg_ld
            m13_half rows_stored xgT_ps xgT_ready m13_done esig_ready eact_ready eactT_ps eactT_ready
            y_ps y_copied x1T_ready x1_sq_ready x1_sq_summed lgT_ready wr_ld wr_scaled preset_done
            both_added final_root first_added fin_ready out_done w_half_ready found_ready rows_ps
            rows_ready x_rows y_rows x_fetch y_store w_hi_half hp_hi_ready hp_lo_ready gate_scaled
            value_scaled""".split()
        S = {n: sem(n) for n in names}
        x_ld = [sem(f"x_ld{c}") for c in range(K // 2)]
        raw_ld = [sem(f"raw_ld{s}") for s in range(2)]
        w13_ld = [sem(f"w13_ld{b}") for b in range(RING)]
        w2_ld = [sem(f"w2_ld{b}") for b in range(RING)]
        gathered = [sem(f"gathered{t}") for t in range(TT)]
        y_st = [sem(f"y_st{s}") for s in range(2)]

        block = ctx.enter_context(nc.Block())
        ds = bass.ds

        @block.sync
        def _(sp):
            def load_x(c):
                sp.dma_start(xt[:, 2 * c:2 * c + 2, :], xT[:, 2 * c:2 * c + 2, :]).then_inc(x_ld[c], 16)

            sp.dma_start(par[:, :, :], params).then_inc(S["par_ld"], 16)
            load_x(0)
            sp.dma_start(w_raw[0][:, :, :, :], stream[0]).then_inc(raw_ld[0], 16)
            load_x(1)
            sp.dma_start(cst[:, :], consts).then_inc(S["cst_ld"], 16)
            for c in range(2, K // 2):
                load_x(c)
            sp.dma_start(w_raw[1][:, :, :, :], stream[1]).then_inc(raw_ld[1], 16)
            with sp.Fori(1, PEND // 2) as i:
                for s in range(2):
                    sp.wait_ge(S["w_lo_ready"], 2 * i + s - 1)
                    sp.dma_start(w_raw[s][:, :, :, :], stream[2 * i + s]).then_inc(raw_ld[s], 16)
            def load13(e, b, half=None):
                for h in range(2) if half is None else (half,):
                    k = slice(h * K // 2, (h + 1) * K // 2)
                    sp.dma_start(ew13[b][:, k, :, :], w13[e, :, k]).then_inc(w13_ld[b], 16)

            def load2(e, b):
                sp.dma_start(ew2[b][:, :, :], w2[e]).then_inc(w2_ld[b], 16)

            sp.wait_ge(S["mm_done"], 2 * PW)
            load13(0, 0)
            load2(0, 0)
            load13(1, 1)
            sp.wait_ge(S["w_lo_ready"], PEND)
            load2(1, 1)
            sp.wait_ge(S["mm_done"], 2 * PEND)
            load13(2, 2)
            for t in range(TT):
                sp.wait_ge(S["h2_ready"], t + 1)
                sp.dma_start(hs[t * P:(t + 1) * P, :], h2[:, t, :]).then_inc(S["rows_stored"], 16)
            load2(2, 2)

            def next_expert(i, b):
                e = RING * i + b
                done = sp.value_load(tab[0:1, ds(T_END + e - RING, 1)], min_val=1, max_val=ITEMS + 1)
                sp.wait_ge(w13_ld[b], 32 * i)
                sp.wait_ge(S["m13_half"], done)
                load13(e, b, 0)
                sp.wait_ge(S["m13_done"], done)
                load13(e, b, 1)
                sp.wait_ge(w2_ld[b], 16 * i)
                sp.wait_ge(S["y_ps"], done)
                load2(e, b)

            sp.wait_ge(S["tab_ready"], 1)
            with sp.Fori(1, E // RING) as i:
                for b in range(RING):
                    next_expert(i, b)
            for b in range(E % RING):
                next_expert(E // RING, b)
            sp.wait_ge(S["all_stored"], 1)
            for t in range(TT):
                for k in range(2):
                    sp.dma_start(got[k][t][:, :], ys[k * T + t * P:k * T + (t + 1) * P, :]).then_inc(gathered[t], 16)
            for t in range(TT):
                sp.wait_ge(S["fin_ready"], t + 1)
                sp.dma_start(out[t * P:(t + 1) * P, :], x_tok[:, t, :]).then_inc(S["out_done"], 16)
            sp.wait_ge(S["out_done"], 16 * TT)

        @block.tensor
        def _(pe):
            def tile(acc, s, j, hi, lo, arriving=None):
                for k in range(K):
                    if arriving is not None:
                        pe.wait_ge(arriving, k + 1)
                    nc.tensor.matmul(acc[:, :], w_hi[s][:, j, k, :], hi[:, k, :], start=(k == 0), stop=False)
                    nc.tensor.matmul(acc[:, :], w_hi[s][:, j, k, :], lo[:, k, :], start=False, stop=False)
                    last = nc.tensor.matmul(acc[:, :], w_lo[s][:, j, k, :], hi[:, k, :], start=False, stop=(k == K - 1))
                last.then_inc(S["mm_done"], 1)

            def pair(p, s, q, free, first, second, ready=None, before=None, arriving=None):
                pe.wait_ge(S["w_hi_ready"], p + 1)
                pe.wait_ge(S["w_lo_ready"], p + 1)
                if before is not None:
                    pe.wait_ge(before[0], before[1] + (CREDIT - 1) + s)
                pe.wait_ge(free, q + 1)
                tile(mm[s][0], s, 0, *first, arriving)
                if ready is not None:
                    pe.wait_ge(ready, K)
                tile(mm[s][1], s, 1, *second)

            def stage(base_pair, q0, pairs, free, first, second, ready=None, before=None):
                with pe.Fori(q0 // 2, (q0 + pairs) // 2) as i:
                    for s in range(2):
                        pair(2 * i + (base_pair + s), s, 2 * i + s, free, first, second, ready, before)

            h = (h_hi, h_lo)
            pe.sem_inc(S["b_free"], CREDIT)
            hp = (hp_hi, hp_lo)
            for k in range(K):
                pe.wait_ge(S["hp_lo_ready"], k + 1)
                if k == 0:
                    pe.wait_ge(S["w_half_ready"], 1)
                elif k == K // 2:
                    pe.wait_ge(S["w_lo_ready"], 1)
                for j in range(2):
                    acc = mm[0][j][:, :]
                    nc.tensor.matmul(acc, w_hi[0][:, j, k, :], hp_hi[:, k, :], start=(k == 0), stop=False)
                    nc.tensor.matmul(acc, w_hi[0][:, j, k, :], hp_lo[:, k, :], start=False, stop=False)
                    last = nc.tensor.matmul(acc, w_lo[0][:, j, k, :], hp_hi[:, k, :], start=False, stop=(k == K - 1))
                    if k == K - 1:
                        last.then_inc(S["mm_done"], 1)
                if k == SUMS_AFTER:
                    pe.wait_ge(S["cst_ld"], 16)
                    for half in range(2):
                        pe.wait_ge(S["xsq_sum"], 3 * half + 3)
                        last = nc.tensor.matmul(st[1][:, :], ones, xsq[:, 4 * half, :], start=(half == 0), stop=(half == 1))
                    last.then_inc(S["stat"], 1)
            pair(PB + 1, 1, 1, S["b_free"], hp, hp)
            for q in (2, 3):
                pair(PB + q, q % 2, q, S["b_free"], h, h, arriving=S["h_lo_ready"])
            stage(PB, 4, 4, S["b_free"], h, h)
            pe.sem_inc(S["c_free"], CREDIT)
            stage(PC, 0, 8, S["c_free"], h, h, before=(S["b_free"], 8))
            pe.sem_inc(S["a1_free"], CREDIT)
            stage(PA1, 0, 8, S["a1_free"], h, h, before=(S["c_free"], 8))
            pe.wait_ge(S["vsum_done"], K + 1)
            nc.tensor.matmul(st[0][:, :], ones, v_sum[:, :], start=True, stop=True).then_inc(S["stat"], 1)
            pe.sem_inc(S["a2_free"], CREDIT)
            stage(PA2, 0, 4, S["a2_free"], h, h, before=(S["a1_free"], 8))
            pe.wait_ge(S["v_sq_added"], K + 1)
            nc.tensor.matmul(st[1][:, :], ones, sqv_sum[:, :], start=True, stop=True).then_inc(S["stat"], 1)
            pe.wait_ge(S["v_centred"], K)
            pe.wait_ge(S["zsum_done"], K + 1)
            nc.tensor.matmul(st[0][:, :], ones, z_sum[:, :], start=True, stop=True).then_inc(S["stat"], 1)
            pe.sem_inc(S["ga_free"], CREDIT)
            stage(PGA, 0, 4, S["ga_free"], h, (za_hi, za_lo), S["za_lo_ready"], (S["a2_free"], 4))
            for m in range(K):
                pe.wait_ge(S["v_ready"], m + 1)
                if m == 2:
                    pe.wait_ge(S["z_centred"], K)
                if m >= 4:
                    pe.wait_ge(S["vt_ready"], m - 3)
                for n in range(TT):
                    last = nc.tensor.transpose(mix[m % 4][:, n, :], v[:, m, n * P:(n + 1) * P], ident)
                last.then_inc(S["vt_ps"], 1)
            pe.wait_ge(S["ws_ld"], 32)
            for m in range(K):
                if m < 4:
                    pe.wait_ge(S["vt_ready"], m + 5)
                if m >= 4:
                    pe.wait_ge(S["mix_free"], m - 3)
                for n in range(TT):
                    last = nc.tensor.matmul(mix[m % 4][:, n, :], v[:, m, n * P:(n + 1) * P], ws_sb[:, m, :],
                                            start=True, stop=True)
                last.then_inc(S["mix_ps"], 1)
            stage(PGA, 4, 4, S["ga_free"], h, (za_hi, za_lo), S["za_lo_ready"])
            pe.wait_ge(S["mix_free"], K)
            pe.wait_ge(S["z_sq_added"], K + 1)
            pe.wait_ge(S["v_root"], 1)
            nc.tensor.matmul(st[1][:, :], ones, sqz_sum[:, :], start=True, stop=True).then_inc(S["stat"], 1)
            pe.sem_inc(S["gc_free"], CREDIT)
            stage(PGC, 0, 8, S["gc_free"], h, (zc_hi, zc_lo), S["zc_lo_ready"], (S["ga_free"], 8))
            pe.sem_inc(S["gb_free"], CREDIT)
            stage(PGB, 0, 8, S["gb_free"], h, (zb_hi, zb_lo), S["zb_lo_ready"], (S["gc_free"], 8))

            def logits(m):
                pe.wait_ge(S["x1T_ready"], m + 1)
                nc.tensor.matmul(st[0][0:P // 2, :], wr_sb[:, m, :], x1T[:, m, :], start=(m == 0), stop=(m == K - 1))
                pe.wait_ge(S["x1_sq_ready"], m + 1)
                nc.tensor.matmul(st[0][P // 2:, :], ones[:, 0:P // 2], sq1[m % 2][:, :],
                                 start=(m == 0), stop=(m == K - 1)).then_inc(S["x1_sq_summed"], 1)

            def to_tokens(m):
                if m >= 2:
                    pe.wait_ge(S["x1_ready"], m - 1)
                for n in range(TT):
                    last = nc.tensor.transpose(tr[m % 2][:, n, :], x1T[:, m, n * P:(n + 1) * P], ident)
                last.then_inc(S["x1_ps"], 1)

            pe.wait_ge(S["wr_scaled"], 1)
            for q in range(4):
                p, s = PW + q, q % 2
                pe.wait_ge(S["w_hi_ready"], p + 1)
                pe.wait_ge(S["w_lo_ready"], p + 1)
                if q < 2:
                    pe.wait_ge(S["gb_free"], 7 + q + CREDIT)
                else:
                    pe.wait_ge(S["x1T_ready"], 2 * q - 2)
                tile(mm[s][0], s, 0, m_hi, m_lo, S["m_lo_ready"] if q == 0 else None)
                tile(mm[s][1], s, 1, m_hi, m_lo)
                if q:
                    for m in (2 * q - 2, 2 * q - 1):
                        logits(m)
                        to_tokens(m)
            for m in (K - 2, K - 1):
                logits(m)
            for m in (K - 2, K - 1):
                to_tokens(m)

            pe.wait_ge(S["lgT_ready"], 1)
            for t in range(TT):
                last = nc.tensor.transpose(st[1][:, t * P:(t + 1) * P], lgT[:, t * P:(t + 1) * P], ident)
            last.then_inc(S["logits_ps"], 1)
            pe.wait_ge(S["hot_ready"], 1)
            nc.tensor.matmul(st[0][:, 0:(TT + 1) * E], ones, earlier[:, :, :].rearrange("p t e -> p (t e)"),
                             start=True, stop=False)
            nc.tensor.matmul(st[0][:, 0:TT * E], upper, both[:, :, :].rearrange("p t e -> p (t e)"),
                             start=False, stop=True).then_inc(S["ranks_ps"], 1)
            pe.wait_ge(S["found_ready"], 1)
            for a in range(2 * TT):
                last = nc.tensor.matmul(st[1][0:SLOTS, 0:RUN], is_q[:, a, :], is_item[:, a, :],
                                        start=(a == 0), stop=(a == 2 * TT - 1))
            last.then_inc(S["rows_ps"], 1)

            pe.wait_ge(S["tab_ready"], 1)
            pairs = pe.value_load(tab[0:1, T_N:T_N + 1], min_val=PAIRS_MIN, max_val=ITEMS // 2)
            pe.sem_inc(S["m13_half"], 1)
            pe.sem_inc(S["m13_done"], 1)
            pe.sem_inc(S["y_ps"], 1)

            def rows_T():
                for k in range(K):
                    last = nc.tensor.transpose(tr[k // 4][:, k % 4, :], xg[:, k * P:(k + 1) * P], ident)
                last.then_inc(S["xgT_ps"], 1)

            def up(s, w):
                for k in range(K):
                    for j in range(2):
                        last = nc.tensor.matmul(mm[s][0][j * SLOTS:(j + 1) * SLOTS, :], xgT[:, k, s * SLOTS:(s + 1) * SLOTS],
                                                ew13[w][:, k, j, :], start=(k == 0), stop=(k == K - 1))
                    if k == K // 2 - 1:
                        last.then_inc(S["m13_half"], 1)
                last.then_inc(S["m13_done"], 1)

            def down(s, w):
                for c in range(FF // P):
                    for j in range(2):
                        last = nc.tensor.matmul(mm[s][1][j * SLOTS:(j + 1) * SLOTS, :],
                                                eactT[s][:, c % 2, (c // 2) * SLOTS:(c // 2 + 1) * SLOTS],
                                                ew2[w][:, c, j * FF:(j + 1) * FF],
                                                start=(c == 0), stop=(c == FF // P - 1))
                last.then_inc(S["y_ps"], 1)

            def by_buffer(buf, turn, landed, products, s):
                with pe.If(buf == 0):
                    pe.wait_ge(landed[0], turn)
                    products(s, 0)
                with pe.Else():
                    with pe.If(buf == 1):
                        pe.wait_ge(landed[1], turn)
                        products(s, 1)
                    with pe.Else():
                        pe.wait_ge(landed[2], turn)
                        products(s, 2)

            pe.wait_ge(S["xg_ld"], 32)
            rows_T()
            with pe.Fori(0, pairs) as i:
                for s in range(2):
                    n = 2 * i + s
                    turn = pe.value_load(tab[0:1, ds(n + T_TURN, 1)], min_val=16, max_val=16 * TURNS)
                    turn13 = pe.snap(turn * 2)
                    buf = pe.value_load(tab[0:1, ds(n + T_BUF, 1)], min_val=0, max_val=RING - 1)
                    pe.wait_ge(S["xgT_ready"], i + 1)
                    by_buffer(buf, turn13, w13_ld, up, s)
                    if s == 1:
                        pe.wait_ge(S["xg_ld"], i * 32 + 64)
                        rows_T()
                    pe.wait_ge(S["eact_ready"], n + 1)
                    for c in range(2):
                        last = nc.tensor.transpose(st[s][:, c * P:(c + 1) * P], eact[s][:, c * P:(c + 1) * P], ident)
                    last.then_inc(S["eactT_ps"], 1)
                    pe.wait_ge(S["eactT_ready"], n + 1)
                    by_buffer(buf, turn, w2_ld, down, s)

        @block.scalar
        def _(act):
            A = nc.scalar.activation

            def split(p, s, turn, done=None):
                if done is not None:
                    act.wait_ge(S["mm_done"], done)
                act.wait_ge(raw_ld[s], 16 * turn)
                A(w_hi[s][:, :, :, :], w_raw[s][:, :, :, :], ACT.Copy).then_inc(S["w_hi_ready"], 1)

            for c in range(K // 2):
                act.wait_ge(x_ld[c], 16)
                A(xsq[:, 2 * c:2 * c + 2, :], xt[:, 2 * c:2 * c + 2, :], ACT.Square).then_inc(S["xsq_ready"], 1)
                act.wait_ge(S["par_ld"], 16)
                for k in (2 * c, 2 * c + 1):
                    A(hp_hi[:, k, :], xt[:, k, :], ACT.Copy, scale=par[:, k, V_GM:V_GM + 1]).then_inc(S["hp_hi_ready"], 1)
                if c == 0:
                    act.wait_ge(raw_ld[0], 16)
                    for half, done in ((0, S["w_hi_half"]), (1, S["w_hi_ready"])):
                        k = slice(half * K // 2, (half + 1) * K // 2)
                        A(w_hi[0][:, :, k, :], w_raw[0][:, :, k, :], ACT.Copy).then_inc(done, 1)
            split(1, 1, 1)
            act.wait_ge(S["stat"], 1)
            act.wait_ge(S["eps_set"], 2)
            A(tmp[0][:, :], st[1][:, :], ACT.Sqrt, scale=1.0 / D, bias=eps_rms).then_inc(S["rms_root"], 1)
            split(0, 0, 2, 2)

            def first_gate(s):
                act.wait_ge(S["gate_scaled"], s + 1)
                A(sig[s][:, :], tmp[1][:, :], ACT.Sigmoid).then_inc(S["sig_ready"], 1)

            for k in range(K):
                act.wait_ge(S["h_ready"], k + 1)
                A(h_hi[:, k, :], xt[:, k, :], ACT.Copy).then_inc(S["h_hi_ready"], 1)
                if k == GATE_AFTER:
                    first_gate(0)
            first_gate(1)
            split(1, 1, 2)

            with act.Fori(1, 4) as i:
                for s in range(2):
                    p = 2 * i + (PB + s)
                    act.wait_ge(S["mm_done"], 2 * p + 2)
                    A(sig[s][:, :], mm[s][1][:, :], ACT.Sigmoid).then_inc(S["sig_ready"], 1)
                    split(p, s, i + (PB // 2 + 2))
            with act.Fori(0, 4) as i:
                for s in range(2):
                    p, q = 2 * i + (PC + s), 2 * i + s
                    act.wait_ge(S["mm_done"], 2 * p + 1)
                    A(u[:, q, :], mm[s][0][:, :], ACT.Gelu_apprx_tanh)
                    act.wait_ge(S["mm_done"], 2 * p + 2)
                    A(v[:, q, :], mm[s][1][:, :], ACT.Gelu_apprx_tanh).then_inc(S["c_free"], 1)
                    split(p, s, i + (PC // 2 + 2))
            with act.Fori(0, 4) as i:
                for s in range(2):
                    p = 2 * i + (PA1 + s)
                    act.wait_ge(S["mm_done"], 2 * p + 1)
                    A(sig[s][:, :], mm[s][0][:, :], ACT.Copy).then_inc(S["ca_ready"], 1)
                    split(p, s, i + (PA1 // 2 + 2), 2 * p + 2)
            def squares(a, q, ring, centred, ready, added):
                for j in range(2):
                    act.wait_ge(centred, 2 * q + (j + 1))
                    act.wait_ge(added, 2 * q + j if j else 2 * q + 1)
                    A(ring[j][:, :], a[:, ds(2 * q + j, 1), :], ACT.Square).then_inc(ready, 1)

            with act.Fori(0, 2) as i:
                for s in range(2):
                    p, q = 2 * i + (PA2 + s), 2 * i + s
                    squares(v, q, sqv, S["v_centred"], S["v_sq"], S["v_sq_added"])
                    for j in range(2):
                        act.wait_ge(S["za_ready"], 2 * q + j + 1)
                        A(za_hi[:, 2 * q + j, :], tmp[j][:, :], ACT.Copy).then_inc(S["za_hi_ready"], 1)
                    split(p, s, i + (PA2 // 2 + 2), 2 * p + 2)
            act.wait_ge(S["stat"], 3)
            act.wait_ge(S["za_lo_ready"], K)
            A(v_rstd, st[1][:, :], ACT.Sqrt, scale=1.0 / D, bias=eps_ln).then_inc(S["v_root"], 1)

            def gate(p, s):
                act.wait_ge(S["mm_done"], 2 * p + 1)
                A(sig[s][:, :], mm[s][0][:, :], ACT.Sigmoid).then_inc(S["sig_ready"], 1)

            with act.Fori(0, 2) as i:
                for s in range(2):
                    p = 2 * i + (PGA + s)
                    squares(zb, 2 * i + s, sqz, S["z_centred"], S["z_sq"], S["z_sq_added"])
                    gate(p, s)
                    split(p, s, i + (PGA // 2 + 2), 2 * p + 2)
            for m in range(K):
                act.wait_ge(S["vt_ps"], m + 1)
                A(v[:, m, :].rearrange("p (n q) -> p n q", n=TT), mix[m % 4], ACT.Copy).then_inc(S["vt_ready"], 1)
            for m in range(K):
                act.wait_ge(S["zc_ready"], m + 1)
                A(zc_hi[:, m, :], u[:, m, :], ACT.Copy).then_inc(S["zc_hi_ready"], 1)
            with act.Fori(2, 4) as i:
                for s in range(2):
                    p = 2 * i + (PGA + s)
                    gate(p, s)
                    split(p, s, i + (PGA // 2 + 2), 2 * p + 2)
            act.wait_ge(S["stat"], 5)
            A(z_rstd, st[1][:, :], ACT.Sqrt, scale=1.0 / D, bias=eps_ln).then_inc(S["z_root"], 1)
            with act.Fori(0, 4) as i:
                for s in range(2):
                    p, q = 2 * i + (PGC + s), 2 * i + s
                    act.wait_ge(S["z_normed"], q + 1)
                    A(tmp[s][:, :], zb[:, ds(q, 1), :], ACT.Sigmoid,
                      scale=par[:, ds(q, 1), V_BG:V_BG + 1], bias=par[:, ds(q, 1), V_BB:V_BB + 1]).then_inc(S["z_sig"], 1)
                    gate(p, s)
                    act.wait_ge(S["zb_ready"], q + 1)
                    A(zb_hi[:, ds(q, 1), :], zb[:, ds(q, 1), :], ACT.Copy).then_inc(S["zb_hi_ready"], 1)
                    split(p, s, i + (PGC // 2 + 2), 2 * p + 2)
            with act.Fori(0, 4) as i:
                for s in range(2):
                    p, q = 2 * i + (PGB + s), 2 * i + s
                    gate(p, s)
                    act.wait_ge(S["gb_free"], q + 1 + CREDIT)
                    A(m_hi[:, ds(q, 1), :], merged[:, ds(q, 1), :], ACT.Copy).then_inc(S["m_hi_ready"], 1)
                    split(p, s, i + (PGB // 2 + 2), 2 * p + 2)
            act.wait_ge(S["gb_free"], 8 + CREDIT)
            A(small[:, 2:3], eps_ln, ACT.Sqrt)
            for q in range(4):
                s, p = q % 2, PW + q
                if q < 2:
                    split(p, s, p // 2 + 2, 2 * p + 2)
                for j in range(2):
                    m = 2 * q + j
                    act.wait_ge(S["x1T_ready"], m + 1)
                    if m >= 2:
                        act.wait_ge(S["x1_sq_summed"], m - 1)
                    A(sq1[j][:, :], x1T[:, m, :], ACT.Square).then_inc(S["x1_sq_ready"], 1)
            act.wait_ge(S["x1_sq_summed"], K)
            A(lgT[:, :], st[0][:, :], ACT.Copy).then_inc(S["lgT_ready"], 1)
            act.wait_ge(S["logits_ps"], 1)
            A(rstd, st[1][:, :].rearrange("p (t r) -> p t r", t=TT)[:, :, P // 2], ACT.Sqrt,
              scale=1.0 / D, bias=eps_rms).then_inc(S["x1_root"], 1)
            for m in (K - 2, K - 1):
                act.wait_ge(S["x1_ps"], m + 1)
                A(x_tok[:, :, m * P:(m + 1) * P], tr[m % 2][:, :, :], ACT.Copy).then_inc(S["x1_ready"], 1)
            act.wait_ge(S["x1_rstd"], 1)
            act.wait_ge(S["x1_ready"], K)
            for t in range(TT):
                A(h2[:, t, :], x_tok[:, t, :], ACT.Copy, scale=rstd[:, t:t + 1]).then_inc(S["h2_ready"], 1)
            act.wait_ge(S["exp_wanted"], 1)
            A(gexp[:, :, :], gexp[:, :, :], ACT.Exp).then_inc(S["exp_ready"], 1)
            act.wait_ge(S["exp_wanted"], 2)
            A(wgt[1][:, :], wgt[1][:, :], ACT.Exp).then_inc(S["exp_ready"], 1)
            A(small[:, 3:4], eps_ln, ACT.Sigmoid)

            act.wait_ge(S["tab_ready"], 1)
            act.wait_ge(S["rows_stored"], 16 * TT)
            pairs = act.value_load(tab[0:1, T_N:T_N + 1], min_val=PAIRS_MIN, max_val=ITEMS // 2)

            def item(s, n, stored):
                act.wait_ge(S["m13_done"], n + 2)
                A(esig[s][:, :], mm[s][0][:, 0:FF // 2], ACT.Sigmoid).then_inc(S["esig_ready"], 1)
                act.wait_ge(S["eactT_ps"], n + 1)
                A(eactT[s][:, :, :].rearrange("p a b -> p (a b)"), st[s][:, 0:2 * P], ACT.Copy).then_inc(S["eactT_ready"], 1)
                if stored is not None:
                    act.wait_ge(y_st[s], stored)
                act.wait_ge(S["y_ps"], n + 2)
                A(ey[s][:, :], mm[s][1][:, :], ACT.Copy).then_inc(S["y_copied"], 1)

            for s in range(2):
                item(s, s, None)
            with act.Fori(1, pairs) as i:
                for s in range(2):
                    item(s, 2 * i + s, 32 * i)
            for t in range(TT):
                act.wait_ge(S["both_added"], t + 1)
                A(junk[:, :], x_tok[:, t, :], ACT.Square, accum_out=sum_sq[:, t:t + 1]).then_inc(S["ss_ready"], 1)
                act.wait_ge(S["ss_ready"], t + 1)
                A(rstd[:, t:t + 1], sum_sq[:, t:t + 1], ACT.Sqrt, scale=1.0 / D, bias=eps_rms).then_inc(S["final_root"], 1)

        @block.gpsimd
        def _(pool):
            TTo = nc.gpsimd.tensor_tensor
            def split(p, s):
                pool.wait_ge(S["w_hi_ready"], p + 1)
                TTo(w_lo[s][:, :, :, :], w_raw[s][:, :, :, :], w_hi[s][:, :, :, :].bitcast(F32),
                    ALU.subtract).then_inc(S["w_lo_ready"], 1)

            for half, taken, done in ((0, S["w_hi_half"], S["w_half_ready"]), (1, S["w_hi_ready"], S["w_lo_ready"])):
                pool.wait_ge(taken, 1)
                k = slice(half * K // 2, (half + 1) * K // 2)
                TTo(w_lo[0][:, :, k, :], w_raw[0][:, :, k, :], w_hi[0][:, :, k, :].bitcast(F32), ALU.subtract)\
                    .then_inc(done, 1)
            split(1, 1)

            with pool.Fori(0, 4) as i:
                for s in range(2):
                    split(2 * i + (PB + 2 + s), s)
            nc.gpsimd.memset(v_sum[:, :], 0.0).then_inc(S["vsum_done"], 1)
            nc.gpsimd.memset(z_sum[:, :], 0.0).then_inc(S["zsum_done"], 1)
            with pool.Fori(0, 4) as i:
                for s in range(2):
                    q = 2 * i + s
                    pool.wait_ge(S["c_free"], q + 1 + CREDIT)
                    pool.wait_ge(S["vsum_done"], q + 1)
                    TTo(v_sum[:, :], v_sum[:, :], v[:, q, :], ALU.add).then_inc(S["vsum_done"], 1)
                    split(2 * i + (PC + 2 + s), s)
                pool.wait_ge(S["zb_conv"], i + 1)
                pool.wait_ge(S["zsum_done"], i + 1)
                TTo(z_sum[:, :], z_sum[:, :], zb[:, ds(i, 1), :], ALU.add).then_inc(S["zsum_done"], 1)
            with pool.Fori(0, 4) as i:
                for s in range(2):
                    split(2 * i + (PA1 + 2 + s), s)
                pool.wait_ge(S["zb_conv"], i + 5)
                pool.wait_ge(S["zsum_done"], i + 5)
                TTo(z_sum[:, :], z_sum[:, :], zb[:, ds(i + 4, 1), :], ALU.add).then_inc(S["zsum_done"], 1)
            pool.wait_ge(S["zsum_done"], K + 1)

            def squares(acc, q, ring, ready, added):
                for j in range(2):
                    pool.wait_ge(ready, 2 * q + (j + 1))
                    pool.wait_ge(added, 2 * q + (j + 1))
                    TTo(acc[:, :], acc[:, :], ring[j][:, :], ALU.add).then_inc(added, 1)

            pool.wait_ge(S["zb_conv"], K)
            nc.gpsimd.memset(sqv_sum[:, :], 0.0).then_inc(S["v_sq_added"], 1)
            with pool.Fori(0, 2) as i:
                for s in range(2):
                    squares(sqv_sum, 2 * i + s, sqv, S["v_sq"], S["v_sq_added"])
                    split(2 * i + (PA2 + 2 + s), s)
            pool.wait_ge(S["za_lo_ready"], K)
            nc.gpsimd.memset(sqz_sum[:, :], 0.0).then_inc(S["z_sq_added"], 1)
            pool.dma_start(ws_sb[:, :, :], wsT).then_inc(S["ws_ld"], 16)
            pool.dma_start(bs_sb[:, :, :].rearrange("p a b -> p (a b)"), bs.partition_broadcast(P)).then_inc(S["ws_ld"], 16)
            with pool.Fori(0, 2) as i:
                for s in range(2):
                    squares(sqz_sum, 2 * i + s, sqz, S["z_sq"], S["z_sq_added"])
                    split(2 * i + (PGA + 2 + s), s)
            with pool.Fori(2, 4) as i:
                for s in range(2):
                    split(2 * i + (PGA + 2 + s), s)
            pool.wait_ge(S["mix_free"], K)
            pool.wait_ge(S["z_root"], 1)
            pool.dma_start(x1T[:, :, :], xT).then_inc(S["x_again_ld"], 16)
            with pool.Fori(0, 4) as i:
                for s in range(2):
                    split(2 * i + (PGC + 2 + s), s)
            pool.wait_ge(S["zb_ready"], K)
            pool.dma_start(wr_sb[:, :, :], wr).then_inc(S["wr_ld"], 16)
            pool.dma_start(rb_sb, rbias.partition_broadcast(P)).then_inc(S["rbias_ld"], 16)
            pool.wait_ge(S["wr_ld"], 16)
            TTo(wr_sb[:, :, :], wr_sb[:, :, :], par[:, :, V_GF:V_GF + 1].to_broadcast([P, K, P // 2]), ALU.mult)\
                .then_inc(S["wr_scaled"], 1)
            with pool.Fori(4, (PEND - PGC) // 2 - 1) as i:
                for s in range(2):
                    split(2 * i + (PGC + 2 + s), s)
            def half_empty(n):
                return pool.value_load(less[0:1, ds(n, 1)], min_val=0, max_val=1) == 1

            def fetch_rows(s, rows):
                nc.gpsimd.indirect_dma_start(
                    xg[s * SLOTS:s * SLOTS + rows, :], None, hs[:, :],
                    bass.IndirectOffsetOnAxis(ap=next_rows[s][0:rows, :], axis=0),
                    bounds_check=T - 1).then_inc(S["xg_ld"], 16)

            def rows_of(n, s):
                nc.gpsimd.tensor_copy(next_rows[s][:, :], row_x[0:SLOTS, ds(n, 1)]).then_inc(S["x_rows"], 1)
                pool.wait_ge(S["x_rows"], n + 1)
                pool.sem_inc(S["x_fetch"], 1)

            def fetch_pair(i):
                short = [half_empty(2 * i + s) for s in range(2)]
                pool.wait_ge(S["xgT_ps"], i)
                for s in range(2):
                    rows_of(2 * i + s, s)
                    with pool.If(short[s]):
                        fetch_rows(s, SLOTS // 2)
                    with pool.Else():
                        fetch_rows(s, SLOTS)

            def store_rows(s, rows):
                for j in range(2):
                    nc.gpsimd.indirect_dma_start(
                        ys_halves, bass.IndirectOffsetOnAxis(ap=item_rows[s][0:rows, j:j + 1], axis=0),
                        ey[s][j * SLOTS:j * SLOTS + rows, :], None,
                        bounds_check=2 * (2 * T + RUN * SLOTS) - 1).then_inc(y_st[s], 16)

            def store(n, s):
                short = half_empty(n)
                pool.wait_ge(S["y_copied"], n + 1)
                nc.gpsimd.tensor_copy(item_rows[s][:, :], row_y[0:SLOTS, ds(n, 1), :].rearrange("p a j -> p (a j)"))\
                    .then_inc(S["y_rows"], 1)
                pool.wait_ge(S["y_rows"], n + 1)
                pool.sem_inc(S["y_store"], 1)
                with pool.If(short):
                    store_rows(s, SLOTS // 2)
                with pool.Else():
                    store_rows(s, SLOTS)

            pool.wait_ge(S["rows_stored"], 16 * TT)
            pool.dma_start(gfin_sb[:, :], gfin.partition_broadcast(P)).then_inc(S["gfin_ld"], 16)
            pool.wait_ge(S["rows_ready"], 1)
            for n in range(4):
                if n == 2:
                    pool.wait_ge(S["xgT_ps"], 1)
                rows_of(n, n % 2)
                fetch_rows(n % 2, SLOTS)
            pool.wait_ge(S["rows_ready"], 2)
            pool.wait_ge(S["tab_ready"], 1)
            pairs = pool.value_load(tab[0:1, T_N:T_N + 1], min_val=PAIRS_MIN, max_val=ITEMS // 2)
            with pool.Fori(0, pairs) as i:
                store(2 * i, 0)
                fetch_pair(i + 2)
                store(2 * i + 1, 1)
            stored = pool.snap(pairs * 32)
            loaded = pool.snap(pairs * 32 + 64)
            for s in range(2):
                pool.wait_ge(y_st[s], stored)
            pool.wait_ge(S["xg_ld"], loaded)
            for b in range(RING):
                turns = (E - b + RING - 1) // RING
                pool.wait_ge(w13_ld[b], 32 * turns)
                pool.wait_ge(w2_ld[b], 16 * turns)
            pool.sem_inc(S["all_stored"], 1)

        @block.vector
        def _(dve):
            V = nc.vector
            STT, TTo, TS = V.scalar_tensor_tensor, V.tensor_tensor, V.tensor_scalar

            for edge in (zb_pad[:, :, 0:PAD_B], zb_pad[:, :, PAD_B + T:]):
                V.memset(edge, 0.0).then_inc(S["edge_set"], 1)
            V.memset(eps_rms, RMS_EPS).then_inc(S["eps_set"], 1)
            V.memset(eps_ln, LN_EPS).then_inc(S["eps_set"], 1)
            dve.wait_ge(S["par_ld"], 16)
            for c in range(K // 2):
                for k in (2 * c, 2 * c + 1):
                    dve.wait_ge(S["hp_hi_ready"], k + 1)
                    STT(hp_lo[:, k, :], xt[:, k, :], par[:, k, V_GM:V_GM + 1], hp_hi[:, k, :].bitcast(F32),
                        ALU.mult, ALU.subtract).then_inc(S["hp_lo_ready"], 1)
                dve.wait_ge(S["xsq_ready"], c + 1)
                TTo(xsq[:, 2 * c, :], xsq[:, 2 * c, :], xsq[:, 2 * c + 1, :], ALU.add).then_inc(S["xsq_sum"], 1)
                if c % 2:
                    dve.wait_ge(S["xsq_sum"], 3 * (c // 2) + 2)
                    TTo(xsq[:, 2 * c - 2, :], xsq[:, 2 * c - 2, :], xsq[:, 2 * c, :], ALU.add).then_inc(S["xsq_sum"], 1)
            dve.wait_ge(S["rms_root"], 1)
            rms = tmp[0][:, :]
            V.reciprocal(rms, rms).then_inc(S["h_step"], 1)
            dve.wait_ge(S["h_step"], 1)
            dve.wait_ge(S["hp_lo_ready"], K)

            def scale_gate(s):
                dve.wait_ge(S["mm_done"], 2 * s + 2)
                TTo(tmp[1][:, :], mm[s][1][:, :], rms, ALU.mult).then_inc(S["gate_scaled"], 1)

            def scale_value(s):
                z = zb_pad[:, s, PAD_B:PAD_B + T]
                dve.wait_ge(S["sig_ready"], s + 1)
                TTo(z, mm[s][0][:, :], sig[s][:, :], ALU.mult).then_inc(S["b_free"], 1)
                dve.wait_ge(S["b_free"], s + 1 + CREDIT)
                TTo(z, z, rms, ALU.mult).then_inc(S["value_scaled"], 1)

            for k in range(K + 1):
                if k < K:
                    STT(xt[:, k, :], xt[:, k, :], par[:, k, V_GM:V_GM + 1], rms, ALU.mult, ALU.mult)\
                        .then_inc(S["h_ready"], 1)
                if k:
                    dve.wait_ge(S["h_hi_ready"], k)
                    TTo(h_lo[:, k - 1, :], xt[:, k - 1, :], h_hi[:, k - 1, :].bitcast(F32), ALU.subtract)\
                        .then_inc(S["h_lo_ready"], 1)
                if k == GATE_AFTER:
                    scale_gate(0)
                elif k == GATE_AFTER + 3:
                    scale_value(0)
            dve.wait_ge(S["h_lo_ready"], K)
            for edge in (ca_pad[:, :, 0:PAD_A], ca_pad[:, :, PAD_A + T:]):
                V.memset(edge, 0.0).then_inc(S["edge_set"], 1)
            dve.wait_ge(S["edge_set"], 4)

            def taps_b(m, j0, j1):
                for j in range(j0, j1):
                    acc = zb[:, ds(m, 1), :] if j % 2 == 0 else tmp[0][:, :]
                    z = zb_pad[:, ds(m, 1), j:j + T]
                    w = par[:, ds(m, 1), V_CB + j:V_CB + j + 1]
                    if j < 2:
                        TS(acc, z, w, None, ALU.mult).then_inc(S["tap_done"], 1)
                    else:
                        dve.wait_ge(S["tap_done"], m * (TAPS_B + 1) + (j - 1))
                        STT(acc, z, w, acc, ALU.mult, ALU.add).then_inc(S["tap_done"], 1)
                if j1 == TAPS_B:
                    dve.wait_ge(S["tap_done"], m * (TAPS_B + 1) + TAPS_B)
                    TTo(zb[:, ds(m, 1), :], zb[:, ds(m, 1), :], tmp[0][:, :], ALU.add).then_inc(S["zb_conv"], 1)
                    dve.wait_ge(S["zb_conv"], m + 1)
                    dve.sem_inc(S["tap_done"], 1)

            def conv_part(m, s):
                half = (TAPS_B + 1) // 2
                taps_b(m, *((0, half) if s == 0 else (half, TAPS_B)))

            def value_gated(q, s):
                dve.wait_ge(S["sig_ready"], q + 1)
                TTo(zb_pad[:, ds(q, 1), PAD_B:PAD_B + T], mm[s][0][:, :], sig[s][:, :], ALU.mult)\
                    .then_inc(S["b_free"], 1)

            def a_product(q, s):
                dve.wait_ge(S["ca_ready"], q + 1)
                dve.wait_ge(S["mm_done"], 2 * q + (2 * (PA1 + 1)))
                TTo(ca_pad[:, ds(q, 1), PAD_A:PAD_A + T], mm[s][1][:, :], sig[s][:, :], ALU.mult)\
                    .then_inc(S["a1_free"], 1)

            scale_gate(1)
            scale_value(1)
            dve.wait_ge(S["value_scaled"], 2)
            with dve.Fori(1, 4) as i:
                for s in range(2):
                    value_gated(2 * i + s, s)
                    dve.wait_ge(S["b_free"], i + (1 + CREDIT))
                    conv_part(i - 1, s)
            dve.wait_ge(S["b_free"], 8 + CREDIT)
            with dve.Fori(3, 7) as i:
                for s in range(2):
                    conv_part(i, s)
            for s in range(2):
                a_product(s, s)
                conv_part(K - 1, s)
            with dve.Fori(1, 4) as i:
                for s in range(2):
                    a_product(2 * i + s, s)
            def centre(a, m, done):
                STT(a[:, ds(m, 1), :], st[0][:, :], -1.0 / D, a[:, ds(m, 1), :], ALU.mult, ALU.add).then_inc(done, 1)

            dve.wait_ge(S["stat"], 2)
            dve.wait_ge(S["a1_free"], 8 + CREDIT)
            with dve.Fori(0, 2) as i:
                for s in range(2):
                    p, q = 2 * i + (PA2 + s), 2 * i + s
                    for j in range(2):
                        centre(v, 2 * q + j, S["v_centred"])
                    for j in range(2):
                        m = 2 * q + j
                        for tap in range(TAPS_A):
                            c = ca_pad[:, ds(m, 1), tap:tap + T]
                            w = par[:, ds(m, 1), V_CA + tap:V_CA + tap + 1]
                            if tap == 0:
                                TS(sig[j][:, :], c, w, None, ALU.mult).then_inc(S["za_step"], 1)
                            else:
                                STT(sig[j][:, :], c, w, sig[j][:, :], ALU.mult, ALU.add).then_inc(S["za_step"], 1)
                            dve.wait_ge(S["za_step"], m * TAPS_A + (tap + 1))
                        dve.wait_ge(S["mm_done"], 2 * p + j + 1)
                        TTo(tmp[j][:, :], mm[s][j][:, :], sig[j][:, :], ALU.mult).then_inc(S["za_ready"], 1)
                    dve.wait_ge(S["za_ready"], 2 * q + 2)
                    dve.sem_inc(S["a2_free"], 1)
                    for j in range(2):
                        m = 2 * q + j
                        dve.wait_ge(S["za_hi_ready"], m + 1)
                        TTo(za_lo[:, ds(m, 1), :], tmp[j][:, :], za_hi[:, ds(m, 1), :].bitcast(F32), ALU.subtract)\
                            .then_inc(S["za_lo_ready"], 1)
            dve.wait_ge(S["v_root"], 1)
            V.reciprocal(v_rstd, v_rstd).then_inc(S["v_step"], 1)
            dve.wait_ge(S["v_step"], 1)
            dve.wait_ge(S["v_centred"], K)

            def first_gated(q, s):
                dve.wait_ge(S["sig_ready"], q + 9)
                dve.wait_ge(S["mm_done"], 2 * q + (2 * (PGA + 1)))
                TTo(merged[:, ds(q, 1), :], mm[s][1][:, :], sig[s][:, :], ALU.mult).then_inc(S["ga_free"], 1)

            dve.wait_ge(S["stat"], 4)
            with dve.Fori(0, 2) as i:
                for s in range(2):
                    q = 2 * i + s
                    for m in (2 * q, 2 * q + 1):
                        TTo(v[:, ds(m, 1), :], v[:, ds(m, 1), :], v_rstd, ALU.mult).then_inc(S["v_step"], 1)
                        centre(zb, m, S["z_centred"])
                    for m in (2 * q, 2 * q + 1):
                        dve.wait_ge(S["v_step"], m + 2)
                        TS(v[:, ds(m, 1), :], v[:, ds(m, 1), :], par[:, ds(m, 1), V_CG:V_CG + 1],
                           par[:, ds(m, 1), V_CBI:V_CBI + 1], ALU.mult, ALU.add).then_inc(S["v_ready"], 1)
                    first_gated(q, s)
            dve.wait_ge(S["ws_ld"], 32)
            for m in range(K):
                dve.wait_ge(S["mix_ps"], m + 1)
                t = tmp[m % 2]
                TTo(t[:, :].rearrange("p (n q) -> p n q", n=TT), mix[m % 4],
                    bs_sb[:, m, :].unsqueeze(1).to_broadcast([P, TT, P]), ALU.add).then_inc(S["mix_free"], 1)
                dve.wait_ge(S["mix_free"], m + 1)
                TTo(u[:, m, :], u[:, m, :], t[:, :], ALU.mult).then_inc(S["zc_ready"], 1)
            for m in range(K):
                dve.wait_ge(S["zc_hi_ready"], m + 1)
                TTo(zc_lo[:, m, :], u[:, m, :], zc_hi[:, m, :].bitcast(F32), ALU.subtract).then_inc(S["zc_lo_ready"], 1)
            with dve.Fori(2, 4) as i:
                for s in range(2):
                    first_gated(2 * i + s, s)
            dve.wait_ge(S["ga_free"], 8 + CREDIT)
            dve.wait_ge(S["z_root"], 1)
            V.reciprocal(z_rstd, z_rstd).then_inc(S["z_inv"], 1)
            dve.wait_ge(S["z_inv"], 1)

            def add_gated(p, q, s, first_sig, step, free):
                dve.wait_ge(S["sig_ready"], q + first_sig)
                dve.wait_ge(S["mm_done"], 2 * p + 2)
                TTo(sig[s][:, :], mm[s][1][:, :], sig[s][:, :], ALU.mult).then_inc(S["gated"], 1)
                dve.wait_ge(S["gated"], q + step)
                TTo(merged[:, ds(q, 1), :], merged[:, ds(q, 1), :], sig[s][:, :], ALU.add).then_inc(free, 1)

            with dve.Fori(0, 4) as i:
                for s in range(2):
                    p, q = 2 * i + (PGC + s), 2 * i + s
                    z = zb[:, ds(q, 1), :]
                    TTo(z, z, z_rstd, ALU.mult).then_inc(S["z_normed"], 1)
                    dve.wait_ge(S["z_sig"], q + 1)
                    TS(z, z, par[:, ds(q, 1), V_BG:V_BG + 1], par[:, ds(q, 1), V_BB:V_BB + 1], ALU.mult, ALU.add)\
                        .then_inc(S["z_affine"], 1)
                    dve.wait_ge(S["z_affine"], q + 1)
                    TTo(z, z, tmp[s][:, :], ALU.mult).then_inc(S["zb_ready"], 1)
                    add_gated(p, q, s, 17, 1, S["gc_free"])
                    dve.wait_ge(S["zb_hi_ready"], q + 1)
                    TTo(zb_lo[:, ds(q, 1), :], z, zb_hi[:, ds(q, 1), :].bitcast(F32), ALU.subtract)\
                        .then_inc(S["zb_lo_ready"], 1)
            dve.wait_ge(S["gc_free"], 8 + CREDIT)
            with dve.Fori(0, 4) as i:
                for s in range(2):
                    p, q = 2 * i + (PGB + s), 2 * i + s
                    add_gated(p, q, s, 25, 9, S["gb_free"])
                    dve.wait_ge(S["m_hi_ready"], q + 1)
                    TTo(m_lo[:, ds(q, 1), :], merged[:, ds(q, 1), :], m_hi[:, ds(q, 1), :].bitcast(F32), ALU.subtract)\
                        .then_inc(S["m_lo_ready"], 1)
            dve.wait_ge(S["x_again_ld"], 16)
            for q in range(4):
                for j in range(2):
                    m = 2 * q + j
                    dve.wait_ge(S["mm_done"], 2 * PW + m + 1)
                    TTo(x1T[:, m, :], mm[q % 2][j][:, :], x1T[:, m, :], ALU.add).then_inc(S["x1T_ready"], 1)
                if q:
                    for m in (2 * q - 2, 2 * q - 1):
                        dve.wait_ge(S["x1_ps"], m + 1)
                        V.tensor_copy(x_tok[:, :, m * P:(m + 1) * P], tr[m % 2][:, :, :]).then_inc(S["x1_ready"], 1)

            steps = [0]

            def step(ins):
                steps[0] += 1
                ins.then_inc(S["route_step"], 1)
                dve.wait_ge(S["route_step"], steps[0])

            def over(ap, shape, axis):
                return ap.unsqueeze(axis).to_broadcast(shape)

            def first_max(values, top, hot, where, width):
                shape = [P, TT, width]
                index = over(cst[:, C_I32:C_I32 + width], shape, 1)
                step(V.tensor_reduce(top[:, :], values, AX.X, ALU.max))
                step(TTo(hot[:, :, :], values, over(top[:, :], shape, 2), ALU.is_equal))
                step(STT(hot[:, :, :], hot[:, :, :], -100.0, index, ALU.mult, ALU.add))
                step(V.tensor_reduce(where[:, :], hot[:, :, :], AX.X, ALU.min))
                step(STT(hot[:, :, :], index, -100.0, over(where[:, :], shape, 2), ALU.add, ALU.is_equal))

            dve.wait_ge(S["x1_ps"], K)
            for zero in (earlier[:, 0, :], blocks[:, 0:E // 2], scan[0][:, 0:E // 2], scan[1][:, 0:E // 2]):
                V.memset(zero, 0.0).then_inc(S["preset_done"], 1)
            V.memset(lessf[:, ITEMS:], 1.0).then_inc(S["preset_done"], 1)
            dve.wait_ge(S["preset_done"], 5)
            dve.wait_ge(S["logits_ps"], 1)
            dve.wait_ge(S["x1_root"], 1)
            V.reciprocal(rstd, rstd).then_inc(S["x1_rstd"], 1)
            dve.wait_ge(S["x1_rstd"], 1)
            step(TTo(lg[:, :, :], st[1][:, :].rearrange("p (t r) -> p t r", t=TT)[:, :, 0:G + E],
                     over(rstd, [P, TT, G + E], 2), ALU.mult))
            dve.wait_ge(S["rbias_ld"], 16)
            step(TTo(lg[:, :, :], lg[:, :, :], over(rb_sb, [P, TT, G + E], 1), ALU.add))
            first_max(lg[:, :, 0:G], gmax, ghot, gidx, G)
            step(TTo(gexp[:, :, :], lg[:, :, 0:G], over(gmax[:, :], [P, TT, G], 2), ALU.subtract))
            dve.sem_inc(S["exp_wanted"], 1)
            step(TS(ghot[:, :, :], ghot[:, :, :], BIG, -BIG, ALU.mult, ALU.add))
            by_group = [P, TT, G, EPG]
            step(TTo(elog[0][:, :, :].rearrange("p t (g e) -> p t g e", g=G),
                     lg[:, :, G:].rearrange("p t (g e) -> p t g e", g=G), over(ghot[:, :, :], by_group, 3), ALU.add))
            first_max(elog[0][:, :, :], emax[0], ehot[0], eidx[0], E)
            step(STT(elog[1][:, :, :], ehot[0][:, :, :], -4 * BIG, elog[0][:, :, :], ALU.mult, ALU.add))
            first_max(elog[1][:, :, :], emax[1], ehot[1], eidx[1], E)
            step(TTo(both[:, :, :], ehot[0][:, :, :], ehot[1][:, :, :], ALU.add))
            for t in range(TT):
                step(TTo(earlier[:, t + 1, :], earlier[:, t, :], both[:, t, :], ALU.add))
            dve.sem_inc(S["hot_ready"], 1)
            step(TTo(wgt[1][:, :], emax[1][:, :], emax[0][:, :], ALU.subtract))
            dve.sem_inc(S["exp_wanted"], 1)
            dve.wait_ge(S["ranks_ps"], 1)
            count = st[0][:, TT * E:(TT + 1) * E]
            cmp = scr[:, 0:E * 8].rearrange("p (e b) -> p e b", e=E)
            step(TTo(cmp, over(count, [P, E, 8], 2), over(cst[:, C_THR:C_THR + 8], [P, E, 8], 1), ALU.is_gt))
            step(V.tensor_reduce(blocks[:, E // 2:], cmp, AX.X, ALU.add))
            sums, n = blocks, 0
            for shift in (1, 2, 4, 8, 16):
                step(TTo(scan[n % 2][:, E // 2:], sums[:, E // 2:], sums[:, E // 2 - shift:E // 2 + E - shift], ALU.add))
                sums, n = scan[n % 2], n + 1
            iend, istart = sums[:, E // 2:], sums[:, E // 2 - 1:E // 2 + E - 1]
            step(STT(slot[:, :, :], over(istart, [P, TT, E], 1), float(SLOTS),
                     st[0][:, 0:TT * E].rearrange("p (t e) -> p t e", t=TT), ALU.mult, ALU.add))
            step(TTo(ehots[:, :, :, :], ehots[:, :, :, :], over(slot[:, :, :], [P, 2, TT, E], 1), ALU.mult))
            step(V.tensor_reduce(posf[:, :, :], ehots[:, :, :, :], AX.X, ALU.add))
            marks = scr[:, 0:8 * (RUN - 1)].rearrange("p (a i) -> p a i", a=8)
            pos8, item8, q8, value8 = (a[:, :, :].rearrange("p k t -> p (k t)") for a in (posf, pitem, pq, value))
            step(STT(marks, over(cst[:, C_ITEM + 1:C_ITEM + RUN], [P, 8, RUN - 1], 1), float(SLOTS),
                     over(pos8, [P, 8, RUN - 1], 2), ALU.mult, ALU.is_le))
            step(V.tensor_reduce(item8, marks, AX.X, ALU.add))
            step(STT(q8, item8, -float(SLOTS), pos8, ALU.mult, ALU.add))
            step(TTo(value8, cst[:, C_TOK:C_TOK + 8], pos8, ALU.subtract))
            step(TTo(is_item[:, :, :], over(cst[:, C_ITEM:C_ITEM + RUN], [P, 8, RUN], 1), over(item8, [P, 8, RUN], 2),
                     ALU.is_equal))
            step(TTo(is_item[:, :, :], is_item[:, :, :], over(value8, [P, 8, RUN], 2), ALU.mult))
            step(TTo(is_q[:, :, :], over(cst[:, C_Q:C_Q + SLOTS], [P, 8, SLOTS], 1), over(q8, [P, 8, SLOTS], 2),
                     ALU.is_equal))
            dve.sem_inc(S["found_ready"], 1)
            owner = scr[:, :].rearrange("p (i e) -> p i e", e=E)
            step(TTo(owner, over(iend, [P, ITEMS, E], 1), over(cst[:, C_ITEM:C_ITEM + ITEMS], [P, ITEMS, E], 2), ALU.is_le))
            dve.wait_ge(S["rows_ps"], 1)
            part = slice(0, SLOTS)
            step(TTo(filled[part, :], st[1][part, 0:RUN], cst[part, C_SLOT:C_SLOT + RUN], ALU.add))
            step(TS(past[part, :], filled[part, :], float(T), -float(T), ALU.is_ge, ALU.mult))
            step(TTo(past[part, :], past[part, :], filled[part, :], ALU.add))
            step(TS(row_x[part, :], past[part, :], float(T - 1), None, ALU.min))
            dve.sem_inc(S["rows_ready"], 1)
            for j in range(2):
                step(TS(row_y[part, :, j], filled[part, :], 2.0, float(j), ALU.mult, ALU.add))
            step(V.tensor_reduce(itemf[:, :], owner, AX.X, ALU.add))
            step(TS(itemf[:, :], itemf[:, :], float(E - 1), None, ALU.min))
            thirds = scr[:, 0:ITEMS * TURNS].rearrange("p (i j) -> p i j", j=TURNS)
            step(TTo(thirds, over(itemf[:, :], [P, ITEMS, TURNS], 2),
                     over(cst[:, C_TURN:C_TURN + TURNS], [P, ITEMS, TURNS], 1), ALU.is_ge))
            step(V.tensor_reduce(turnf[:, :], thirds, AX.X, ALU.add))
            step(STT(buff[:, :], turnf[:, :], -float(RING), itemf[:, :], ALU.mult, ALU.add))
            evens = scr[:, 0:ITEMS // 2]
            step(TTo(evens, iend[:, E - 1:E].to_broadcast([P, ITEMS // 2]), cst[:, C_EVEN:C_EVEN + ITEMS // 2], ALU.is_gt))
            step(V.tensor_reduce(tabf[:, 0:1], evens, AX.X, ALU.add))
            step(TS(tab[:, T_END:T_END + E], iend, 1.0, None, ALU.add))
            step(V.tensor_copy(tab[:, T_N:T_N + 1], tabf[:, 0:1]))
            step(TS(tab[:, T_TURN:T_TURN + ITEMS], turnf[:, :], 16.0, None, ALU.mult))
            step(TS(tab[:, T_BUF:T_BUF + ITEMS], buff[:, :], float(RING), None, ALU.add))
            dve.sem_inc(S["tab_ready"], 1)
            dve.wait_ge(S["exp_ready"], 2)
            step(V.tensor_reduce(gden[:, :], gexp[:, :, :], AX.X, ALU.add))
            step(STT(wgt[0][:, :], wgt[1][:, :], 1.0, gden[:, :], ALU.add, ALU.mult))
            step(V.reciprocal(wgt[0][:, :], wgt[0][:, :]))
            step(TTo(wgt[1][:, :], wgt[1][:, :], wgt[0][:, :], ALU.mult))

            def rows(i):
                dve.wait_ge(S["xgT_ps"], i + 1)
                for half in range(2):
                    k = slice(4 * half, 4 * half + 4)
                    last = TTo(xgT[:, k, :], tr[half][:, :, :], par[:, k, V_GF:V_GF + 1].to_broadcast([P, 4, P]), ALU.mult)
                last.then_inc(S["xgT_ready"], 1)

            dve.wait_ge(S["rows_stored"], 16 * TT)
            rows(0)
            step(STT(reach[:, :], istart, float(SLOTS), count, ALU.mult, ALU.add))
            step(TS(reach[:, :], reach[:, :], -float(SLOTS // 2), None, ALU.add))
            step(STT(owner, over(cst[:, C_ITEM:C_ITEM + ITEMS], [P, ITEMS, E], 2), float(SLOTS),
                     over(reach[:, :], [P, ITEMS, E], 1), ALU.mult, ALU.is_ge))
            step(V.tensor_reduce(lessf[:, 0:ITEMS], owner, AX.X, ALU.add))
            step(TTo(lessf[:, 0:ITEMS], lessf[:, 0:ITEMS], itemf[:, :], ALU.subtract))
            step(V.tensor_copy(less[:, :], lessf[:, :]))
            dve.sem_inc(S["rows_ready"], 1)
            pairs = dve.value_load(tab[0:1, T_N:T_N + 1], min_val=PAIRS_MIN, max_val=ITEMS // 2)
            with dve.Fori(0, pairs) as i:
                for s in range(2):
                    n = 2 * i + s
                    dve.wait_ge(S["esig_ready"], n + 1)
                    TTo(eup[s][:, :], mm[s][0][:, 0:FF // 2], esig[s][:, :], ALU.mult).then_inc(S["eup_ready"], 1)
                    dve.wait_ge(S["eup_ready"], n + 1)
                    TTo(eact[s][:, :], mm[s][0][:, FF // 2:], eup[s][:, :], ALU.mult).then_inc(S["eact_ready"], 1)
                    if s == 1:
                        rows(i + 1)
            dve.wait_ge(S["gfin_ld"], 16)
            for t in range(TT + 1):
                if t < TT:
                    dve.wait_ge(gathered[t], 32)
                    for k in range(2):
                        STT(x_tok[:, t, :], got[k][t][:, :], wgt[k][:, t:t + 1], x_tok[:, t, :], ALU.mult, ALU.add)\
                            .then_inc(S["both_added"] if k else S["first_added"], 1)
                        if k == 0:
                            dve.wait_ge(S["first_added"], t + 1)
                if t:
                    dve.wait_ge(S["final_root"], t)
                    V.reciprocal(rstd[:, t - 1:t], rstd[:, t - 1:t]).then_inc(S["final_inv"], 1)
                    dve.wait_ge(S["final_inv"], t)
                    STT(x_tok[:, t - 1, :], x_tok[:, t - 1, :], rstd[:, t - 1:t], gfin_sb[:, :], ALU.mult, ALU.mult)\
                        .then_inc(S["fin_ready"], 1)


def kernel(x, norm_mix, w_in, conv_a, w_a_out, conv_b, ln_b_g, ln_b_b, w_b_out, ln_c_g, ln_c_b, w_s, b_s,
           w_c_out, w_o, norm_ffn, w_group, b_group, w_router, b_router, w1, w3, w2, norm_final):
    import numpy as np
    import concourse.bacc as bacc
    from concourse.bass_utils import run_bass_kernel_spmd

    def tiles(w):
        return w.reshape(K, P, -1, P).transpose(2, 1, 0, 3)

    def features(a):
        return a.reshape(-1, K, P).transpose(2, 1, 0)

    w_in = np.asarray(w_in)[0]
    cuts = np.cumsum([D] * 9)
    xa, ba, ca, val, gate, uc, vc, ga, gb, gc = [tiles(a) for a in np.split(w_in, cuts, axis=1)]
    wa, wb, wc, wo = [tiles(np.asarray(a)[0]) for a in (w_a_out, w_b_out, w_c_out, w_o)]

    def two(a, b):
        return np.stack([a, b], axis=2)

    def own(a):
        return two(a[0::2], a[1::2])

    stream = np.concatenate([two(val, gate), two(uc, vc), two(ca, xa), own(ba), two(ga, wa), two(gc, wc),
                             two(gb, wb), own(wo)])
    params = np.concatenate([features(np.asarray(a)) for a in
                             (conv_b[0], conv_a[0], norm_mix, ln_b_g, ln_b_b, ln_c_g, ln_c_b, norm_ffn)],
                            axis=2)
    w13 = np.stack([np.asarray(w1)[0].reshape(E, K, P, 2, FF // 2), np.asarray(w3)[0].reshape(E, K, P, 2, FF // 2)],
                   axis=4).transpose(0, 2, 1, 3, 4, 5).reshape(E, P, K, 2, FF)
    consts = np.zeros((P, C_N), np.float32)
    consts[:, C_ID:C_ID + P] = np.eye(P)
    consts[:, C_ONE:C_ONE + P] = 1
    consts[:, C_UP:C_UP + P] = np.triu(np.ones((P, P)), 1)
    consts[:, C_THR:C_THR + 8] = SLOTS * np.arange(8)
    consts[:, C_I32:C_I32 + E] = np.arange(E)
    consts[:, C_ITEM:C_ITEM + RUN] = np.arange(RUN)
    consts[:, C_EVEN:C_EVEN + ITEMS // 2] = 2 * np.arange(ITEMS // 2)
    consts[:, C_TURN:C_TURN + TURNS] = RING * np.arange(TURNS)
    p, q = np.arange(P)[:, None], np.arange(P)[:, None] % SLOTS
    consts[:, C_Q:C_Q + SLOTS] = np.arange(SLOTS)
    consts[:, C_TOK:C_TOK + 8] = (np.arange(2)[:, None] * T + np.arange(TT) * P).reshape(-1) + p - 2 * T
    consts[:, C_SLOT:C_SLOT + RUN] = 2 * T + np.arange(RUN) * SLOTS + q
    x2 = np.asarray(x)[0]
    arrays = {
        "xT": x2.T.reshape(K, P, T).transpose(1, 0, 2),
        "stream": stream,
        "params": params,
        "wsT": np.asarray(w_s)[0].transpose(2, 0, 1),
        "bs": np.asarray(b_s)[0].reshape(-1),
        "wr": np.concatenate([np.asarray(w_group)[0], np.asarray(w_router)[0],
                              np.zeros((D, P // 2 - G - E), np.float32)], axis=1)
        .reshape(K, P, P // 2).transpose(1, 0, 2),
        "rbias": np.concatenate([np.asarray(b_group)[0], np.asarray(b_router)[0]]),
        "gfin": np.asarray(norm_final),
        "w13": w13,
        "w2": np.asarray(w2)[0].reshape(E, FF // P, P, D).transpose(0, 2, 1, 3),
        "consts": consts,
    }
    nc = bacc.Bacc("TRN2", target_bir_lowering=False, num_devices=1)
    feed, args = {}, []
    for name, a in arrays.items():
        a = np.ascontiguousarray(a, np.float32)
        feed[f"in_{name}"] = a
        args.append(nc.dram_tensor(f"in_{name}", a.shape, F32, kind="ExternalInput").ap())
    args.append(nc.dram_tensor("out_dram", (T, D), F32, kind="ExternalOutput").ap())
    build(nc, *args)
    r = run_bass_kernel_spmd(nc, [feed], core_ids=[0])
    return np.asarray(r.results[0]["out_dram"]).reshape(1, T, D)
```
